# Optimizing a Trainium2 kernel written in Bass

```python
import math
import jax, jax.numpy as jnp
from jax import lax
import numpy as np

D_MODEL = 1024
BATCH = 1
SEQ = 512
DEPTH = 2

CHUNK = 64
Q_BLOCK = 128
RMS_EPS = 1e-6
ROPE_THETA = 500000.0
MLA_ROPE_THETA = 10000.0
MACARON_WEIGHT = 0.5
N_MOD = 9
D_FF = 2816

FOX_HEADS = 8
FOX_HD = 64
FOX_GATE_BIAS = 3.0
DSA_HEADS = 8
DSA_HD = 64
DSA_ROT = DSA_HD // 4
IDX_HEADS = 4
IDX_HD = 64
IDX_ROT = IDX_HD // 4
DSA_TOPK_MAX = 256
MLA_HEADS = 8
MLA_NOPE = 128
MLA_ROPE = 64
MLA_V = 128
MLA_Q_LORA = 384
MLA_KV_LORA = 256
MLA_DOWN = MLA_Q_LORA + MLA_KV_LORA + MLA_ROPE

HYB_SIZES = (FOX_HEADS * FOX_HD, FOX_HEADS * FOX_HD, FOX_HEADS * FOX_HD, FOX_HEADS,
             DSA_HEADS * DSA_HD, DSA_HEADS * DSA_HD, DSA_HEADS * DSA_HD,
             IDX_HEADS * IDX_HD, IDX_HEADS, IDX_HD)
HYB_IN = sum(HYB_SIZES)
HYB_OUT = FOX_HEADS * FOX_HD + DSA_HEADS * DSA_HD
N_EVEN = (DEPTH + 1) // 2
N_ODD = DEPTH // 2


def _rmsnorm(x, g):
    x32 = x.astype(jnp.float32)
    y = x32 * lax.rsqrt(jnp.mean(x32 * x32, axis=-1, keepdims=True) + RMS_EPS)
    return (y * g.astype(jnp.float32)).astype(x.dtype)

def _rope(x, pos, rot_dim, theta):
    half = rot_dim // 2
    inv_freq = jnp.exp(-math.log(theta) * 2.0 * jnp.arange(half, dtype=jnp.float32) / rot_dim)
    ang = pos.astype(jnp.float32)[:, :, None, None] * inv_freq
    cos, sin = jnp.cos(ang), jnp.sin(ang)
    xr = x[..., :rot_dim].astype(jnp.float32)
    x1, x2 = xr[..., :half], xr[..., half:]
    rot = jnp.concatenate([x1 * cos - x2 * sin, x2 * cos + x1 * sin], axis=-1).astype(x.dtype)
    return jnp.concatenate([rot, x[..., rot_dim:]], axis=-1)

def _sweep_query_blocks(fn, *q_args):
    b, s = q_args[0].shape[:2]
    nblk = s // Q_BLOCK
    blocked = tuple(jnp.moveaxis(a.reshape(b, nblk, Q_BLOCK, *a.shape[2:]), 1, 0) for a in q_args)
    out = lax.map(lambda xs: fn(xs[0] * Q_BLOCK + jnp.arange(Q_BLOCK, dtype=jnp.int32), *xs[1:]),
                  (jnp.arange(nblk, dtype=jnp.int32),) + blocked)
    out = jnp.moveaxis(out, 0, 1)
    return out.reshape(b, s, *out.shape[3:])

def _fox_attention(q, k, v, log_f):
    s = k.shape[1]
    cum = jnp.moveaxis(jnp.cumsum(log_f, axis=1), 1, 2)
    s_idx = jnp.arange(s, dtype=jnp.int32)
    scale = q.shape[-1] ** -0.5

    def block(t_idx, qb, cum_q):
        logits = jnp.einsum('bqhd,bshd->bhqs', qb, k, preferred_element_type=jnp.float32) * scale
        logits = logits + (jnp.moveaxis(cum_q, 1, 2)[..., :, None] - cum[..., None, :])
        mask = s_idx[None, :] <= t_idx[:, None]
        logits = jnp.where(mask, logits, -jnp.inf)
        p = jax.nn.softmax(logits, axis=-1).astype(v.dtype)
        return jnp.einsum('bhqs,bshd->bqhd', p, v)

    return _sweep_query_blocks(block, q, jnp.moveaxis(cum, 1, 2))

def _dsa_attention(q, k, v, iq, iw, ik):
    s = k.shape[1]
    top_k = min(DSA_TOPK_MAX, s // 4)
    s_chunk = jnp.arange(s, dtype=jnp.int32) // CHUNK
    scale = q.shape[-1] ** -0.5
    idx_scale = iq.shape[-1] ** -0.5
    gather = jax.vmap(lambda table, ix: table[ix])

    def block(t_idx, qb, iqb, iwb):
        dots = jnp.einsum('bqhd,bsd->bqhs', iqb, ik, preferred_element_type=jnp.float32) * idx_scale
        score = jnp.einsum('bqhs,bqh->bqs', jax.nn.relu(dots), iwb.astype(jnp.float32))
        admissible = s_chunk[None, :] <= (t_idx // CHUNK)[:, None]
        score = jnp.where(admissible[None], score, -jnp.inf)
        sel_score, sel = lax.top_k(score, top_k)
        kg = gather(k, sel)
        vg = gather(v, sel)
        logits = jnp.einsum('bqhd,bqkhd->bhqk', qb, kg, preferred_element_type=jnp.float32) * scale
        valid = jnp.isfinite(sel_score)[:, None]
        logits = jnp.where(valid, logits, -jnp.inf)
        p = jax.nn.softmax(logits, axis=-1).astype(v.dtype)
        return jnp.einsum('bhqk,bqkhd->bqhd', p, vg)

    return _sweep_query_blocks(block, q, iq, iw)

def _mla_attention(q_nope, q_rope, k_nope, k_rope, v):
    s = k_nope.shape[1]
    s_chunk = jnp.arange(s, dtype=jnp.int32) // CHUNK
    scale = (q_nope.shape[-1] + q_rope.shape[-1]) ** -0.5

    def block(t_idx, qn, qr):
        logits = (jnp.einsum('bqhd,bshd->bhqs', qn, k_nope, preferred_element_type=jnp.float32)
                  + jnp.einsum('bqhr,bsr->bhqs', qr, k_rope, preferred_element_type=jnp.float32)) * scale
        mask = s_chunk[None, :] <= (t_idx // CHUNK)[:, None]
        logits = jnp.where(mask, logits, -jnp.inf)
        p = jax.nn.softmax(logits, axis=-1).astype(v.dtype)
        return jnp.einsum('bhqs,bshd->bqhd', p, v)

    return _sweep_query_blocks(block, q_nope, q_rope)

def _hybrid_mixer(u, positions, w_in, b_f, w_out):
    b, s, _ = u.shape
    offsets = np.cumsum(HYB_SIZES)[:-1].tolist()
    fq, fk, fv, ff, dq, dk, dv, iq, iw, ik = jnp.split(u @ w_in, offsets, axis=-1)
    log_f = jax.nn.log_sigmoid((ff + b_f).astype(jnp.float32))
    out_a = _fox_attention(fq.reshape(b, s, FOX_HEADS, FOX_HD), fk.reshape(b, s, FOX_HEADS, FOX_HD),
                           fv.reshape(b, s, FOX_HEADS, FOX_HD), log_f)
    dq = _rope(dq.reshape(b, s, DSA_HEADS, DSA_HD), positions, DSA_ROT, ROPE_THETA)
    dk = _rope(dk.reshape(b, s, DSA_HEADS, DSA_HD), positions, DSA_ROT, ROPE_THETA)
    iq = _rope(iq.reshape(b, s, IDX_HEADS, IDX_HD), positions, IDX_ROT, ROPE_THETA)
    ik = _rope(ik[:, :, None, :], positions, IDX_ROT, ROPE_THETA)[:, :, 0, :]
    iw = iw * IDX_HEADS ** -0.5
    out_b = _dsa_attention(dq, dk, dv.reshape(b, s, DSA_HEADS, DSA_HD), iq, iw, ik)
    mixed = jnp.concatenate([out_a.reshape(b, s, -1), out_b.reshape(b, s, -1)], axis=-1)
    return mixed @ w_out

def _mla_mixer(u, positions, w_down, q_norm, kv_norm, w_uq, w_ukv, w_out):
    b, s, _ = u.shape
    cq, ckv, k_rope = jnp.split(u @ w_down, [MLA_Q_LORA, MLA_Q_LORA + MLA_KV_LORA], axis=-1)
    q = (_rmsnorm(cq, q_norm) @ w_uq).reshape(b, s, MLA_HEADS, MLA_NOPE + MLA_ROPE)
    kv = (_rmsnorm(ckv, kv_norm) @ w_ukv).reshape(b, s, MLA_HEADS, MLA_NOPE + MLA_V)
    q_nope = q[..., :MLA_NOPE]
    q_rope = _rope(q[..., MLA_NOPE:], positions, MLA_ROPE, MLA_ROPE_THETA)
    k_nope, v = kv[..., :MLA_NOPE], kv[..., MLA_NOPE:]
    k_rope = _rope(k_rope[:, :, None, :], positions, MLA_ROPE, MLA_ROPE_THETA)[:, :, 0, :]
    out = _mla_attention(q_nope, q_rope, k_nope, k_rope, v)
    return out.reshape(b, s, -1) @ w_out

def _swiglu(u, w_gate, w_up, w_down):
    return (jax.nn.silu(u @ w_gate) * (u @ w_up)) @ w_down

def first_inputs(seed: int = 0) -> dict:
    key = jax.random.key(seed)
    ks = jax.random.split(key, 20)
    f32 = jnp.float32

    def nrm(k, shape, fan_in):
        return jax.random.normal(k, shape, f32) * fan_in ** -0.5

    x = jax.random.normal(ks[0], (BATCH, SEQ, D_MODEL), f32)
    c = jax.random.normal(ks[1], (BATCH, D_MODEL), f32)
    start = jax.random.randint(ks[2], (BATCH, 1), 0, 4096, dtype=jnp.int32)
    positions = start + jnp.arange(SEQ, dtype=jnp.int32)[None, :]
    ada_w = 0.5 * nrm(ks[3], (DEPTH, D_MODEL, N_MOD * D_MODEL), D_MODEL)
    ada_b = 0.02 * jax.random.normal(ks[4], (DEPTH, N_MOD * D_MODEL), f32)
    norm_g = 1.0 + 0.02 * jax.random.normal(ks[5], (DEPTH, 3, D_MODEL), f32)
    ffn_w_gate = nrm(ks[6], (DEPTH, 2, D_MODEL, D_FF), D_MODEL)
    ffn_w_up = nrm(ks[7], (DEPTH, 2, D_MODEL, D_FF), D_MODEL)
    ffn_w_down = nrm(ks[8], (DEPTH, 2, D_FF, D_MODEL), D_FF)
    hyb_w_in = nrm(ks[9], (N_EVEN, D_MODEL, HYB_IN), D_MODEL)
    fox_b_f = FOX_GATE_BIAS + 0.5 * jax.random.normal(ks[10], (N_EVEN, FOX_HEADS), f32)
    hyb_w_out = nrm(ks[11], (N_EVEN, HYB_OUT, D_MODEL), HYB_OUT)
    mla_w_down = nrm(ks[12], (N_ODD, D_MODEL, MLA_DOWN), D_MODEL)
    mla_q_norm = 1.0 + 0.02 * jax.random.normal(ks[13], (N_ODD, MLA_Q_LORA), f32)
    mla_kv_norm = 1.0 + 0.02 * jax.random.normal(ks[14], (N_ODD, MLA_KV_LORA), f32)
    mla_w_uq = nrm(ks[15], (N_ODD, MLA_Q_LORA, MLA_HEADS * (MLA_NOPE + MLA_ROPE)), MLA_Q_LORA)
    mla_w_ukv = nrm(ks[16], (N_ODD, MLA_KV_LORA, MLA_HEADS * (MLA_NOPE + MLA_V)), MLA_KV_LORA)
    mla_w_out = nrm(ks[17], (N_ODD, MLA_HEADS * MLA_V, D_MODEL), MLA_HEADS * MLA_V)
    final_g = 1.0 + 0.02 * jax.random.normal(ks[18], (D_MODEL,), f32)
    return {'x': x, 'c': c, 'positions': positions, 'ada_w': ada_w, 'ada_b': ada_b,
            'norm_g': norm_g, 'ffn_w_gate': ffn_w_gate, 'ffn_w_up': ffn_w_up,
            'ffn_w_down': ffn_w_down, 'hyb_w_in': hyb_w_in, 'fox_b_f': fox_b_f,
            'hyb_w_out': hyb_w_out, 'mla_w_down': mla_w_down, 'mla_q_norm': mla_q_norm,
            'mla_kv_norm': mla_kv_norm, 'mla_w_uq': mla_w_uq, 'mla_w_ukv': mla_w_ukv,
            'mla_w_out': mla_w_out, 'final_g': final_g}

def first_block(x, c, positions, ada_w, ada_b, norm_g, ffn_w_gate, ffn_w_up, ffn_w_down,
              hyb_w_in, fox_b_f, hyb_w_out, mla_w_down, mla_q_norm, mla_kv_norm,
              mla_w_uq, mla_w_ukv, mla_w_out, final_g):
    h = x
    cond = jax.nn.silu(c)
    for i in range(DEPTH):
        mod = (cond @ ada_w[i] + ada_b[i]).reshape(c.shape[0], N_MOD, D_MODEL)[:, :, None, :]
        sh1, sc1, g1, sh2, sc2, g2, sh3, sc3, g3 = [mod[:, j] for j in range(N_MOD)]
        u = _rmsnorm(h, norm_g[i, 0]) * (1 + sc1) + sh1
        h = h + MACARON_WEIGHT * g1 * _swiglu(u, ffn_w_gate[i, 0], ffn_w_up[i, 0], ffn_w_down[i, 0])
        u = _rmsnorm(h, norm_g[i, 1]) * (1 + sc2) + sh2
        j = i // 2
        if i % 2 == 0:
            mix = _hybrid_mixer(u, positions, hyb_w_in[j], fox_b_f[j], hyb_w_out[j])
        else:
            mix = _mla_mixer(u, positions, mla_w_down[j], mla_q_norm[j], mla_kv_norm[j],
                             mla_w_uq[j], mla_w_ukv[j], mla_w_out[j])
        h = h + g2 * mix
        u = _rmsnorm(h, norm_g[i, 2]) * (1 + sc3) + sh3
        h = h + MACARON_WEIGHT * g3 * _swiglu(u, ffn_w_gate[i, 1], ffn_w_up[i, 1], ffn_w_down[i, 1])
    return _rmsnorm(h, final_g)


D_FF_2 = 4 * D_MODEL
EPS = 1e-6
NEG_BIG = -1e30
M_HEADS = 4
M_DIM = D_MODEL // 16
M_WIDTH = M_HEADS * M_DIM
M_CONV = 4
M_CHUNK = 128
A_HEADS = 4
A_DIM = D_MODEL // 16
A_WIDTH = A_HEADS * 2 * A_DIM
ROT_DIM = A_DIM // 4
H_HEADS = 4
H_DK = D_MODEL // 16
H_DV = D_MODEL // 16
H_WIDTH = H_HEADS * H_DV
H_CHUNK = 64
D_MIX = M_WIDTH + A_WIDTH + H_WIDTH
M_COLS = 4 * M_WIDTH + 2 * M_HEADS
A_COLS = 3 * A_WIDTH
H_COLS = 4 * H_WIDTH
D_IN = M_COLS + A_COLS + H_COLS


def rmsnorm(x, g):
    xf = x.astype(jnp.float32)
    y = xf * lax.rsqrt(jnp.mean(xf * xf, axis=-1, keepdims=True) + EPS)
    return (y * g.astype(jnp.float32)).astype(x.dtype)

def causal_dwconv(x, w):
    K = w.shape[0]
    T = x.shape[1]
    xp = jnp.pad(x, ((0, 0), (K - 1, 0), (0, 0)))
    out = xp[:, 0:T] * w[0]
    for j in range(1, K):
        out = out + xp[:, j:j + T] * w[j]
    return out

def partial_rope(x, pos):
    half = ROT_DIM // 2
    inv = ROPE_THETA ** (-jnp.arange(half, dtype=jnp.float32) / half)
    ang = pos.astype(jnp.float32)[:, None] * inv[None, :]
    cos = jnp.cos(ang)[:, None, :]
    sin = jnp.sin(ang)[:, None, :]
    x1 = x[..., :half]
    x2 = x[..., half:ROT_DIM]
    r1 = x1 * cos - x2 * sin
    r2 = x2 * cos + x1 * sin
    return jnp.concatenate([r1, r2, x[..., ROT_DIM:]], axis=-1)

def to_chunks(a, L):
    B, H, T = a.shape[:3]
    a = a.reshape((B, H, T // L, L) + a.shape[3:])
    return jnp.moveaxis(a, 2, 0)

def from_chunks(a):
    a = jnp.moveaxis(a, 0, 2)
    B, H, NC, L = a.shape[:4]
    return a.reshape((B, H, NC * L) + a.shape[4:])

def mlstm_chunkwise(q, k, v, i_pre, f_pre):
    B, H, T, d = q.shape
    L = M_CHUNK
    k = k * (d ** -0.5)
    logf = jax.nn.log_sigmoid(f_pre)
    xs = (to_chunks(q, L), to_chunks(k, L), to_chunks(v, L), to_chunks(i_pre, L), to_chunks(logf, L))
    causal = jnp.tril(jnp.ones((L, L), dtype=bool))

    def step(carry, xs_c):
        C, n, m = carry
        qb, kb, vb, ib, fb = xs_c
        b = jnp.cumsum(fb, axis=-1)
        D = b[..., :, None] - b[..., None, :] + ib[..., None, :]
        D = jnp.where(causal, D, NEG_BIG)
        inter = b + m[..., None]
        m_t = jnp.maximum(jnp.max(D, axis=-1), inter)
        S = jnp.einsum('bhtd,bhsd->bhts', qb, kb) * jnp.exp(D - m_t[..., None])
        scale = jnp.exp(inter - m_t)
        num = jnp.einsum('bhts,bhsv->bhtv', S, vb) + scale[..., None] * jnp.einsum('bhvk,bhtk->bhtv', C, qb)
        den = jnp.sum(S, axis=-1) + scale * jnp.einsum('bhk,bhtk->bht', n, qb)
        h = num / jnp.maximum(jnp.abs(den), jnp.exp(-m_t))[..., None]
        bL = b[..., -1]
        g = bL[..., None] - b + ib
        m_new = jnp.maximum(bL + m, jnp.max(g, axis=-1))
        w_s = jnp.exp(g - m_new[..., None])
        decay = jnp.exp(bL + m - m_new)
        C_new = decay[..., None, None] * C + jnp.einsum('bhs,bhsv,bhsk->bhvk', w_s, vb, kb)
        n_new = decay[..., None] * n + jnp.einsum('bhs,bhsk->bhk', w_s, kb)
        return (C_new, n_new, m_new), h

    init = (jnp.zeros((B, H, d, d), jnp.float32), jnp.zeros((B, H, d), jnp.float32), jnp.zeros((B, H), jnp.float32))
    _, h = lax.scan(step, init, xs)
    return from_chunks(h)

def mlstm_mixer(q_pre, k_pre, v, o_pre, i_pre, f_pre, conv_w, gate_b, norm_g):
    B, T, _ = q_pre.shape
    f32 = jnp.float32
    qk = jax.nn.silu(causal_dwconv(jnp.concatenate([q_pre, k_pre], axis=-1).astype(f32), conv_w.astype(f32)))
    q, k = qk[..., :M_WIDTH], qk[..., M_WIDTH:]
    heads = lambda a: a.reshape(B, T, M_HEADS, M_DIM).transpose(0, 2, 1, 3)
    gb = gate_b.astype(f32)
    i_g = (i_pre.astype(f32) + gb[0]).transpose(0, 2, 1)
    f_g = (f_pre.astype(f32) + gb[1]).transpose(0, 2, 1)
    h = mlstm_chunkwise(heads(q), heads(k), heads(v.astype(f32)), i_g, f_g)
    h = rmsnorm(h.transpose(0, 2, 1, 3), norm_g)
    h = jax.nn.sigmoid(o_pre.astype(f32)).reshape(B, T, M_HEADS, M_DIM) * h
    return h.reshape(B, T, M_WIDTH)

def diff_attention(q, k, v, qn_g, kn_g, lam_vec, subln_g, lambda_init):
    B, T, _ = q.shape
    f32 = jnp.float32
    pos = jnp.arange(T)
    q = rmsnorm(q.astype(f32).reshape(B, T, A_HEADS, 2, A_DIM), qn_g)
    k = rmsnorm(k.astype(f32).reshape(B, T, A_HEADS, 2, A_DIM), kn_g)
    q = partial_rope(q.reshape(B, T, A_HEADS * 2, A_DIM), pos).reshape(B, T, A_HEADS, 2, A_DIM)
    k = partial_rope(k.reshape(B, T, A_HEADS * 2, A_DIM), pos).reshape(B, T, A_HEADS, 2, A_DIM)
    q = q * (A_DIM ** -0.5)
    v = v.astype(f32).reshape(B, T, A_HEADS, 2 * A_DIM).transpose(0, 2, 1, 3)
    kt = k.transpose(0, 2, 3, 1, 4)
    lv = lam_vec.astype(f32)
    lam = jnp.exp(jnp.sum(lv[0] * lv[1])) - jnp.exp(jnp.sum(lv[2] * lv[3])) + lambda_init
    NB = T // Q_BLOCK
    qb = q.reshape(B, NB, Q_BLOCK, A_HEADS, 2, A_DIM).transpose(1, 0, 3, 4, 2, 5)
    kpos = jnp.arange(T)

    def block(args):
        qi, bi = args
        s = jnp.einsum('bhcqd,bhckd->bhcqk', qi, kt)
        qpos = bi * Q_BLOCK + jnp.arange(Q_BLOCK)
        mask = qpos[:, None] >= kpos[None, :]
        p = jax.nn.softmax(jnp.where(mask, s, NEG_BIG), axis=-1)
        a = p[:, :, 0] - lam * p[:, :, 1]
        return jnp.einsum('bhqk,bhkv->bhqv', a, v)

    o = lax.map(block, (qb, jnp.arange(NB)))
    o = o.transpose(1, 0, 3, 2, 4).reshape(B, T, A_HEADS, 2 * A_DIM)
    o = rmsnorm(o, subln_g) * (1.0 - lambda_init)
    return o.reshape(B, T, A_WIDTH)

def hgrn2_chunkwise(q, logf, k, v):
    B, H, T, dk = q.shape
    dv = v.shape[-1]
    L = H_CHUNK
    xs = (to_chunks(q, L), to_chunks(logf, L), to_chunks(k, L), to_chunks(v, L))
    causal = jnp.tril(jnp.ones((L, L), dtype=bool))[..., None]

    def step(S, xs_c):
        qb, gb, kb, vb = xs_c
        Bc = jnp.cumsum(gb, axis=-2)
        diff = Bc[..., :, None, :] - Bc[..., None, :, :]
        decay = jnp.exp(jnp.where(causal, diff, NEG_BIG))
        A = jnp.einsum('bhtk,bhsk,bhtsk->bhts', qb, kb, decay)
        o = jnp.einsum('bhts,bhsv->bhtv', A, vb) + jnp.einsum('bhtk,bhkv->bhtv', qb * jnp.exp(Bc), S)
        BL = Bc[..., -1:, :]
        S_new = jnp.exp(BL[..., 0, :])[..., None] * S + jnp.einsum('bhsk,bhsv->bhkv', kb * jnp.exp(BL - Bc), vb)
        return S_new, o

    _, o = lax.scan(step, jnp.zeros((B, H, dk, dv), jnp.float32), xs)
    return from_chunks(o)

def hgrn2_mixer(q_pre, f_pre, i_pre, g_pre, lb, norm_g):
    B, T, _ = q_pre.shape
    f32 = jnp.float32
    heads = lambda a, dd: a.astype(f32).reshape(B, T, H_HEADS, dd).transpose(0, 2, 1, 3)
    q = jax.nn.silu(heads(q_pre, H_DK))
    fp = heads(f_pre, H_DK)
    lbh = lb.reshape(H_HEADS, 1, H_DK)
    f = lbh + (1.0 - lbh) * jax.nn.sigmoid(fp)
    logf = jnp.log(f)
    k = (1.0 - lbh) * jax.nn.sigmoid(-fp)
    v = heads(i_pre, H_DV)
    o = hgrn2_chunkwise(q, logf, k, v).transpose(0, 2, 1, 3)
    o = rmsnorm(o, norm_g) * jax.nn.silu(g_pre.astype(f32)).reshape(B, T, H_HEADS, H_DV)
    return o.reshape(B, T, H_WIDTH)

def second_inputs(seed: int = 0) -> dict:
    key = jax.random.key(seed)
    ks = jax.random.split(key, 20)
    f32 = jnp.float32
    nrm = lambda k, shp, s: jax.random.normal(k, shp, f32) * s
    f_bias = jnp.broadcast_to(jnp.linspace(3.0, 6.0, M_HEADS, dtype=f32), (DEPTH, M_HEADS))
    mlstm_gate_b = jnp.stack([nrm(ks[4], (DEPTH, M_HEADS), 0.1), f_bias + nrm(ks[5], (DEPTH, M_HEADS), 0.1)], axis=1)
    return {
        'x': jax.random.normal(ks[0], (BATCH, SEQ, D_MODEL), f32),
        'norm1_g': 1.0 + nrm(ks[1], (DEPTH, D_MODEL), 0.02),
        'w_in': nrm(ks[2], (DEPTH, D_MODEL, D_IN), D_MODEL ** -0.5),
        'mlstm_conv_w': nrm(ks[3], (DEPTH, M_CONV, 2 * M_WIDTH), M_CONV ** -0.5),
        'mlstm_gate_b': mlstm_gate_b,
        'mlstm_norm_g': 1.0 + nrm(ks[6], (DEPTH, M_DIM), 0.02),
        'diff_q_norm_g': 1.0 + nrm(ks[7], (DEPTH, A_DIM), 0.02),
        'diff_k_norm_g': 1.0 + nrm(ks[8], (DEPTH, A_DIM), 0.02),
        'diff_lambda': nrm(ks[9], (DEPTH, 4, A_DIM), 0.1),
        'diff_subln_g': 1.0 + nrm(ks[10], (DEPTH, 2 * A_DIM), 0.02),
        'hgrn_lb_param': nrm(ks[11], (DEPTH, H_HEADS * H_DK), 1.0),
        'hgrn_norm_g': 1.0 + nrm(ks[12], (DEPTH, H_DV), 0.02),
        'w_out': nrm(ks[13], (DEPTH, D_MIX, D_MODEL), D_MIX ** -0.5),
        'norm2_g': 1.0 + nrm(ks[14], (DEPTH, D_MODEL), 0.02),
        'w_up': nrm(ks[15], (DEPTH, D_MODEL, D_FF_2), D_MODEL ** -0.5),
        'w_down': nrm(ks[16], (DEPTH, D_FF_2, D_MODEL), D_FF_2 ** -0.5),
    }

def second_block(x, norm1_g, w_in, mlstm_conv_w, mlstm_gate_b, mlstm_norm_g, diff_q_norm_g, diff_k_norm_g,
              diff_lambda, diff_subln_g, hgrn_lb_param, hgrn_norm_g, w_out, norm2_g, w_up, w_down):
    sm = jax.nn.softmax(hgrn_lb_param.astype(jnp.float32), axis=0)
    lower_bounds = jnp.cumsum(sm, axis=0) - sm[0]
    split_at = np.cumsum([M_WIDTH, M_WIDTH, M_WIDTH, M_WIDTH, M_HEADS, M_HEADS,
                          A_WIDTH, A_WIDTH, A_WIDTH,
                          H_WIDTH, H_WIDTH, H_WIDTH])
    for l in range(DEPTH):
        lambda_init = 0.8 - 0.6 * math.exp(-0.3 * l)
        h = rmsnorm(x, norm1_g[l])
        u = jnp.einsum('btd,de->bte', h, w_in[l])
        (mq, mk, mv, mo, mi, mf, aq, ak, av, hq, hf, hi, hg) = jnp.split(u, split_at, axis=-1)
        y_m = mlstm_mixer(mq, mk, mv, mo, mi, mf, mlstm_conv_w[l], mlstm_gate_b[l], mlstm_norm_g[l])
        y_a = diff_attention(aq, ak, av, diff_q_norm_g[l], diff_k_norm_g[l], diff_lambda[l], diff_subln_g[l], lambda_init)
        y_h = hgrn2_mixer(hq, hf, hi, hg, lower_bounds[l], hgrn_norm_g[l])
        mix = jnp.concatenate([y_m, y_a, y_h], axis=-1).astype(x.dtype)
        x = x + jnp.einsum('bte,ed->btd', mix, w_out[l])
        h2 = rmsnorm(x, norm2_g[l])
        a = jnp.square(jax.nn.relu(jnp.einsum('btd,df->btf', h2, w_up[l])))
        x = x + jnp.einsum('btf,fd->btd', a, w_down[l])
    return x


def setup_inputs(seed=0):
    out = dict(first_inputs(seed))
    for name, value in second_inputs(seed + 1).items():
        if name != "x":
            out[name + "_2"] = value
    return out


def reference(
    x, c, positions, ada_w, ada_b, norm_g, ffn_w_gate, ffn_w_up, ffn_w_down, hyb_w_in, fox_b_f,
    hyb_w_out, mla_w_down, mla_q_norm, mla_kv_norm, mla_w_uq, mla_w_ukv, mla_w_out, final_g,
    norm1_g_2, w_in_2, mlstm_conv_w_2, mlstm_gate_b_2, mlstm_norm_g_2, diff_q_norm_g_2,
    diff_k_norm_g_2, diff_lambda_2, diff_subln_g_2, hgrn_lb_param_2, hgrn_norm_g_2, w_out_2,
    norm2_g_2, w_up_2, w_down_2,
):
    x = first_block(
        x, c, positions, ada_w, ada_b, norm_g, ffn_w_gate, ffn_w_up, ffn_w_down, hyb_w_in,
        fox_b_f, hyb_w_out, mla_w_down, mla_q_norm, mla_kv_norm, mla_w_uq, mla_w_ukv, mla_w_out,
        final_g,
    )
    return second_block(
        x, norm1_g_2, w_in_2, mlstm_conv_w_2, mlstm_gate_b_2, mlstm_norm_g_2, diff_q_norm_g_2,
        diff_k_norm_g_2, diff_lambda_2, diff_subln_g_2, hgrn_lb_param_2, hgrn_norm_g_2, w_out_2,
        norm2_g_2, w_up_2, w_down_2,
    )


_drawn_inputs = setup_inputs


def setup_inputs(seed=0):
    import zlib

    import numpy as np

    out = dict(_drawn_inputs(seed))
    spreads = {}
    factors = {'norm_g': 5.083,
     'fox_b_f': 3.504,
     'mla_q_norm': 8.0,
     'mla_kv_norm': 8.0,
     'mlstm_norm_g_2': 8.0,
     'diff_q_norm_g_2': 7.515,
     'diff_k_norm_g_2': 7.57,
     'diff_subln_g_2': 4.37,
     'hgrn_lb_param_2': 3.283,
     'hgrn_norm_g_2': 8.0}
    for name, (base, spread) in spreads.items():
        noise = np.random.default_rng([zlib.crc32(name.encode()), seed]).standard_normal(out[name].shape)
        drawn = base * np.exp(spread * noise) if base else spread * noise
        out[name] = __import__('jax').numpy.asarray(drawn.astype(out[name].dtype))
    for name, factor in factors.items():
        out[name] = (out[name] * factor).astype(out[name].dtype)
    return out
```

```python
import math
from contextlib import ExitStack

import numpy as np

import concourse.bass as bass
from concourse import mybir

F32 = mybir.dt.float32
I32 = mybir.dt.int32
U32 = mybir.dt.uint32
ALU = mybir.AluOpType
ACT = mybir.ActivationFunctionType
AX = mybir.AxisListType

P = 128
T = 512
NB = T // P
D = 1024
DC = D // P
FF = 2816
FC = FF // P
FF2 = 4 * D
FC2 = FF2 // P
DEPTH = 2
N_MOD = 9
TOPK = 128
NEG = -1e30
LOWEST = -3e38
RMS_EPS = 1e-6

FOX_H = 8
DSA_H = 8
IDX_H = 4
MLA_H = 8
DIFF_H = 4
RING = 4
SLAB = 16 * P
UP0 = 10
N_ADA = DEPTH * N_MOD * D // 256

CONSTS = [("ident", P), ("ones", P), ("blk64", P), ("rot16", P), ("rot64", P),
          ("causal", T), ("chunk", T), ("sel4", 2 * P), ("invf16", 1), ("invf64", 1), ("eps", 1)]
CONSTS2 = [("tri", P), ("levels", 8 * P), ("diff_cos", T), ("diff_sin", T), ("lam", DEPTH * 4 * 64)]


def _offsets(table):
    off, n = {}, 0
    for name, width in table:
        off[name] = (n, width)
        n += width
    return off, n


COFF, NCONST = _offsets(CONSTS)
COFF2, NCONST2 = _offsets(CONSTS2)

SMALL = [("norm_g", DEPTH * 3 * DC), ("final_g", DC), ("norm1", DEPTH * DC), ("norm2", DEPTH * DC),
         ("q_norm", 3), ("kv_norm", 2), ("conv", DEPTH * 4 * 4), ("mnorm", DEPTH),
         ("qn", DEPTH), ("kn", DEPTH), ("subln", DEPTH), ("lb", DEPTH * 2), ("hnorm", DEPTH),
         ("cond", DC), ("foxb", 1), ("gateb", DEPTH * 2)]
SOFF, NSMALL = _offsets(SMALL)


def slab_loop(eng, n, body, chains=(), unroll=RING, peel=0):
    for r in range(peel):
        body(r, 0)
    turns = (n - peel) // unroll
    done = peel
    if turns >= 2:
        for ch, per in chains:
            ch.enter(per * unroll)
        with eng.Fori(0, turns) as it:
            for ch, _ in chains:
                ch.it = it
            for u in range(unroll):
                body(peel + u, it)
        for ch, _ in chains:
            ch.leave(turns)
        done += turns * unroll
    for r in range(done, n):
        body(r, 0)


class Chain:

    def __init__(self, eng, sem):
        self.eng, self.sem, self.n = eng, sem, 0
        self.it, self.per, self.base = None, 0, 0

    def enter(self, per):
        self.base, self.per = self.n, per

    def leave(self, turns):
        assert self.n - self.base == self.per, (self.n - self.base, self.per)
        self.n = self.base + self.per * turns
        self.it = None

    def __call__(self, ins):
        self.n += 1
        ins.then_inc(self.sem, 1)
        self.eng.wait_ge(self.sem, self.n if self.it is None else self.it * self.per + self.n)


class Place:

    def __init__(self, eng, sems):
        self.eng, self.sems = eng, sems
        self.slab = self.group = self.ada = 0
        self.norm = self.sq = self.silu = self.tu = self.ur = 0
        self.rope = self.unit = self.prob = self.head = 0
        self.seen = {}

    def got(self, name, n=1):
        self.seen[name] = self.seen.get(name, 0) + n
        self.eng.wait_ge(self.sems(name), self.seen[name])

    def passed(self, name, n=1):
        self.seen[name] = self.seen.get(name, 0) + n

    def groups_taken(self):
        if self.group:
            self.eng.wait_ge(self.sems("lin_taken0"), (self.group + 1) // 2)
        if self.group > 1:
            self.eng.wait_ge(self.sems("lin_taken1"), self.group // 2)


def at(value, it, per):
    return value if isinstance(it, int) else it * per + value


FQ, FK, DQ, DK, IQ, IK, GT, FV, DV, DMASK = 0, 4, 8, 12, 16, 18, 19, 20, 24, 28
CQ, CKV, KR, QN, QR, KN, MV = 0, 3, 5, 6, 14, 18, 26
XQ, XK, XO, AQ, AK, HQ, HF, HG, GI, GF, XV, AV, HV, SP = 0, 2, 4, 6, 10, 14, 16, 18, 20, 21, 22, 24, 28, 30


def build(nc, x, small, consts, consts2, pos, adab, w, out):
    with ExitStack() as ctx:
        sems = {}

        def s(name):
            if name not in sems:
                sems[name] = ctx.enter_context(nc.semaphore(name))
            return sems[name]

        def sb(name, shape, dt=F32):
            return ctx.enter_context(nc.sbuf_tensor(name, shape, dt))

        h = sb("h", [P, DC, T])
        u = sb("u", [P, DC, T])
        big = sb("big", [P, 32, T])
        ring = sb("ring", [P, RING, SLAB])
        ada_in = sb("ada_in", [P, 2, DC * 256])
        ada_acc = sb("ada_acc", [P, 256])
        cst = sb("cst", [P, NCONST])
        sm = sb("sm", [P, NSMALL])
        mod = sb("mod", [P, N_ADA * 2])
        modb = sb("modb", [P, N_ADA * 2])
        gain = sb("gain", [P, DC])
        gate = sb("gate", [P, DC])
        tmp = sb("tmp", [P, 2, 2 * T])
        rt = sb("rt", [P, T])
        rstd = sb("rstd", [P, T])
        sq = sb("sq", [P, 2, T])
        tabs = sb("tabs", [P, 4, T])
        S = sb("S", [P, 2, T])
        E = sb("E", [P, 4, T])
        ET = sb("ET", [P, 2, T])
        st = sb("st", [P, 64])
        stat = sb("stat", [P, 4, 4])
        csil = sb("csil", [P, DC])
        wk = sb("wk", [P, 6, T])
        tokw = sb("tokw", [P, 4 * NB])
        tmpf = tmp[:, :, :].rearrange("p a b -> p (a b)")

        cst2 = ada_in[:, :, :].rearrange("p a b -> p (a b)")

        LP = [ctx.enter_context(nc.psum_tensor(f"LP{i}", [P, 2, T], F32)) for i in range(2)]
        XB = [ctx.enter_context(nc.psum_tensor(f"XB{i}", [P, T], F32)) for i in range(4)]
        LPF = [t[:, :, :].rearrange("p a b -> p (a b)") for t in LP]

        def cc(name, a=0, n=None):
            t, (o, wd) = (cst, COFF[name]) if name in COFF else (cst2, COFF2[name])
            return t[:, o + a:o + (wd if n is None else a + n)]

        def gate_row(rows, i):
            return tmpf[rows, i * T:(i + 1) * T] if i < 4 else tabs[rows, i - 4, :]

        def ones_row(rows, n=T):
            return cc("ones", 0, 1)[rows, :].to_broadcast([rows.stop - rows.start, n])

        def sp_(name, a=0, n=1):
            return sm[:, SOFF[name][0] + a:SOFF[name][0] + a + n]

        def blk(b):
            return slice(b * P, (b + 1) * P)

        def half(i):
            return slice(64 * (i % 2), 64 * (i % 2) + 64)

        def vals(c0, width):
            n = NB * width // T
            return big[:, c0:c0 + n, :].rearrange("p a b -> p (a b)").rearrange("p (t c) -> p t c", c=width)

        fv, dv = vals(FV, T), vals(DV, T)
        mv = [vals(MV + 2 * i, 256) for i in range(3)] + [tmpf[:, 0:1024].rearrange("p (t c) -> p t c", c=256)]
        xv, av, hv = vals(XV, 256), vals(AV, T), vals(HV, 256)

        ORDER = [("gu00", FC, DC * 256, 1), ("dn00", 2 * DC, FC // 2 * P, 0), ("hyb", 10, DC * 256, 0),
                 ("hybv", 4, DC * 256, 0), ("hybo", 4, DC * 256, 0), ("gu01", FC, DC * 256, 1),
                 ("dn01", 2 * DC, FC // 2 * P, 0), ("gu10", FC, DC * 256, 1), ("dn10", 2 * DC, FC // 2 * P, 0),
                 ("mlad", 3, DC * 256, 0), ("mlaq", 6, 3 * 256, 0), ("mlak", 4, 2 * 256, 0),
                 ("mlav", 4, 2 * 256, 0), ("mlao", 4, DC * 256, 0), ("gu11", FC, DC * 256, 0),
                 ("dn11", 2 * DC, FC // 2 * P, 0)]
        for l in range(DEPTH):
            ORDER += [(f"in{l}", 11, DC * 256, 0), (f"inv{l}", 4, DC * 256, 0), (f"wo{l}", 4, DC * 256, 0),
                      (f"up{l}", 16, DC * 256, 0), (f"down{l}", 16, 16 * P, 0)]
        WIDTH = {name: (n, width, ada) for name, n, width, ada in ORDER}

        def beside(pl, name):
            n, _, ada = WIDTH[name]
            return min(n, N_ADA - (UP0 + 1) - pl.ada) if ada else 0

        block = ctx.enter_context(nc.Block())

        @block.sync
        def _(sp):
            pl = Place(sp, s)
            for dst, src in ((sm[:, :], small), (cst[:, :], consts), (h[:, :, :], x),
                             (sq[:, 0, :].bitcast(I32), pos), (modb[:, :], adab)):
                sp.dma_start(dst, src).then_inc(s("const_in"), 16)

            def load_ada(a, it):
                if a >= 2:
                    sp.wait_ge(s("ada_summed"), at(a - 1, it, RING))
                src = w["ada"][a] if isinstance(it, int) else w["ada"][it * RING + a]
                sp.dma_start(ada_in[:, a % 2, :], src).then_inc(s(f"ada_in{a % 2}"), 16)

            for a in range(UP0 + 1):
                load_ada(a, 0)
            consts2_at = "gu11"
            for name, n, width, _ in ORDER:
                n_ada = beside(pl, name)
                if name == consts2_at:
                    sp.wait_ge(s("ada_summed"), N_ADA)
                    sp.dma_start(cst2[:, 0:NCONST2], consts2).then_inc(s("const2_in"), 16)

                def load(k, it):
                    slab = pl.slab + k
                    if slab >= RING:
                        sp.wait_ge(s("lin_done"), at(slab - RING + 1, it, RING))
                    src = w[name][k] if isinstance(it, int) else w[name][it * RING + k]
                    sp.dma_start(ring[:, slab % RING, 0:width], src).then_inc(s(f"w_in{slab % RING}"), 16)
                    if n_ada == n or k < n_ada:
                        load_ada(UP0 + 1 + pl.ada + k, it)

                slab_loop(sp, n, load, peel=4 if pl.slab == 0 else n_ada if n_ada < n else 0)
                pl.slab += n
                pl.ada += n_ada
            sp.wait_ge(s("lin_taken0"), GROUPS // 2 + GROUPS % 2)
            sp.wait_ge(s("lin_taken1"), GROUPS // 2)
            sp.dma_start(out, h[:, :, :]).then_inc(s("out_stored"), 16)
            sp.wait_ge(s("out_stored"), 16)

        @block.tensor
        def _(pe):
            pl = Place(pe, s)

            def mm(o, lhsT, rhs, start=True, stop=True):
                return pe.matmul(o, lhsT=lhsT, rhs=rhs, start=start, stop=stop)

            def ada_sum(a, it):
                pe.wait_ge(s("ada_summed"), at(a + 1, it, RING))
                for f in range(2):
                    last = mm(XB[3][:, f:f + 1], ada_acc[:, f * P:(f + 1) * P], cc("ones", 0, 1))
                last.then_inc(s("ada_col"), 1)

            def linear(name, kind, src, parts=1):
                n, width, _ = WIDTH[name]
                n_ada = beside(pl, name)

                def body(k, it):
                    slab, group = pl.slab + k, pl.group + k // parts
                    slot, p = slab % RING, group % 2
                    per = RING // parts // 2
                    if k % parts == 0 and group >= 2:
                        pe.wait_ge(s(f"lin_taken{p}"), at(group // 2, it, per))
                    pe.wait_ge(s(f"w_in{slot}"), at(16 * (slab // RING + 1), it, 16))
                    r = ring[:, slot, 0:width]
                    if kind == "down":
                        kc = width // P
                        for c in range(kc):
                            last = mm(LP[p][:, 0, :], r[:, blk(c)], src((k % parts) * kc + c),
                                      start=c == 0 and k % parts == 0, stop=c == kc - 1 and k % parts == parts - 1)
                    elif kind == "fm":
                        kc = width // 256
                        for f in range(2):
                            for c in range(kc):
                                last = mm(LP[p][:, f, :], r[:, c * 256 + f * P:c * 256 + f * P + P], src(c),
                                          start=c == 0, stop=c == kc - 1)
                    else:
                        kc = width // 256
                        for b in range(NB):
                            for c in range(kc):
                                last = mm(LPF[p][:, b * 256:(b + 1) * 256], src(c)[:, blk(b)],
                                          r[:, c * 256:(c + 1) * 256], start=c == 0, stop=c == kc - 1)
                    last.then_inc(s("lin_done"), 1)
                    if n_ada == n or k < n_ada:
                        ada_sum(UP0 + pl.ada + k, it)

                slab_loop(pe, n, body, peel=4 if pl.slab == 0 else n_ada if n_ada < n else 0)
                pl.slab += n
                pl.group += n // parts
                pl.ada += n_ada

            def square_sum(n, weights):
                if pl.norm:
                    pe.wait_ge(s("rt_ready"), pl.norm)
                for c in range(n):
                    pe.wait_ge(s("sq_ready"), pl.sq + c + 1)
                    mm(XB[0][:, :], weights, sq[:, c % 2, :], start=c == 0, stop=c == n - 1)\
                        .then_inc(s("sq_used"), 1)
                pl.sq += n
                pl.norm += 1

            def norm(modulated):
                square_sum(DC, cc("ones"))
                pl.tu += DC
                if modulated:
                    pl.ur += DC
                    pe.wait_ge(s("u_ready"), pl.ur)
                else:
                    pe.wait_ge(s("u_scaled"), pl.tu)

            def ffn(up, down):
                norm(True)
                linear(up, "fm", lambda c: u[:, c, :])
                if up == "gu10":
                    ada_sum(N_ADA - 1, 0)
                pl.groups_taken()
                linear(down, "down", lambda c: big[:, c, :], parts=2)

            def rotate(chunks, weights):
                for i, c in enumerate(chunks):
                    if pl.rope + i >= 2:
                        pe.wait_ge(s("rope_done"), pl.rope + i - 1)
                    mm(XB[1 + (pl.rope + i) % 2][:, :], weights, big[:, c, :]).then_inc(s("rot_done"), 1)
                pl.rope += len(chunks)

            def attention(heads, score, val, hd, maps=1):
                per = P // hd
                n_units = heads * NB
                pl.groups_taken()
                if pl.rope:
                    pe.wait_ge(s("rope_done"), pl.rope)
                u0, p0, h0 = pl.unit, pl.prob, pl.head
                for n in range(n_units + 2):
                    if n < n_units:
                        hh, qb = divmod(n, NB)
                        for m in range(maps):
                            k = u0 + n * maps + m
                            if k >= 2:
                                pe.wait_ge(s("smax_done"), k - 1)
                            score(hh, m, qb, XB[k % 2]).then_inc(s("scores_done"), 1)
                    if 0 <= n - 1 < n_units:
                        i, qb = n - 1, (n - 1) % NB
                        k = p0 + i
                        if k >= 2:
                            pe.wait_ge(s("pt_done"), k - 1)
                        pe.wait_ge(s("probs_done"), k + 1)
                        src = wk[:, 4 + k % 2, :] if maps == 2 else E[:, k % 4, :]
                        for b in range(qb + 1):
                            last = pe.transpose(XB[2 + k % 2][:, blk(b)], src[:, blk(b)], cc("ident"))
                        last.then_inc(s("transposed"), 1)
                    if n >= 2:
                        i = n - 2
                        hh, qb = divmod(i, NB)
                        k, g = p0 + i, h0 + hh // per
                        if i % (per * NB) == 0 and g >= 2:
                            pe.wait_ge(s("o_taken"), g - 1)
                        pe.wait_ge(s("pt_done"), k + 1)
                        o = LP[0][half(hh) if per == 2 else slice(0, P), g % 2, blk(qb)]
                        for b in range(qb + 1):
                            last = mm(o, val(hh, b), ET[:, k % 2, blk(b)], start=b == 0, stop=b == qb)
                        last.then_inc(s("pv_done"), 1)
                pl.unit += n_units * maps
                pl.prob += n_units
                pl.head += heads // per

            pe.wait_ge(s("const_in"), 80)
            for a in range(UP0):
                if a:
                    pe.wait_ge(s("ada_done"), a)
                ada_sum(a, 0)
            ffn("gu00", "dn00")

            norm(True)
            linear("hyb", "fm", lambda c: u[:, c, :])
            linear("hybv", "tm", lambda c: u[:, c, :])
            rotate(list(range(DQ, DQ + 8)) + [IQ, IQ + 1, IK], cc("rot16"))
            for b in range(NB):
                last = mm(XB[3][:, 4 * b:4 * b + 4], big[32:36, GT, blk(b)], cc("ident")[32:36, 32:36])
            last.then_inc(s("iw_raw"), 1)

            def fox_score(hh, _, qb, bank):
                W = (qb + 1) * P
                r, o = half(hh), bank[:, 0:(qb + 1) * P]
                mm(o, big[r, FQ + hh // 2, blk(qb)], big[r, FK + hh // 2, 0:W], stop=False)
                one = cc("ident")[0:8, hh:hh + 1]
                mm(o, gate_row(slice(0, 8), 3)[:, blk(qb)], one.to_broadcast([8, W]), start=False, stop=False)
                return mm(o, one.to_broadcast([8, P]), gate_row(slice(0, 8), 0)[:, 0:W], start=False)

            pl.got("cum_ready")
            attention(FOX_H, fox_score, lambda hh, b: fv[:, b, 64 * hh:64 * hh + 64], 64)

            pe.wait_ge(s("smax_done"), pl.unit)
            for n in range(3 * IDX_H):
                qb, i = n // IDX_H + 1, n % IDX_H
                if n >= 2:
                    pe.wait_ge(s("idx_relu"), n - 1)
                mm(XB[n % 2][:, 0:(qb + 1) * P], big[half(i), IQ + i // 2, blk(qb)],
                   big[half(i), IK, 0:(qb + 1) * P]).then_inc(s("idx_done"), 1)
            pe.wait_ge(s("idx_relu"), 3 * IDX_H)

            def dsa_score(hh, _, qb, bank):
                r = half(hh)
                return mm(bank[:, 0:(qb + 1) * P], big[r, DQ + hh // 2, blk(qb)],
                          big[r, DK + hh // 2, 0:(qb + 1) * P])

            attention(DSA_H, dsa_score, lambda hh, b: dv[:, b, 64 * hh:64 * hh + 64], 64)
            pe.wait_ge(s("o_taken"), pl.head)
            linear("hybo", "fm", lambda c: u[:, c, :])
            ffn("gu01", "dn01")

            ffn("gu10", "dn10")
            norm(True)
            linear("mlad", "fm", lambda c: u[:, c, :])
            square_sum(3, cc("ones"))
            square_sum(2, cc("ones"))
            pl.got("latent_ready", 2)
            linear("mlaq", "fm", lambda c: big[:, CQ + c, :])
            linear("mlak", "fm", lambda c: big[:, CKV + c, :])
            linear("mlav", "tm", lambda c: big[:, CKV + c, :])
            rotate([KR] + list(range(QR, QR + 4)), cc("rot64"))

            def mla_score(hh, _, qb, bank):
                W = (qb + 1) * P
                mm(bank[:, 0:W], big[:, QN + hh, blk(qb)], big[:, KN + hh, 0:W], stop=False)
                return mm(bank[:, 0:W], big[half(hh), QR + hh // 2, blk(qb)], big[half(hh), KR, 0:W],
                          start=False)

            attention(MLA_H, mla_score, lambda hh, b: mv[hh // 2][:, b, blk(hh % 2)], P)
            pe.wait_ge(s("o_taken"), pl.head)
            linear("mlao", "fm", lambda c: u[:, c, :])
            ffn("gu11", "dn11")

            pe.wait_ge(s("const2_in"), 16)
            square_sum(DC, cc("ones"))
            pl.tu += DC
            for l in range(DEPTH):
                norm(False)
                linear(f"in{l}", "fm", lambda c: u[:, c, :])
                linear(f"inv{l}", "tm", lambda c: u[:, c, :])

                for i in range(8):
                    square_sum(1, cc("blk64"))
                pl.got("qk_normed", 8)
                rotate(range(AQ, AQ + 8), cc("rot16"))

                def diff_score(hh, m, qb, bank):
                    return mm(bank[:, 0:(qb + 1) * P], big[half(m), AQ + hh, blk(qb)],
                              big[half(m), AK + hh, 0:(qb + 1) * P])

                attention(DIFF_H, diff_score, lambda hh, b: av[:, b, blk(hh)], P, maps=2)
                for i in range(DIFF_H):
                    square_sum(1, cc("ones"))

                pl.got("gates_rows")
                for b in range(NB):
                    last = mm(XB[3][:, 4 * b:4 * b + 4], gate_row(slice(0, 4), 3)[:, blk(b)], cc("ident")[0:4, 0:4])
                last.then_inc(s("a_cols"), 1)
                pl.got("conv_silu", 4)
                u0 = l * 4 * NB

                def weighted(n):
                    hh, b = divmod(n, NB)
                    pe.wait_ge(s("ms_ready"), u0 + n + 1)
                    o = (half(hh), hh // 2, slice(b * P, T))
                    mm(LP[0][o], xv[:, b, 64 * hh:64 * hh + 64], S[:, n % 2, 0:T - b * P],
                       start=b == 0, stop=b == NB - 1)
                    mm(LP[1][o], cc("ones", 0, 64), S[:, n % 2, 0:T - b * P],
                       start=b == 0, stop=b == NB - 1).then_inc(s("m_out"), 1)

                for n in range(4 * NB + 1):
                    hh, b = divmod(n, NB)
                    if n < 4 * NB:
                        if b == 0:
                            if l * 4 + hh:
                                pe.wait_ge(s("g_taken"), l * 4 + hh)
                            mm(XB[0][:, :], cc("ident")[0:4, hh:hh + 1].to_broadcast([4, P]),
                               gate_row(slice(0, 4), 5)).then_inc(s("g_ready"), 1)
                        if u0 + n >= 2:
                            pe.wait_ge(s("ms_ready"), u0 + n - 1)
                        mm(XB[1 + n % 2][:, 0:T - b * P], big[half(hh), XK + hh // 2, blk(b)],
                           big[half(hh), XQ + hh // 2, b * P:T]).then_inc(s("mqk_done"), 1)
                    if n:
                        weighted(n - 1)
                pl.got("em_rows")
                for cp in range(2):
                    if cp:
                        pl.got("em_taken")
                    mm(XB[3][:, :], cc("sel4", cp * P, P)[0:4, :], gate_row(slice(0, 4), 6)).then_inc(s("em_ready"), 1)
                    square_sum(1, cc("blk64"))
                pl.got("em_taken")

                for cp in range(2):
                    for step in range(10):
                        pl.got("z_ready")
                        for j in range(2):
                            k = (l * 2 + cp) * 20 + 2 * step + j
                            r = half(j)
                            if k >= 4:
                                pe.wait_ge(s("level_taken"), k - 3)
                            bank, z = XB[k % 4], E[r, step % 2, :]
                            if step == 0:
                                for b in range(NB):
                                    last = mm(bank[:, blk(b)], big[r, SP + cp, blk(b)], big[r, HQ + cp, blk(b)])
                            elif step < 8:
                                for b in range(NB):
                                    last = mm(bank[:, blk(b)], z[:, blk(b)], z[:, blk(b)])
                            elif step == 8:
                                for i, b in enumerate((0, 2)):
                                    last = mm(bank[:, blk(i)], z[:, blk(b)], z[:, blk(b + 1)])
                            else:
                                for b in range(2):
                                    last = mm(bank[:, b * 256:b * 256 + 256], z[:, blk(b)], z[:, 256:T])
                            last.then_inc(s("level_mm"), 1)
                    pl.got("a_done")
                    for j in range(2):
                        for b in range(NB):
                            v = hv[:, b, 64 * (2 * cp + j):64 * (2 * cp + j) + 64]
                            last = mm(LP[0][half(j), cp, blk(b)], v, wk[:, 2 + j, blk(b)],
                                      start=b == 0, stop=b == NB - 1)
                            if b < NB - 1:
                                o = (0, 384, 640)[b]
                                mm(LP[0][half(j), cp, (b + 1) * P:T], v,
                                   tmp[:, j, o:o + (NB - 1 - b) * P], start=False, stop=False)
                    last.then_inc(s("h_out"), 1)
                    square_sum(1, cc("blk64"))
                pl.got("mix_ready")
                linear(f"wo{l}", "fm", lambda c: u[:, c, :])
                norm(False)
                linear(f"up{l}", "fm", lambda c: u[:, c, :])
                pl.groups_taken()
                linear(f"down{l}", "down", lambda c: big[:, c, :], parts=2)

        @block.scalar
        def _(act):
            pl = Place(act, s)

            def f(o, i, fn, **kw):
                return act.activation(o, i, fn, **kw)

            def rms(srcs, size):
                for c, src in enumerate(srcs):
                    if pl.sq + c >= 2:
                        act.wait_ge(s("sq_used"), pl.sq + c - 1)
                    f(sq[:, c % 2, :], src, ACT.Square).then_inc(s("sq_ready"), 1)
                pl.sq += len(srcs)
                act.wait_ge(s("sq_used"), pl.sq)
                if pl.norm:
                    act.wait_ge(s("rstd_ready"), pl.norm)
                f(rt[:, :], XB[0][:, :], ACT.Sqrt, scale=1.0 / size, bias=cc("eps")).then_inc(s("rt_ready"), 1)
                pl.norm += 1

            def hrms():
                pl.groups_taken()
                rms([h[:, c, :] for c in range(DC)], D)

            def skip(name, parts=1):
                n = WIDTH[name][0]
                pl.slab += n
                pl.group += n // parts

            def ffn(up, down):
                hrms()
                silu0 = pl.slab

                def body(k, it):
                    act.wait_ge(s("lin_done"), at(silu0 + k + 1, it, RING))
                    p = (pl.group + k) % 2
                    f(tmp[:, p, 0:T], LP[p][:, 0, :], ACT.Silu).then_inc(s("silu_done"), 1)

                n_ada = beside(pl, up)
                slab_loop(act, FC, body, peel=4 if pl.slab == 0 else n_ada if 0 < n_ada < FC else 0)
                pl.ada += n_ada
                skip(up)
                skip(down, 2)

            def attention(heads, scale, hd, maps=1):
                n_units = heads * NB
                u0, p0 = pl.unit, pl.prob
                for n in range(n_units + 1):
                    if n < n_units:
                        W = (n % NB + 1) * P
                        for m in range(maps):
                            k = u0 + n * maps + m
                            act.wait_ge(s("smax_done"), k + 1)
                            if maps == 2:
                                if p0 + n >= 2:
                                    act.wait_ge(s("probs_done"), p0 + n - 1)
                            elif p0 + n >= 4:
                                act.wait_ge(s("transposed"), p0 + n - 3)
                            e = (2 * (p0 + n) + m) % 4 if maps == 2 else (p0 + n) % 4
                            f(E[:, e, 0:W], S[:, k % 2, 0:W], ACT.Exp, scale=scale, bias=stat[:, k % 4, 0:1],
                              accum_out=stat[:, k % 4, 1:2]).then_inc(s("exp_done"), 1)
                    if n:
                        k = p0 + n - 1
                        W = ((n - 1) % NB + 1) * P
                        act.wait_ge(s("transposed"), k + 1)
                        if k >= 2:
                            act.wait_ge(s("pv_done"), k - 1)
                        f(ET[:, k % 2, 0:W], XB[2 + k % 2][:, 0:W], ACT.Copy).then_inc(s("pt_done"), 1)
                pl.unit += n_units * maps
                pl.prob += n_units

            act.wait_ge(s("const_in"), 80)
            f(csil[:, :], sp_("cond", 0, DC), ACT.Silu).then_inc(s("cond_ready"), 1)
            for i in range(4):
                pl.got("ang_ready")
                f(tabs[:, i, :], wk[:, 4 + i % 2, :], ACT.Sin).then_inc(s("tab_ready"), 1)
            ffn("gu00", "dn00")

            hrms()
            skip("hyb")
            skip("hybv")

            def log_sigmoid_parts(row):
                pl.got("gate_abs")
                r = slice(0, row)
                f(gate_row(r, 2), gate_row(r, 2), ACT.Exp, scale=-1.0).then_inc(s("scalar_chain"), 1)
                pl.got("scalar_chain")
                f(gate_row(r, 2), gate_row(r, 2), ACT.Ln, bias=1.0).then_inc(s("gate_ln"), 1)

            log_sigmoid_parts(8)
            attention(FOX_H, 0.125, 64)
            for n in range(3 * IDX_H):
                act.wait_ge(s("idx_done"), n + 1)
                if n >= 2:
                    act.wait_ge(s("idx_used"), n - 1)
                W = (n // IDX_H + 2) * P
                f(S[:, n % 2, 0:W], XB[n % 2][:, 0:W], ACT.Relu, scale=0.125).then_inc(s("idx_relu"), 1)
            attention(DSA_H, 0.125, 64)
            skip("hybo")
            ffn("gu01", "dn01")

            ffn("gu10", "dn10")
            hrms()
            skip("mlad")
            pl.groups_taken()
            rms([big[:, CQ + c, :] for c in range(3)], 384)
            rms([big[:, CKV + c, :] for c in range(2)], 256)
            skip("mlaq")
            skip("mlak")
            skip("mlav")
            attention(MLA_H, 192.0 ** -0.5, P)
            skip("mlao")
            ffn("gu11", "dn11")

            hrms()
            pl.tu += DC
            act.wait_ge(s("u_scaled"), 7 * DC)
            pl.got("lb_shifted")
            f(st[:, 22:26], st[:, 18:22], ACT.Exp).then_inc(s("lb_exp"), 1)
            pl.got("lam_dots")
            f(st[:, 46:50], st[:, 42:46], ACT.Exp).then_inc(s("lam_exp"), 1)
            for l in range(DEPTH):
                if l == 0:
                    rms([h[:, c, :] for c in range(DC)], D)
                else:
                    hrms()
                skip(f"in{l}")
                skip(f"inv{l}")
                pl.groups_taken()
                for c in range(8):
                    rms([big[:, AQ + c, :]], 64)
                attention(DIFF_H, 0.125, P, maps=2)
                act.wait_ge(s("o_taken"), 4 + 4 + 8 + 4 * (l + 1))
                for c in range(DIFF_H):
                    rms([u[:, 2 + c, :]], P)

                for c in range(4):
                    pl.got("conv_raw")
                    f(big[:, XQ + c, :], wk[:, c % 2, :], ACT.Silu).then_inc(s("conv_silu"), 1)
                for c in range(2):
                    f(big[:, XO + c, :], big[:, XO + c, :], ACT.Sigmoid).then_inc(s("o_sigmoid"), 1)
                log_sigmoid_parts(4)
                pl.got("em_log")
                f(gate_row(slice(0, 4), 6), gate_row(slice(0, 4), 6), ACT.Exp, scale=-1.0).then_inc(s("em_rows"), 1)
                for n in range(4 * NB):
                    hh, b = divmod(n, NB)
                    pl.got("g_diag")
                    bias = tokw[:, 4 * b + hh:4 * b + hh + 1]
                    last = f(E[:, n % 4, 0:P], wk[:, 2 + n % 2, 0:P], ACT.Exp, bias=bias)
                    if b < NB - 1:
                        last = f(E[:, n % 4, P:T - b * P], wk[:, hh % 2, (b + 1) * P:T], ACT.Exp, bias=bias)
                    last.then_inc(s("me_done"), 1)
                for cp in range(2):
                    pl.got("m_mix")
                    rms([u[:, cp, :]], 64)

                for cp in range(2):
                    f(big[:, HQ + cp, :], big[:, HQ + cp, :], ACT.Silu)
                    f(big[:, HG + cp, :], big[:, HG + cp, :], ACT.Silu)
                    f(wk[:, 4, :], big[:, HF + cp, :], ACT.Sigmoid, scale=-1.0).then_inc(s("scalar_chain"), 1)
                    pl.got("scalar_chain")
                    f(big[:, HF + cp, :], big[:, HF + cp, :], ACT.Sigmoid).then_inc(s("h_sig"), 1)
                    pl.got("h_f")
                    f(big[:, HF + cp, :], big[:, HF + cp, :], ACT.Ln).then_inc(s("h_lnf"), 1)
                    for step in range(1, 10):
                        pl.got("x_ready")
                        k = (l * 2 + cp) * 10 + step
                        act.wait_ge(s("z_ready"), k - 1)
                        f(S[:, step % 2, :], wk[:, step % 2, :], ACT.Exp).then_inc(s("ex_ready"), 1)
                    pl.got("h_mix")
                    rms([u[:, 6 + cp, :]], 64)
                skip(f"wo{l}")
                hrms()
                g0, s0 = pl.group, pl.slab

                def relu(k, it):
                    act.wait_ge(s("lin_done"), at(s0 + k + 1, it, RING))
                    p = (g0 + k) % 2
                    f(tmp[:, p, :], LPF[p], ACT.Relu).then_inc(s("silu_done"), 1)

                slab_loop(act, 16, relu)
                skip(f"up{l}")
                skip(f"down{l}", 2)

        @block.gpsimd
        def _(gp):
            pl = Place(gp, s)
            norms = [0]

            def shift(l, j):
                for c in range(DC):
                    gp.wait_ge(s("u_scaled"), pl.tu + c + 1)
                    m = (l * N_MOD + 3 * j) * DC + c
                    gp.tensor_scalar(u[:, c, :], u[:, c, :], mod[:, m:m + 1], None, ALU.add)\
                        .then_inc(s("u_ready"), 1)
                pl.tu += DC

            def turn(chunks, t):
                for i, c in enumerate(chunks):
                    k = pl.rope + i
                    if k >= 2:
                        gp.wait_ge(s("rope_done"), k - 1)
                    gp.wait_ge(s("rot_done"), k + 1)
                    gp.tensor_tensor(S[:, k % 2, :], big[:, c, :], t, ALU.mult).then_inc(s("rope_cos"), 1)
                pl.rope += len(chunks)

            gp.wait_ge(s("const_in"), 80)
            shift(0, 0)
            shift(0, 1)
            turn(list(range(DQ, DQ + 8)) + [IQ, IQ + 1, IK], tabs[:, 1, :])
            shift(0, 2)
            shift(1, 0)
            shift(1, 1)
            turn([KR] + list(range(QR, QR + 4)), tabs[:, 3, :])
            shift(1, 2)
            gp.wait_ge(s("const2_in"), 16)
            for l in range(DEPTH):
                turn(range(AQ, AQ + 8), cc("diff_cos"))
                for cp in range(2):
                    pl.got("h_kb")
                    for step in range(10):
                        k = (l * 2 + cp) * 10 + step
                        if step == 0:
                            gp.nop().then_inc(s("z_ready"), 1)
                            continue
                        pl.got("ex_ready")
                        b = 1 << (step - 1)
                        if k >= 2:
                            gp.wait_ge(s("level_mm"), 2 * (k - 1))
                        z, e, kk, q = (t.rearrange("p (j i b) -> p j i b", i=2, b=b) for t in
                                       (E[:, step % 2, :], S[:, step % 2, :], big[:, SP + cp, :], big[:, HQ + cp, :]))
                        gp.tensor_tensor(z[:, :, 0, :], e[:, :, 0, :], kk[:, :, 0, :], ALU.mult)
                        gp.tensor_tensor(z[:, :, 1, :], e[:, :, 1, :], q[:, :, 1, :], ALU.mult)\
                            .then_inc(s("z_ready"), 1)

        @block.vector
        def _(dve):
            pl = Place(dve, s)
            link = Chain(dve, s("vector_chain"))
            tt, ts, stt = dve.tensor_tensor, dve.tensor_scalar, dve.scalar_tensor_tensor

            def ada_acc_(a, it):
                dve.wait_ge(s(f"ada_in{a % 2}"), at(16 * (a // 2 + 1), it, 16 * RING // 2))
                wv = ada_in[:, a % 2, :]
                link(ts(ada_acc[:, :], wv[:, 0:256], csil[:, 0:1], None, ALU.mult))
                for c in range(1, DC):
                    ins = stt(ada_acc[:, :], wv[:, c * 256:(c + 1) * 256], csil[:, c:c + 1], ada_acc[:, :],
                              ALU.mult, ALU.add)
                    if c < DC - 1:
                        link(ins)
                ins.then_inc(s("ada_summed"), 1)

            def ada_take(a, it):
                dve.wait_ge(s("ada_col"), at(a + 1, it, RING))
                if isinstance(it, int):
                    o, b = mod[:, 2 * a:2 * a + 2], modb[:, 2 * a:2 * a + 2]
                else:
                    o, b = (t[:, bass.ds(it * 2 * RING + 2 * a, 2)] for t in (mod, modb))
                tt(o, XB[3][:, 0:2], b, ALU.add).then_inc(s("ada_done"), 1)

            def take(name, body, parts=1, chains=()):
                n = WIDTH[name][0]
                n_ada = beside(pl, name)

                def one(k, it):
                    last_slab = pl.slab + (k + 1) * parts
                    dve.wait_ge(s("lin_done"), at(last_slab, it, RING))
                    body(k, it, (pl.group + k) % 2)
                    if n_ada == n or k < n_ada:
                        ada_take(UP0 + pl.ada + k, it)
                        a = UP0 + 1 + pl.ada + k
                        if a < N_ADA or not isinstance(it, int):
                            ada_acc_(a, it)

                slab_loop(dve, n // parts, one, unroll=RING // parts,
                          chains=[(link, DC - 1)] if n_ada == n else (),
                          peel=4 if pl.slab == 0 else n_ada if n_ada < n else 0)
                pl.slab += n
                pl.group += n // parts
                pl.ada += n_ada

            def dyn(t, k, it, step, n):
                a = step * k
                return slice(a, a + n) if isinstance(it, int) else bass.ds(it * step * RING + a, n)

            def root():
                dve.wait_ge(s("rt_ready"), pl.norm + 1)
                pl.norm += 1
                dve.reciprocal(rstd[:, :], rt[:, :]).then_inc(s("rstd_ready"), 1)
                dve.wait_ge(s("rstd_ready"), pl.norm)

            def scale_in(dst, gains):
                root()
                for c in range(DC):
                    stt(dst[:, c, :], h[:, c, :], gains[:, c:c + 1], rstd[:, :], ALU.mult, ALU.mult)\
                        .then_inc(s("u_scaled"), 1)
                pl.tu += DC

            def mod_vec(l, j):
                return mod[:, (l * N_MOD + j) * DC:(l * N_MOD + j + 1) * DC]

            def ada_ready(n):
                dve.wait_ge(s("ada_done"), n)

            def mod_in(l, j):
                ada_ready(min(N_ADA, ((l * N_MOD + 3 * j + 2) * DC) // 2))
                link(stt(gain[:, :], mod_vec(l, 3 * j + 1), 1.0, sp_("norm_g", (l * 3 + j) * DC, DC),
                         ALU.add, ALU.mult))
                scale_in(u, gain)

            def mod_gate(l, j, weight):
                ada_ready(min(N_ADA, ((l * N_MOD + 3 * j + 3) * DC) // 2))
                link(ts(gate[:, :], mod_vec(l, 3 * j + 2), weight, None, ALU.mult))

            def hidden(k, it, p):
                dve.wait_ge(s("silu_done"), at(pl.silu + k + 1, it, RING))
                tt(big[:, dyn(big, k, it, 1, 1), :], tmp[:, p, 0:T].unsqueeze(1), LP[p][:, 1:2, :], ALU.mult)\
                    .then_inc(s(f"lin_taken{p}"), 1)

            def ffn(l, j, up, down):
                mod_in(l, j)
                take(up, hidden)
                pl.silu += FC
                if up == "gu10":
                    ada_take(N_ADA - 1, 0)
                mod_gate(l, j, 0.5)

                def add(k, it, p):
                    at_ = slice(k, k + 1) if isinstance(it, int) else bass.ds(it * (RING // 2) + k, 1)
                    o, g = h[:, at_, :], gate[:, at_]
                    stt(o, LP[p][:, 0:1, :], g, o, ALU.mult, ALU.add).then_inc(s(f"lin_taken{p}"), 1)
                take(down, add, parts=2)

            def residual(l, j, name):
                mod_gate(l, j, 1.0)

                def add(k, it, p):
                    for i in range(2):
                        c = 2 * k + i
                        ins = stt(h[:, c, :], LP[p][:, i, :], gate[:, c:c + 1], h[:, c, :], ALU.mult, ALU.add)
                    ins.then_inc(s(f"lin_taken{p}"), 1)
                take(name, add)

            def plain(dst0):
                def body(k, it, p):
                    ts(big[:, bass.ds(it * 2 * RING + 2 * k + dst0, 2) if not isinstance(it, int)
                           else slice(dst0 + 2 * k, dst0 + 2 * k + 2), :], LP[p][:, :, :], 1.0, None, ALU.mult)\
                        .then_inc(s(f"lin_taken{p}"), 1)
                return body

            def tokens(dsts):
                def body(k, it, p):
                    ts(dsts[k], LPF[p].rearrange("p (t c) -> p t c", c=256), 1.0, None, ALU.mult)\
                        .then_inc(s(f"lin_taken{p}"), 1)
                return body

            def turn(chunks, t):
                for i, c in enumerate(chunks):
                    k = pl.rope + i
                    dve.wait_ge(s("rot_done"), k + 1)
                    link(tt(wk[:, k % 2, :], t, XB[1 + k % 2][:, :], ALU.mult))
                    dve.wait_ge(s("rope_cos"), k + 1)
                    tt(big[:, c, :], wk[:, k % 2, :], S[:, k % 2, :], ALU.add).then_inc(s("rope_done"), 1)
                pl.rope += len(chunks)
                dve.wait_ge(s("rope_done"), pl.rope)

            def attention(heads, scale, hd, mask, dst, maps=1, lam=None):
                per = P // hd
                n_units = heads * NB
                u0, p0, h0 = pl.unit, pl.prob, pl.head

                def out_of(g):
                    dve.wait_ge(s("pv_done"), p0 + (g + 1) * per * NB)
                    dve.tensor_copy(u[:, dst + g, :], LP[0][:, (h0 + g) % 2, :]).then_inc(s("o_taken"), 1)

                for n in range(n_units + 2):
                    if n < n_units:
                        qb = n % NB
                        W = (qb + 1) * P
                        for m in range(maps):
                            k = u0 + n * maps + m
                            dve.wait_ge(s("scores_done"), k + 1)
                            if k >= 2:
                                dve.wait_ge(s("exp_done"), k - 1)
                            link(dve.tensor_tensor_reduce(
                                out=S[:, k % 2, 0:W], in0=XB[k % 2][:, 0:W], in1=mask(qb, W), scale=1.0,
                                scalar=LOWEST, op0=ALU.add, op1=ALU.max, accum_out=stat[:, k % 4, 2:3]))
                            ts(stat[:, k % 4, 0:1], stat[:, k % 4, 2:3], -scale, None, ALU.mult)\
                                .then_inc(s("smax_done"), 1)
                    if 1 <= n <= n_units:
                        i = n - 1
                        W = (i % NB + 1) * P
                        k = p0 + i
                        for m in range(maps):
                            q = u0 + i * maps + m
                            dve.wait_ge(s("exp_done"), q + 1)
                            link(dve.reciprocal(stat[:, q % 4, 3:4], stat[:, q % 4, 1:2]))
                        if maps == 1:
                            ts(E[:, k % 4, 0:W], E[:, k % 4, 0:W], stat[:, q % 4, 3:4], None, ALU.mult)\
                                .then_inc(s("probs_done"), 1)
                        else:
                            q0 = u0 + 2 * i
                            link(ts(stat[:, q % 4, 3:4], stat[:, q % 4, 3:4], lam, None, ALU.mult))
                            link(ts(wk[:, 3, 0:W], E[:, 2 * k % 4, 0:W], stat[:, q0 % 4, 3:4], None, ALU.mult))
                            if k >= 2:
                                dve.wait_ge(s("transposed"), k - 1)
                            stt(wk[:, 4 + k % 2, 0:W], E[:, (2 * k + 1) % 4, 0:W], stat[:, q % 4, 3:4],
                                wk[:, 3, 0:W], ALU.mult, ALU.add).then_inc(s("probs_done"), 1)
                    if n >= 2 and (n - 1) % (per * NB) == 0:
                        out_of((n - 1) // (per * NB) - 1)
                pl.unit += n_units * maps
                pl.prob += n_units
                pl.head += heads // per

            def log_sigmoid(src, rows, bias):
                link(ts(gate_row(rows, 0), src, bias, None, ALU.add))
                link(ts(gate_row(rows, 1), gate_row(rows, 0), 0.0, None, ALU.min))
                stt(gate_row(rows, 2), gate_row(rows, 0), -1.0, gate_row(rows, 0), ALU.mult, ALU.max).then_inc(s("gate_abs"), 1)
                pl.got("gate_ln")
                link(tt(gate_row(rows, 0), gate_row(rows, 1), gate_row(rows, 2), ALU.subtract))

            dve.wait_ge(s("const_in"), 80)
            dve.wait_ge(s("cond_ready"), 1)
            ada_acc_(0, 0)
            for a in range(UP0):
                ada_take(a, 0)
                ada_acc_(a + 1, 0)

            C1 = 6.28125
            C2 = float(np.float32(2 * math.pi - C1).view(np.int32) & ~0xfff and
                       (np.array(2 * math.pi - C1, np.float32).view(np.int32) & np.int32(~0xfff)).view(np.float32))
            C3 = 2 * math.pi - C1 - C2
            MAGIC = 1.5 * 2 ** 23
            link(dve.tensor_copy(wk[:, 0, :], sq[:, 0, :].bitcast(I32)))
            for i, (freq, quarter) in enumerate((("invf16", 0), ("invf16", 1), ("invf64", 0), ("invf64", 1))):
                o = 4 + i % 2
                if i >= 2:
                    dve.wait_ge(s("tab_ready"), i - 1)
                link(ts(wk[:, 1, :], wk[:, 0, :], cc(freq), None, ALU.mult))
                link(ts(wk[:, 2, :], wk[:, 1, :], 1 / (2 * math.pi), 0.25 * quarter, ALU.mult, ALU.add))
                link(ts(wk[:, 2, :], wk[:, 2, :], MAGIC, None, ALU.add))
                link(ts(wk[:, 2, :], wk[:, 2, :], MAGIC, None, ALU.subtract))
                link(stt(wk[:, 1, :], wk[:, 2, :], -C1, wk[:, 1, :], ALU.mult, ALU.add))
                link(stt(wk[:, 1, :], wk[:, 2, :], -C2, wk[:, 1, :], ALU.mult, ALU.add))
                link(stt(wk[:, 1, :], wk[:, 2, :], -C3, wk[:, 1, :], ALU.mult, ALU.add))
                link(ts(wk[:, 1, :], wk[:, 1, :], math.pi / 2 * quarter, -3.1415925, ALU.add, ALU.max))
                ts(wk[:, o, :], wk[:, 1, :], 3.1415925, None, ALU.min).then_inc(s("ang_ready"), 1)
                dve.wait_ge(s("ang_ready"), i + 1)
            pl.got("tab_ready", 4)
            ffn(0, 0, "gu00", "dn00")

            mod_in(0, 1)
            take("hyb", plain(0))
            take("hybv", tokens([fv[:, :, 0:256], fv[:, :, 256:512], dv[:, :, 0:256], dv[:, :, 256:512]]))
            turn(list(range(DQ, DQ + 8)) + [IQ, IQ + 1, IK], tabs[:, 0, :])
            r8 = slice(0, 8)
            log_sigmoid(big[0:8, GT, :], r8, sp_("foxb")[0:8, :])
            link(dve.tensor_tensor_scan(gate_row(r8, 1), ones_row(r8), gate_row(r8, 0), 0.0,
                                        ALU.mult, ALU.add))
            link(ts(gate_row(r8, 3), gate_row(r8, 1), 8.0, None, ALU.mult))
            ts(gate_row(r8, 0), gate_row(r8, 1), -8.0, None, ALU.mult).then_inc(s("cum_ready"), 1)
            pl.got("iw_raw")
            link(ts(tokw[:, :], XB[3][:, 0:16], 0.5, None, ALU.mult))

            def causal(qb, W):
                return cc("causal", T - W, W)

            def chunked(qb, W):
                return cc("chunk", T - W, W)

            attention(FOX_H, 0.125, 64, causal, 0)

            for qb in range(1, NB):
                W = (qb + 1) * P
                sc, work, eq = wk[:, 0, 0:W], wk[:, 1, 0:W], wk[:, 2, 0:W]
                for i in range(IDX_H):
                    n = (qb - 1) * IDX_H + i
                    dve.wait_ge(s("idx_relu"), n + 1)
                    iwc = tokw[:, 4 * qb + i:4 * qb + i + 1]
                    if i == 0:
                        ins = ts(sc, S[:, n % 2, 0:W], iwc, None, ALU.mult)
                    else:
                        ins = stt(sc, S[:, n % 2, 0:W], iwc, sc, ALU.mult, ALU.add)
                    ins.then_inc(s("idx_used"), 1)
                    dve.wait_ge(s("idx_used"), n + 1)
                link(tt(sc, sc, chunked(qb, W), ALU.add))
                for i in range(TOPK // 8):
                    src = work if i else sc
                    link(dve.max(st[:, 0:8], src))
                    if i < TOPK // 8 - 1:
                        link(dve.match_replace(work, st[:, 0:8], src, LOWEST))
                thr = st[:, 7:8]
                link(ts(work, sc, thr, 0.0, ALU.is_gt, ALU.add, accum_out=st[:, 8:9]))
                link(ts(st[:, 9:10], st[:, 8:9], -1.0, float(TOPK), ALU.mult, ALU.add))
                link(ts(eq, sc, thr, None, ALU.is_equal))
                link(dve.tensor_tensor_scan(sc, ones_row(slice(0, P), W), eq, 0.0, ALU.mult, ALU.add))
                link(stt(sc, sc, st[:, 9:10], eq, ALU.is_le, ALU.mult))
                link(tt(sc, sc, work, ALU.add))
                link(ts(big[:, DMASK + qb, 0:W], sc, -NEG, NEG, ALU.mult, ALU.add))

            def selected(qb, W):
                return big[:, DMASK + qb, 0:W] if qb else chunked(0, P)

            attention(DSA_H, 0.125, 64, selected, 4)
            residual(0, 1, "hybo")
            ffn(0, 2, "gu01", "dn01")

            ffn(1, 0, "gu10", "dn10")
            mod_in(1, 1)
            take("mlad", plain(0))
            for c0, n, name in ((CQ, 3, "q_norm"), (CKV, 2, "kv_norm")):
                root()
                for c in range(n):
                    ins = stt(big[:, c0 + c, :], big[:, c0 + c, :], sp_(name, c), rstd[:, :], ALU.mult, ALU.mult)
                ins.then_inc(s("latent_ready"), 1)
                pl.got("latent_ready")
            take("mlaq", plain(QN))
            take("mlak", plain(KN))
            take("mlav", tokens(mv))
            turn([KR] + list(range(QR, QR + 4)), tabs[:, 2, :])
            attention(MLA_H, 192.0 ** -0.5, P, chunked, 0)
            residual(1, 1, "mlao")
            ffn(1, 2, "gu11", "dn11")

            dve.wait_ge(s("const2_in"), 16)
            scale_in(h, sp_("final_g", 0, DC))
            dve.wait_ge(s("u_scaled"), pl.tu)
            lb = sp_("lb", 0, 4)
            link(tt(st[:, 16:18], lb[:, 0:2], lb[:, 2:4], ALU.max))
            for l in range(DEPTH):
                ins = tt(st[:, 18 + 2 * l:20 + 2 * l], lb[:, 2 * l:2 * l + 2], st[:, 16:18], ALU.subtract)
            ins.then_inc(s("lb_shifted"), 1)
            pl.got("lb_exp")
            link(tt(st[:, 26:28], st[:, 22:24], st[:, 24:26], ALU.add))
            link(dve.reciprocal(st[:, 28:30], st[:, 26:28]))
            for l in range(DEPTH):
                link(tt(st[:, 30 + 2 * l:32 + 2 * l], st[:, 22 + 2 * l:24 + 2 * l], st[:, 28:30], ALU.mult))
            link(tt(st[:, 34:36], st[:, 30:32], st[:, 30:32], ALU.subtract))
            link(tt(st[:, 36:38], st[:, 30:32], st[:, 32:34], ALU.add))
            link(tt(st[:, 36:38], st[:, 36:38], st[:, 30:32], ALU.subtract))
            link(ts(st[:, 38:42], st[:, 34:38], -1.0, 1.0, ALU.mult, ALU.add))
            for l in range(DEPTH):
                for i in range(2):
                    a = l * 256 + 128 * i
                    link(dve.tensor_tensor_reduce(
                        out=wk[:, 0, 0:64], in0=cc("lam", a, 64), in1=cc("lam", a + 64, 64), scale=1.0,
                        scalar=0.0, op0=ALU.mult, op1=ALU.add, accum_out=st[:, 42 + 2 * l + i:43 + 2 * l + i]))
            dve.nop().then_inc(s("lam_dots"), 1)
            pl.got("lam_exp")
            for l in range(DEPTH):
                init = 0.8 - 0.6 * math.exp(-0.3 * l)
                link(tt(st[:, 50 + l:51 + l], st[:, 47 + 2 * l:48 + 2 * l], st[:, 46 + 2 * l:47 + 2 * l], ALU.subtract))
                link(ts(st[:, 50 + l:51 + l], st[:, 50 + l:51 + l], -init, None, ALU.add))

            for l in range(DEPTH):
                init = 0.8 - 0.6 * math.exp(-0.3 * l)
                scale_in(u, sp_("norm1", l * DC, DC))
                take(f"in{l}", plain(0))
                take(f"inv{l}", tokens([xv[:, :, :], av[:, :, 0:256], av[:, :, 256:512], hv[:, :, :]]))
                for i in range(8):
                    root()
                    stt(big[:, AQ + i, :], big[:, AQ + i, :], sp_("qn" if i < 4 else "kn", l), rstd[:, :],
                        ALU.mult, ALU.mult).then_inc(s("qk_normed"), 1)
                    pl.got("qk_normed")
                turn(range(AQ, AQ + 8), cc("diff_sin"))
                attention(DIFF_H, 0.125, P, causal, 2, maps=2, lam=st[:, 50 + l:51 + l])
                link(ts(st[:, 52:53], sp_("subln", l), 1.0 - init, None, ALU.mult))
                for c in range(DIFF_H):
                    root()
                    link(stt(u[:, 2 + c, :], u[:, 2 + c, :], st[:, 52:53], rstd[:, :], ALU.mult, ALU.mult))

                for c in range(4):
                    if c >= 2:
                        pl.got("conv_silu")
                    y, xx = wk[:, c % 2, :], big[:, XQ + c, :]
                    tap = [sp_("conv", (l * 4 + c) * 4 + i) for i in range(4)]
                    link(ts(y, xx, tap[3], None, ALU.mult))
                    for d in (1, 2, 3):
                        ins = stt(y[:, d:T], xx[:, 0:T - d], tap[3 - d], y[:, d:T], ALU.mult, ALU.add)
                        if d < 3:
                            link(ins)
                    ins.then_inc(s("conv_raw"), 1)
                pl.got("conv_silu", 2)
                r4 = slice(0, 4)
                log_sigmoid(big[0:4, GF, :], r4, sp_("gateb", 2 * l + 1)[0:4, :])
                link(ts(gate_row(r4, 1), big[0:4, GI, :], sp_("gateb", 2 * l)[0:4, :], None, ALU.add))
                link(dve.tensor_tensor_scan(gate_row(r4, 4), ones_row(r4), gate_row(r4, 0), 0.0,
                                            ALU.mult, ALU.add))
                link(tt(gate_row(r4, 3), gate_row(r4, 1), gate_row(r4, 4), ALU.subtract))
                link(dve.tensor_tensor_scan(gate_row(r4, 2), gate_row(r4, 3), gate_row(r4, 3), 0.0,
                                            ALU.max, ALU.max))
                link(tt(gate_row(r4, 6), gate_row(r4, 2), gate_row(r4, 4), ALU.add))
                dve.nop().then_inc(s("em_log"), 1)
                link(ts(gate_row(r4, 5), gate_row(r4, 2), -1.0, None, ALU.mult))
                dve.nop().then_inc(s("gates_rows"), 1)
                pl.got("a_cols")
                link(dve.tensor_copy(tokw[:, :], XB[3][:, 0:16]))
                u0 = l * 4 * NB
                for n in range(4 * NB + 1):
                    if n < 4 * NB:
                        hh, b = divmod(n, NB)
                        if b == 0:
                            pl.got("g_ready")
                            dve.tensor_copy(wk[:, hh % 2, :], XB[0][:, :]).then_inc(s("g_taken"), 1)
                            dve.wait_ge(s("g_taken"), l * 4 + hh + 1)
                        tt(wk[:, 2 + n % 2, 0:P], wk[:, hh % 2, blk(b)], cc("tri"), ALU.add)\
                            .then_inc(s("g_diag"), 1)
                    if n:
                        i = n - 1
                        hh, b = divmod(i, NB)
                        W = T - b * P
                        dve.wait_ge(s("me_done"), u0 + i + 1)
                        dve.wait_ge(s("mqk_done"), u0 + i + 1)
                        if u0 + i >= 2:
                            dve.wait_ge(s("m_out"), u0 + i - 1)
                        stt(S[:, i % 2, 0:W], XB[1 + i % 2][:, 0:W], 0.125, E[:, i % 4, 0:W], ALU.mult, ALU.mult)\
                            .then_inc(s("ms_ready"), 1)
                dve.wait_ge(s("m_out"), u0 + 4 * NB)
                for cp in range(2):
                    pl.got("em_ready")
                    dve.tensor_copy(wk[:, 2, :], XB[3][:, :]).then_inc(s("em_taken"), 1)
                    dve.wait_ge(s("em_taken"), 2 * l + cp + 1)
                    link(stt(wk[:, 3, :], LP[1][:, cp, :], -1.0, wk[:, 2, :], ALU.mult, ALU.max))
                    link(tt(wk[:, 3, :], wk[:, 3, :], LP[1][:, cp, :], ALU.max))
                    link(dve.reciprocal(wk[:, 3, :], wk[:, 3, :]))
                    tt(u[:, cp, :], wk[:, 3, :], LP[0][:, cp, :], ALU.mult).then_inc(s("m_mix"), 1)
                    root()
                    link(stt(u[:, cp, :], u[:, cp, :], sp_("mnorm", l), rstd[:, :], ALU.mult, ALU.mult))
                    pl.got("o_sigmoid")
                    link(tt(u[:, cp, :], u[:, cp, :], big[:, XO + cp, :], ALU.mult))

                for cp in range(2):
                    c = 2 * l + cp
                    lbc, olb = st[:, 34 + c:35 + c], st[:, 38 + c:39 + c]
                    pl.got("h_sig")
                    ts(big[:, HF + cp, :], big[:, HF + cp, :], olb, lbc, ALU.mult, ALU.add)\
                        .then_inc(s("h_f"), 1)
                    link(ts(big[:, SP + cp, :], wk[:, 4, :], olb, None, ALU.mult))
                    pl.got("h_lnf")
                    link(dve.tensor_tensor_scan(big[:, XQ + cp, :], ones_row(slice(0, P)), big[:, HF + cp, :], 0.0,
                                                ALU.mult, ALU.add))
                    dve.nop().then_inc(s("h_kb"), 1)
                    B = big[:, XQ + cp, :]

                    def exponents(step):
                        b = 1 << (step - 1)
                        Bv, X = (t.rearrange("p (j i b) -> p j i b", i=2, b=b) for t in (B, wk[:, step % 2, :]))
                        ref = Bv[:, :, 0, b - 1:b].to_broadcast([P, T // (2 * b), b])
                        if step >= 3:
                            dve.wait_ge(s("ex_ready"), (2 * l + cp) * 9 + step - 2)
                        tt(X[:, :, 0, :], ref, Bv[:, :, 0, :], ALU.subtract)
                        tt(X[:, :, 1, :], Bv[:, :, 1, :], ref, ALU.subtract).then_inc(s("x_ready"), 1)

                    exponents(1)
                    for step in range(10):
                        if 1 <= step < 9:
                            exponents(step + 1)
                        for j in range(2):
                            k = (l * 2 + cp) * 20 + 2 * step + j
                            bank = XB[k % 4]
                            dve.wait_ge(s("level_mm"), k + 1)
                            ad = wk[:, 2 + j, :].rearrange("p (b t) -> p b t", b=NB)
                            bk = bank[:, :].rearrange("p (b t) -> p b t", b=NB)
                            m = cc("levels", step * P, P).unsqueeze(1).to_broadcast([P, NB, P]) if step < 8 else None
                            if step == 0:
                                ins = tt(ad, m, bk, ALU.mult)
                            elif step < 8:
                                ins = dve.copy_predicated(ad, m.bitcast(U32), bk)
                            elif step == 8:
                                dve.tensor_copy(tmp[:, j, 0:P], bank[:, 0:P])
                                ins = dve.tensor_copy(tmp[:, j, 640:768], bank[:, P:2 * P])
                            else:
                                ins = dve.tensor_copy(tmp[:, j, P:640], bank[:, :])
                            ins.then_inc(s("level_taken"), 1)
                            dve.wait_ge(s("level_taken"), k + 1)
                    dve.nop().then_inc(s("a_done"), 1)
                    pl.got("h_out")
                    dve.tensor_copy(u[:, 6 + cp, :], LP[0][:, cp, :]).then_inc(s("h_mix"), 1)
                    root()
                    link(stt(u[:, 6 + cp, :], u[:, 6 + cp, :], sp_("hnorm", l), rstd[:, :], ALU.mult, ALU.mult))
                    link(tt(u[:, 6 + cp, :], u[:, 6 + cp, :], big[:, HG + cp, :], ALU.mult))
                dve.nop().then_inc(s("mix_ready"), 1)

                def add2(k, it, p):
                    tt(h[:, 2 * k:2 * k + 2, :], h[:, 2 * k:2 * k + 2, :], LP[p][:, :, :], ALU.add)\
                        .then_inc(s(f"lin_taken{p}"), 1)

                take(f"wo{l}", add2)
                scale_in(u, sp_("norm2", l * DC, DC))

                def square(k, it, p):
                    dve.wait_ge(s("silu_done"), at(pl.silu + k + 1, it, RING))
                    t = tmp[:, p, :].rearrange("p (a b) -> p a b", a=2)
                    tt(big[:, dyn(big, k, it, 2, 2), :], t, t, ALU.mult).then_inc(s(f"lin_taken{p}"), 1)

                take(f"up{l}", square)
                pl.silu += 16

                def add1(k, it, p):
                    a = k
                    o = h[:, a:a + 1, :] if isinstance(it, int) else h[:, bass.ds(it * 2 + a, 1), :]
                    tt(o, o, LP[p][:, 0:1, :], ALU.add).then_inc(s(f"lin_taken{p}"), 1)

                take(f"down{l}", add1, parts=2)


GROUPS = 4 * (FC + DC) + 18 + 3 + 6 + 4 + 4 + 4 + DEPTH * (11 + 4 + 4 + 16 + 8)



def _const_table(lam):
    c = np.zeros((P, NCONST), np.float32)
    c2 = np.zeros((P, NCONST2), np.float32)

    def put(name, a):
        t, (o, wd) = (c, COFF[name]) if name in COFF else (c2, COFF2[name])
        t[:a.shape[0], o:o + a.shape[1]] = a

    put("lam", np.broadcast_to(lam.reshape(1, -1), (P, DEPTH * 256)))

    i = np.arange(P)
    t = np.arange(T)
    put("ident", np.eye(P))
    put("ones", np.ones((P, P)))
    put("blk64", (i[:, None] // 64 == i[None, :] // 64) * 1.0)
    for name, half in (("rot16", 8), ("rot64", 32)):
        r = np.zeros((P, P))
        for b in (0, 64):
            for k in range(half):
                r[b + half + k, b + k] = -1.0
                r[b + k, b + half + k] = 1.0
        put(name, r)
    m = np.zeros((P, T))
    m[:, T - P:] = np.where(i[None, :] <= i[:, None], 0.0, NEG)
    put("causal", m)
    m = np.zeros((P, T))
    m[:, T - P:] = np.where(i[None, :] // 64 <= i[:, None] // 64, 0.0, NEG)
    put("chunk", m)
    put("tri", np.where(i[:, None] <= i[None, :], 0.0, NEG))
    lv = [np.eye(P)]
    for k in range(7):
        b = 1 << k
        same = i[:, None] // (2 * b) == i[None, :] // (2 * b)
        lv.append((same & (i[:, None] // b % 2 == 0) & (i[None, :] // b % 2 == 1)) * 1.0)
    put("levels", np.concatenate(lv, 1))
    for name, rot, theta in (("invf16", 16, 500000.0), ("invf64", 64, 10000.0)):
        half = rot // 2
        f = np.exp(np.float32(-math.log(theta) * 2.0) * np.arange(half, dtype=np.float32) / np.float32(rot))
        col = np.zeros((64, 1), np.float32)
        col[:half, 0] = f
        col[half:rot, 0] = f
        put(name, np.concatenate([col, col]))
    put("eps", np.full((P, 1), RMS_EPS))
    half = 8
    inv = np.float32(500000.0) ** (-np.arange(half, dtype=np.float32) / half)
    ang = t.astype(np.float32)[None, :] * inv[:, None].astype(np.float32)
    cos, sin = np.ones((64, T)), np.zeros((64, T))
    for k in (0, half):
        cos[k:k + half] = np.cos(ang.astype(np.float64))
        sin[k:k + half] = np.sin(ang.astype(np.float64))
    put("diff_cos", np.concatenate([cos, cos]))
    put("diff_sin", np.concatenate([sin, sin]))
    sel = np.zeros((4, 2 * P))
    for cp in range(2):
        for half in range(2):
            sel[2 * cp + half, cp * P + 64 * half:cp * P + 64 * half + 64] = 1.0
    put("sel4", sel)
    return c, c2


def _columns(v):
    return np.asarray(v).reshape(-1, P).T


def _fm(wt):
    K, F = wt.shape
    return np.ascontiguousarray(wt.reshape(K // P, P, F // 256, 256).transpose(2, 1, 0, 3)).reshape(F // 256, P, -1)


def _halves(wt):
    K = wt.shape[0]
    return np.ascontiguousarray(
        wt.reshape(2, K // (2 * P), P, DC, P).transpose(3, 0, 2, 1, 4)).reshape(2 * DC, P, -1)


def kernel(**inp):
    import concourse.bacc as _bacc
    from concourse.bass_utils import run_bass_kernel_spmd as _run

    a = {k: np.asarray(v) for k, v in inp.items()}
    small = np.zeros((P, NSMALL), np.float32)

    def put(name, v, at=0, rows=P):
        o = SOFF[name][0] + at
        small[:rows, o:o + v.shape[1]] = v

    put("norm_g", _columns(a["norm_g"]))
    put("final_g", _columns(a["final_g"]))
    put("norm1", _columns(a["norm1_g_2"]))
    put("norm2", _columns(a["norm2_g_2"]))
    put("q_norm", _columns(a["mla_q_norm"]))
    put("kv_norm", _columns(a["mla_kv_norm"]))
    put("conv", a["mlstm_conv_w_2"].reshape(DEPTH, 4, 4, P).transpose(3, 0, 2, 1).reshape(P, -1))
    for l in range(DEPTH):
        for name, key in (("mnorm", "mlstm_norm_g_2"), ("qn", "diff_q_norm_g_2"), ("kn", "diff_k_norm_g_2"),
                          ("hnorm", "hgrn_norm_g_2")):
            put(name, np.tile(a[key][l], 2)[:, None], l)
        put("subln", a["diff_subln_g_2"][l][:, None], l)
        for i in range(2):
            put("gateb", a["mlstm_gate_b_2"][l, i][:, None], 2 * l + i, rows=4)
    put("lb", _columns(a["hgrn_lb_param_2"]))
    put("cond", _columns(a["c"]))
    put("foxb", a["fox_b_f"][0][:, None], rows=8)
    W = {"ada": np.concatenate([_fm(a["ada_w"][l]) for l in range(DEPTH)])}
    for l in range(DEPTH):
        for j in range(2):
            g, up, dn = (a[k][l, j] for k in ("ffn_w_gate", "ffn_w_up", "ffn_w_down"))
            gu = np.stack([g.reshape(D, FC, P), up.reshape(D, FC, P)], 2).reshape(D, 2 * FF)
            W[f"gu{l}{j}"] = _fm(gu)
            W[f"dn{l}{j}"] = _halves(dn)
    hw = a["hyb_w_in"][0]
    off = np.cumsum([0, 512, 512, 512, 8, 512, 512, 512, 256, 4, 64])
    fq, fk, fvw, ff, dq, dk, dvw, iq, iwt, ik = (hw[:, off[i]:off[i + 1]] for i in range(10))
    z = lambda n: np.zeros((D, n), np.float32)
    W["hyb"] = _fm(np.concatenate([fq, fk, dq, dk, iq, ik, ik, ff, z(24), iwt, z(92)], 1))
    W["hybv"] = _fm(np.concatenate([fvw, dvw], 1))
    W["hybo"] = _fm(a["hyb_w_out"][0])
    md = a["mla_w_down"][0]
    W["mlad"] = _fm(np.concatenate([md, md[:, 640:704]], 1))
    uq = a["mla_w_uq"][0].reshape(384, MLA_H, 192)
    W["mlaq"] = _fm(np.concatenate([uq[:, :, :128].reshape(384, -1), uq[:, :, 128:].reshape(384, -1)], 1))
    ukv = a["mla_w_ukv"][0].reshape(256, MLA_H, 256)
    W["mlak"] = _fm(np.ascontiguousarray(ukv[:, :, :128]).reshape(256, -1))
    W["mlav"] = _fm(np.ascontiguousarray(ukv[:, :, 128:]).reshape(256, -1))
    W["mlao"] = _fm(a["mla_w_out"][0])
    for l in range(DEPTH):
        wi = a["w_in_2"][l]
        off = np.cumsum([0, 256, 256, 256, 256, 4, 4, 512, 512, 512, 256, 256, 256, 256])
        mq, mk, mvw, mo, mi, mf, aq, ak, avw, hq, hf, hi, hg = (wi[:, off[i]:off[i + 1]] for i in range(13))
        W[f"in{l}"] = _fm(np.concatenate([mq, mk, mo, aq, ak, hq, hf, hg, mi, z(124), mf, z(124)], 1))
        W[f"inv{l}"] = _fm(np.concatenate([mvw, avw, hi], 1))
        W[f"wo{l}"] = _fm(a["w_out_2"][l])
        W[f"up{l}"] = _fm(a["w_up_2"][l])
        W[f"down{l}"] = _halves(a["w_down_2"][l])

    consts, consts2 = _const_table(a["diff_lambda_2"])
    arrays = {
        "x": np.ascontiguousarray(a["x"][0].T.reshape(DC, P, T).transpose(1, 0, 2)),
        "small": small,
        "consts": consts,
        "consts2": consts2,
        "pos": np.ascontiguousarray(np.broadcast_to(a["positions"].astype(np.int32), (P, T))),
        "adab": np.ascontiguousarray(_columns(a["ada_b"])),
    }
    nc = _bacc.Bacc("TRN2", target_bir_lowering=False, num_devices=1)

    def dram(name, arr):
        return nc.dram_tensor(name, arr.shape, mybir.dt.from_np(arr.dtype), kind="ExternalInput").ap()

    aps = {k: dram(k, v) for k, v in arrays.items()}
    w = {k: dram("w_" + k, v) for k, v in W.items()}
    arrays.update({"w_" + k: v for k, v in W.items()})
    out = nc.dram_tensor("out", (P, DC, T), F32, kind="ExternalOutput").ap()
    build(nc, aps["x"], aps["small"], aps["consts"], aps["consts2"], aps["pos"], aps["adab"], w, out)
    r = _run(nc, [arrays], core_ids=[0])
    got = r.results[0]["out"]
    return np.ascontiguousarray(got.transpose(1, 0, 2).reshape(D, T).T)[None]
```

```python
import math
from contextlib import ExitStack

import numpy as np

import concourse.bass as bass
from concourse import mybir

F32 = mybir.dt.float32
F32R = mybir.dt.float32r
I32 = mybir.dt.int32
U32 = mybir.dt.uint32
ALU = mybir.AluOpType
ACT = mybir.ActivationFunctionType
AX = mybir.AxisListType

P = 128
T = 512
NB = T // P
D = 1024
DC = D // P
FF = 2816
FC = FF // P
FF2 = 4 * D
FC2 = FF2 // P
DEPTH = 2
N_MOD = 9
TOPK = 128
NEG = -1e30
LOWEST = -3e38
RMS_EPS = 1e-6

FOX_H = 8
DSA_H = 8
IDX_H = 4
MLA_H = 8
DIFF_H = 4
RING = 4
SLAB = 16 * P
UP0 = 10
N_ADA = DEPTH * N_MOD * D // 256

CONSTS = [("ident", P), ("ones", P), ("blk64", P), ("rot16", P), ("rot64", P),
          ("causal", T), ("chunk", T), ("sel4", 2 * P), ("invf16", 1), ("invf64", 1), ("eps", 1)]
CONSTS2 = [("tri", P), ("levels", 8 * P), ("diff_cos", T), ("diff_sin", T), ("lam", DEPTH * 4 * 64)]


def _offsets(table):
    off, n = {}, 0
    for name, width in table:
        off[name] = (n, width)
        n += width
    return off, n


COFF, NCONST = _offsets(CONSTS)
COFF2, NCONST2 = _offsets(CONSTS2)

SMALL = [("norm_g", DEPTH * 3 * DC), ("final_g", DC), ("norm1", DEPTH * DC), ("norm2", DEPTH * DC),
         ("q_norm", 3), ("kv_norm", 2), ("conv", DEPTH * 4 * 4), ("mnorm", DEPTH),
         ("qn", DEPTH), ("kn", DEPTH), ("subln", DEPTH), ("lb", DEPTH * 2), ("hnorm", DEPTH),
         ("cond", DC), ("foxb", 1), ("gateb", DEPTH * 2)]
SOFF, NSMALL = _offsets(SMALL)


def slab_loop(eng, n, body, chains=(), unroll=RING, peel=2):
    peel = min(peel, n)
    for r in range(peel):
        body(r, 0)
    turns = (n - peel) // unroll
    done = peel
    if turns >= 2:
        for ch, per in chains:
            ch.enter(per * unroll)
        with eng.Fori(0, turns) as it:
            for ch, _ in chains:
                ch.it = it
            for u in range(unroll):
                body(peel + u, it)
        for ch, _ in chains:
            ch.leave(turns)
        done += turns * unroll
    for r in range(done, n):
        body(r, 0)


class Chain:

    def __init__(self, eng, sem):
        self.eng, self.sem, self.n = eng, sem, 0
        self.it, self.per, self.base = None, 0, 0

    def enter(self, per):
        self.base, self.per = self.n, per

    def leave(self, turns):
        assert self.n - self.base == self.per, (self.n - self.base, self.per)
        self.n = self.base + self.per * turns
        self.it = None

    def __call__(self, ins):
        self.n += 1
        ins.then_inc(self.sem, 1)
        self.eng.wait_ge(self.sem, self.n if self.it is None else self.it * self.per + self.n)


class Place:

    def __init__(self, eng, sems):
        self.eng, self.sems = eng, sems
        self.slab = self.group = self.ada = 0
        self.cut = self.cut_end = 0
        self.norm = self.sq = self.silu = self.tu = self.ur = 0
        self.rope = self.unit = self.prob = self.head = 0
        self.seen = {}

    def got(self, name, n=1):
        self.seen[name] = self.seen.get(name, 0) + n
        self.eng.wait_ge(self.sems(name), self.seen[name])

    def passed(self, name, n=1):
        self.seen[name] = self.seen.get(name, 0) + n

    def groups_taken(self):
        if self.group:
            self.eng.wait_ge(self.sems("lin_taken0"), (self.group + 1) // 2)
        if self.group > 1:
            self.eng.wait_ge(self.sems("lin_taken1"), self.group // 2)


    def chunk_final(self, c, per):
        g = self.group - DC // per + c // per
        if self.group:
            self.eng.wait_ge(self.sems(f"lin_taken{g % 2}"), g // 2 + 1)


def at(value, it, per):
    return value if isinstance(it, int) else it * per + value


FQ, FK, DQ, DK, IQ, IK, GT, FV, DV, DMASK = 0, 4, 8, 12, 16, 18, 19, 20, 24, 28
CQ, CKV, KR, QN, QR, KN, MV = 0, 3, 5, 6, 14, 18, 26
XQ, XK, XO, AQ, AK, HQ, HF, HG, GI, GF, XV, AV, HV, SP = 0, 2, 4, 6, 10, 14, 16, 18, 20, 21, 22, 24, 28, 30


def build(nc, x, small, consts, consts2, pos, adab, w, out):
    with ExitStack() as ctx:
        sems = {}

        def s(name):
            if name not in sems:
                sems[name] = ctx.enter_context(nc.semaphore(name))
            return sems[name]

        place = {}

        def sb(name, shape, dt=F32):
            place[name] = -(-place.get("end", nc.sbuf_base) // 32) * 32
            place["end"] = place[name] + 4 * int(np.prod(shape[1:]))
            assert place["end"] <= nc.sbuf_usable_end, (name, place["end"], nc.sbuf_usable_end)
            return nc.alloc_sbuf_tensor_at(name, shape, dt, offset=place[name])

        def over(name, shape, base, chunk=0):
            return nc.alloc_sbuf_tensor_at(name, shape, F32R, offset=place[base] + 4 * T * chunk)

        h = sb("h", [P, DC, T])
        u = sb("u", [P, DC, T])
        big = sb("big", [P, 32, T])
        wk = sb("wk", [P, 6, T])
        tabs = sb("tabs", [P, 4, T])
        ring = sb("ring", [P, RING, SLAB])
        S = sb("S", [P, 2, T])
        E = sb("E", [P, 4, T])
        ET = sb("ET", [P, 2, T])
        ada_in = sb("ada_in", [P, 2, DC * 256])
        ada_acc = sb("ada_acc", [P, 256])
        cst = sb("cst", [P, NCONST])
        sm = sb("sm", [P, NSMALL])
        mod = sb("mod", [P, N_ADA * 2])
        modb = sb("modb", [P, N_ADA * 2])
        gain = sb("gain", [P, DC])
        gate = sb("gate", [P, DC])
        tmp = sb("tmp", [P, 2, 2 * T])
        rt = sb("rt", [P, T])
        rstd = sb("rstd", [P, T])
        sq = sb("sq", [P, 2, T])
        st = sb("st", [P, 64])
        stat = sb("stat", [P, 4, 4])
        csil = sb("csil", [P, DC])
        tokw = sb("tokw", [P, 4 * NB])
        u_lo = over("u_lo", [P, DC, T], "u")
        u_hi1 = over("u_hi1", [P, DC, T], "big", 28)
        u_hi2 = over("u_hi2", [P, DC, T], "wk")
        w_lo = over("w_lo", [P, RING, SLAB], "ring")
        w_hi = over("w_hi", [P, 2, SLAB], "S")
        posi = big[:, 24, :].bitcast(I32)
        sqa = wk[:, 3, :]
        tmpf = tmp[:, :, :].rearrange("p a b -> p (a b)")

        cst2 = ada_in[:, :, :].rearrange("p a b -> p (a b)")

        LP = [ctx.enter_context(nc.psum_tensor(f"LP{i}", [P, 2, T], F32)) for i in range(2)]
        XB = [ctx.enter_context(nc.psum_tensor(f"XB{i}", [P, T], F32)) for i in range(4)]
        LPF = [t[:, :, :].rearrange("p a b -> p (a b)") for t in LP]

        rts, rstds = [rt[:, :], wk[:, 4, :]], [rstd[:, :], wk[:, 5, :]]

        def cc(name, a=0, n=None):
            t, (o, wd) = (cst, COFF[name]) if name in COFF else (cst2, COFF2[name])
            return t[:, o + a:o + (wd if n is None else a + n)]

        def gate_row(rows, i):
            return tmpf[rows, i * T:(i + 1) * T] if i < 4 else tabs[rows, i - 4, :]

        def ones_row(rows, n=T):
            return cc("ones", 0, 1)[rows, :].to_broadcast([rows.stop - rows.start, n])

        def sp_(name, a=0, n=1):
            return sm[:, SOFF[name][0] + a:SOFF[name][0] + a + n]

        def blk(b):
            return slice(b * P, (b + 1) * P)

        def half(i):
            return slice(64 * (i % 2), 64 * (i % 2) + 64)

        def vals(c0, width):
            n = NB * width // T
            return big[:, c0:c0 + n, :].rearrange("p a b -> p (a b)").rearrange("p (t c) -> p t c", c=width)

        fv, dv = vals(FV, T), vals(DV, T)
        mv = [vals(MV + 2 * i, 256) for i in range(3)] + [tmpf[:, 0:1024].rearrange("p (t c) -> p t c", c=256)]
        xv, av, hv = vals(XV, 256), vals(AV, T), vals(HV, 256)

        ORDER = [("gu00", FC, DC * 256, 1), ("dn00", 2 * DC, FC // 2 * P, 0), ("hyb", 10, DC * 256, 0),
                 ("hybv", 4, DC * 256, 0), ("hybo", 4, DC * 256, 0), ("gu01", FC, DC * 256, 1),
                 ("dn01", 2 * DC, FC // 2 * P, 0), ("gu10", FC, DC * 256, 1), ("dn10", 2 * DC, FC // 2 * P, 0),
                 ("mlad", 3, DC * 256, 0), ("mlaq", 6, 3 * 256, 0), ("mlak", 4, 2 * 256, 0),
                 ("mlav", 4, 2 * 256, 0), ("mlao", 4, DC * 256, 0), ("gu11", FC, DC * 256, 0),
                 ("dn11", 2 * DC, FC // 2 * P, 0)]
        for l in range(DEPTH):
            ORDER += [(f"in{l}", 11, DC * 256, 0), (f"inv{l}", 4, DC * 256, 0), (f"wo{l}", 4, DC * 256, 0),
                      (f"up{l}", 16, DC * 256, 0), (f"down{l}", 16, 16 * P, 0)]
        RUNS = {"gu00": ["gu00"], "hyb": ["hyb", "hybv"], "gu01": ["gu01"], "gu10": ["gu10"], "mlad": ["mlad"],
                "gu11": ["gu11"]}
        for l in range(DEPTH):
            RUNS.update({f"in{l}": [f"in{l}", f"inv{l}"], f"up{l}": [f"up{l}"]})
        CUT = {name for run in RUNS.values() for name in run}
        WIDTH = {name: (n, width, ada) for name, n, width, ada in ORDER}

        def beside(pl, name):
            n, _, ada = WIDTH[name]
            return min(n, N_ADA - (UP0 + 1) - pl.ada) if ada else 0

        block = ctx.enter_context(nc.Block())

        @block.sync
        def _(sp):
            pl = Place(sp, s)
            for dst, src in ((sm[:, :], small), (cst[:, :], consts), (h[:, :, :], x),
                             (posi, pos), (modb[:, :], adab)):
                sp.dma_start(dst, src).then_inc(s("const_in"), 16)

            def load_ada(a, it):
                if a >= 2:
                    sp.wait_ge(s("ada_summed"), at(a - 1, it, RING))
                src = w["ada"][a] if isinstance(it, int) else w["ada"][it * RING + a]
                sp.dma_start(ada_in[:, a % 2, :], src).then_inc(s(f"ada_in{a % 2}"), 16)

            for a in range(UP0 + 1):
                load_ada(a, 0)
            consts2_at = "gu11"
            for name, n, width, _ in ORDER:
                n_ada = beside(pl, name)
                if name == consts2_at:
                    sp.wait_ge(s("ada_summed"), N_ADA)
                    sp.dma_start(cst2[:, 0:NCONST2], consts2).then_inc(s("const2_in"), 16)

                def load(k, it):
                    slab = pl.slab + k
                    if slab >= RING:
                        sp.wait_ge(s("lin_done"), at(slab - RING + 1, it, RING))
                    src = w[name][k] if isinstance(it, int) else w[name][it * RING + k]
                    sp.dma_start(ring[:, slab % RING, 0:width], src).then_inc(s(f"w_in{slab % RING}"), 16)
                    if n_ada == n or k < n_ada:
                        load_ada(UP0 + 1 + pl.ada + k, it)

                slab_loop(sp, n, load, peel=4 if pl.slab == 0 else n_ada if 0 < n_ada < n else 2)
                pl.slab += n
                pl.ada += n_ada
            sp.wait_ge(s("lin_taken0"), GROUPS // 2 + GROUPS % 2)
            sp.wait_ge(s("lin_taken1"), GROUPS // 2)
            sp.dma_start(out, h[:, :, :]).then_inc(s("out_stored"), 16)
            sp.wait_ge(s("out_stored"), 16)

        @block.tensor
        def _(pe):
            pl = Place(pe, s)

            def mm(o, lhsT, rhs, start=True, stop=True):
                return pe.matmul(o, lhsT=lhsT, rhs=rhs, start=start, stop=stop)

            def ada_sum(a, it):
                pe.wait_ge(s("ada_summed"), at(a + 1, it, RING))
                for f in range(2):
                    last = mm(XB[3][:, f:f + 1], ada_acc[:, f * P:(f + 1) * P], cc("ones", 0, 1))
                last.then_inc(s("ada_col"), 1)

            def linear(name, kind, src, parts=1):
                n, width, _ = WIDTH[name]
                n_ada = beside(pl, name)
                cut = name in CUT

                def products(o, n_c, weights, inputs, tokens_out):
                    for c in range(n_c):
                        if cut:
                            (wh, wl), (xh, xl) = weights(c), inputs(c)
                            passes = ((wh, xh), (wh, xl), (wl, xh))
                        else:
                            passes = ((weights(c), inputs(c)),)
                        for i, (a, b) in enumerate(passes):
                            if tokens_out:
                                a, b = b, a
                            last = mm(o, a, b, start=c == 0 and i == 0, stop=c == n_c - 1 and i == len(passes) - 1)
                    return last

                def body(k, it):
                    slab, group = pl.slab + k, pl.group + k // parts
                    slot, p = slab % RING, group % 2
                    per = RING // parts // 2
                    if k % parts == 0 and group >= 2:
                        pe.wait_ge(s(f"lin_taken{p}"), at(group // 2, it, per))
                    if cut:
                        pe.wait_ge(s("w_cut"), at(pl.cut + k + 1, it, RING))
                        high, rest = w_hi[:, (pl.cut + k) % 2, :], w_lo[:, slot, :]
                    else:
                        pe.wait_ge(s(f"w_in{slot}"), at(16 * (slab // RING + 1), it, 16))
                    r = ring[:, slot, 0:width]
                    if kind == "down":
                        kc = width // P
                        for c in range(kc):
                            last = mm(LP[p][:, 0, :], r[:, blk(c)], src((k % parts) * kc + c),
                                      start=c == 0 and k % parts == 0, stop=c == kc - 1 and k % parts == parts - 1)
                    elif kind == "fm":
                        kc = width // 256
                        for f in range(2):
                            def chunk(c):
                                cols = slice(c * 256 + f * P, c * 256 + f * P + P)
                                return (high[:, cols], rest[:, cols]) if cut else r[:, cols]
                            last = products(LP[p][:, f, :], kc, chunk, src, False)
                    else:
                        kc = width // 256
                        for b in range(NB):
                            def chunk(c):
                                cols = slice(c * 256, (c + 1) * 256)
                                return (high[:, cols], rest[:, cols]) if cut else r[:, cols]

                            def tokens_of(c):
                                x_ = src(c)
                                return tuple(t[:, blk(b)] for t in x_) if cut else x_[:, blk(b)]
                            last = products(LPF[p][:, b * 256:(b + 1) * 256], kc, chunk, tokens_of, True)
                    last.then_inc(s("lin_done"), 1)
                    if n_ada == n or k < n_ada:
                        ada_sum(UP0 + pl.ada + k, it)

                slab_loop(pe, n, body, peel=4 if pl.slab == 0 else n_ada if 0 < n_ada < n else 2)
                pl.slab += n
                pl.group += n // parts
                pl.ada += n_ada
                pl.cut += n if cut else 0

            def square_sum(n, weights):
                if pl.norm:
                    pe.wait_ge(s("rt_ready"), pl.norm)
                for c in range(n):
                    pe.wait_ge(s("sq_ready"), pl.sq + c + 1)
                    mm(XB[0][:, :], weights, sq[:, c % 2, :], start=c == 0, stop=c == n - 1)\
                        .then_inc(s("sq_used"), 1)
                pl.sq += n
                pl.norm += 1

            def square_sums(n, weights):
                for i in range(n):
                    pe.wait_ge(s("rt_ready"), pl.norm - (i > 0))
                    pe.wait_ge(s("sq_ready"), pl.sq + 1)
                    mm(XB[i % 2][:, :], weights, sq[:, i % 2, :]).then_inc(s("sq_used"), 1)
                    pl.sq += 1
                    pl.norm += 1

            def total_sum():
                if pl.norm:
                    pe.wait_ge(s("rt_ready"), pl.norm)
                pl.got("squares_summed")
                mm(XB[0][:, :], cc("ones"), sqa).then_inc(s("total_ready"), 1)
                pl.norm += 1

            def norm(high):
                total_sum()
                first = pl.ur
                pl.ur += DC
                used = set()

                def src(c):
                    if c not in used:
                        used.add(c)
                        pe.wait_ge(s("u_ready"), first + c + 1)
                    return high[:, c, :], u_lo[:, c, :]
                return src

            def ffn(up, down):
                linear(up, "fm", norm(u_hi1))
                if up == "gu10":
                    ada_sum(N_ADA - 1, 0)
                pl.groups_taken()
                linear(down, "down", lambda c: big[:, c, :], parts=2)

            def rotate(chunks, weights):
                for i, c in enumerate(chunks):
                    if pl.rope + i >= 2:
                        pe.wait_ge(s("rope_done"), pl.rope + i - 1)
                    mm(XB[1 + (pl.rope + i) % 2][:, :], weights, big[:, c, :]).then_inc(s("rot_done"), 1)
                pl.rope += len(chunks)

            def attention(heads, score, val, hd, maps=1):
                per = P // hd
                n_units = heads * NB
                pl.groups_taken()
                if pl.rope:
                    pe.wait_ge(s("rope_done"), pl.rope)
                u0, p0, h0 = pl.unit, pl.prob, pl.head
                for n in range(n_units + 3):
                    if n < n_units:
                        hh, qb = divmod(n, NB)
                        for m in range(maps):
                            k = u0 + n * maps + m
                            if k >= 2:
                                pe.wait_ge(s("smax_done"), k - 1)
                            score(hh, m, qb, XB[k % 2]).then_inc(s("scores_done"), 1)
                    if 0 <= n - 2 < n_units:
                        i, qb = n - 2, (n - 2) % NB
                        k = p0 + i
                        if k >= 2:
                            pe.wait_ge(s("pt_done"), k - 1)
                        pe.wait_ge(s("probs_done"), k + 1)
                        src = wk[:, 4 + k % 2, :] if maps == 2 else E[:, k % 4, :]
                        for b in range(qb + 1):
                            last = pe.transpose(XB[2 + k % 2][:, blk(b)], src[:, blk(b)], cc("ident"))
                        last.then_inc(s("transposed"), 1)
                    if n >= 3:
                        i = n - 3
                        hh, qb = divmod(i, NB)
                        k, g = p0 + i, h0 + hh // per
                        if i % (per * NB) == 0 and g >= 2:
                            pe.wait_ge(s("o_taken"), g - 1)
                        pe.wait_ge(s("pt_done"), k + 1)
                        o = LP[0][half(hh) if per == 2 else slice(0, P), g % 2, blk(qb)]
                        for b in range(qb + 1):
                            last = mm(o, val(hh, b), ET[:, k % 2, blk(b)], start=b == 0, stop=b == qb)
                        last.then_inc(s("pv_done"), 1)
                pl.unit += n_units * maps
                pl.prob += n_units
                pl.head += heads // per

            pe.wait_ge(s("const_in"), 80)
            pe.wait_ge(s("cond_ready"), 1)
            for a in range(UP0):
                pe.wait_ge(s(f"ada_in{a % 2}"), 16 * (a // 2 + 1))
                if a:
                    pe.wait_ge(s("ada_done"), a)
                for f in range(2):
                    for c in range(DC):
                        last = mm(XB[3][:, f:f + 1], ada_in[:, a % 2, c * 256 + f * P:c * 256 + f * P + P],
                                  csil[:, c:c + 1], start=c == 0, stop=c == DC - 1)
                last.then_inc(s("ada_summed"), 1)
            ffn("gu00", "dn00")

            src = norm(u_hi1)
            linear("hyb", "fm", src)
            linear("hybv", "tm", src)
            rotate(list(range(DQ, DQ + 8)) + [IQ, IQ + 1, IK], cc("rot16"))
            for b in range(NB):
                last = mm(XB[3][:, 4 * b:4 * b + 4], big[32:36, GT, blk(b)], cc("ident")[32:36, 32:36])
            last.then_inc(s("iw_raw"), 1)

            def fox_score(hh, _, qb, bank):
                W = (qb + 1) * P
                r, o = half(hh), bank[:, 0:(qb + 1) * P]
                mm(o, big[r, FQ + hh // 2, blk(qb)], big[r, FK + hh // 2, 0:W], stop=False)
                one = cc("ident")[0:8, hh:hh + 1]
                mm(o, gate_row(slice(0, 8), 3)[:, blk(qb)], one.to_broadcast([8, W]), start=False, stop=False)
                return mm(o, one.to_broadcast([8, P]), gate_row(slice(0, 8), 0)[:, 0:W], start=False)

            pl.got("cum_ready")
            attention(FOX_H, fox_score, lambda hh, b: fv[:, b, 64 * hh:64 * hh + 64], 64)

            pe.wait_ge(s("smax_done"), pl.unit)
            for n in range(3 * IDX_H):
                qb, i = n // IDX_H + 1, n % IDX_H
                if n >= 2:
                    pe.wait_ge(s("idx_relu"), n - 1)
                mm(XB[n % 2][:, 0:(qb + 1) * P], big[half(i), IQ + i // 2, blk(qb)],
                   big[half(i), IK, 0:(qb + 1) * P]).then_inc(s("idx_done"), 1)
            pe.wait_ge(s("idx_relu"), 3 * IDX_H)

            def dsa_score(hh, _, qb, bank):
                r = half(hh)
                return mm(bank[:, 0:(qb + 1) * P], big[r, DQ + hh // 2, blk(qb)],
                          big[r, DK + hh // 2, 0:(qb + 1) * P])

            attention(DSA_H, dsa_score, lambda hh, b: dv[:, b, 64 * hh:64 * hh + 64], 64)
            pe.wait_ge(s("o_taken"), pl.head)
            linear("hybo", "fm", lambda c: u[:, c, :])
            ffn("gu01", "dn01")

            ffn("gu10", "dn10")
            linear("mlad", "fm", norm(u_hi1))
            square_sum(3, cc("ones"))
            square_sum(2, cc("ones"))
            pl.got("latent_ready", 2)
            linear("mlaq", "fm", lambda c: big[:, CQ + c, :])
            linear("mlak", "fm", lambda c: big[:, CKV + c, :])
            linear("mlav", "tm", lambda c: big[:, CKV + c, :])
            rotate([KR] + list(range(QR, QR + 4)), cc("rot64"))

            def mla_score(hh, _, qb, bank):
                W = (qb + 1) * P
                mm(bank[:, 0:W], big[:, QN + hh, blk(qb)], big[:, KN + hh, 0:W], stop=False)
                return mm(bank[:, 0:W], big[half(hh), QR + hh // 2, blk(qb)], big[half(hh), KR, 0:W],
                          start=False)

            attention(MLA_H, mla_score, lambda hh, b: mv[hh // 2][:, b, blk(hh % 2)], P)
            pe.wait_ge(s("o_taken"), pl.head)
            linear("mlao", "fm", lambda c: u[:, c, :])
            ffn("gu11", "dn11")

            pe.wait_ge(s("const2_in"), 16)
            total_sum()
            for l in range(DEPTH):
                src = norm(u_hi2)
                linear(f"in{l}", "fm", src)
                linear(f"inv{l}", "tm", src)

                square_sums(8, cc("blk64"))
                pl.got("qk_normed", 8)
                rotate(range(AQ, AQ + 8), cc("rot16"))

                def diff_score(hh, m, qb, bank):
                    return mm(bank[:, 0:(qb + 1) * P], big[half(m), AQ + hh, blk(qb)],
                              big[half(m), AK + hh, 0:(qb + 1) * P])

                attention(DIFF_H, diff_score, lambda hh, b: av[:, b, blk(hh)], P, maps=2)
                square_sums(DIFF_H, cc("ones"))

                pl.got("gates_rows")
                for b in range(NB):
                    last = mm(XB[3][:, 4 * b:4 * b + 4], gate_row(slice(0, 4), 3)[:, blk(b)], cc("ident")[0:4, 0:4])
                last.then_inc(s("a_cols"), 1)
                pl.got("conv_silu", 4)
                u0 = l * 4 * NB

                def weighted(n):
                    hh, b = divmod(n, NB)
                    pe.wait_ge(s("ms_ready"), u0 + n + 1)
                    o = (half(hh), hh // 2, slice(b * P, T))
                    mm(LP[0][o], xv[:, b, 64 * hh:64 * hh + 64], S[:, n % 2, 0:T - b * P],
                       start=b == 0, stop=b == NB - 1)
                    mm(LP[1][o], cc("ones", 0, 64), S[:, n % 2, 0:T - b * P],
                       start=b == 0, stop=b == NB - 1).then_inc(s("m_out"), 1)

                for n in range(4 * NB + 1):
                    hh, b = divmod(n, NB)
                    if n < 4 * NB:
                        if b == 0:
                            if l * 4 + hh:
                                pe.wait_ge(s("g_taken"), l * 4 + hh)
                            mm(XB[0][:, :], cc("ident")[0:4, hh:hh + 1].to_broadcast([4, P]),
                               gate_row(slice(0, 4), 5)).then_inc(s("g_ready"), 1)
                        if u0 + n >= 2:
                            pe.wait_ge(s("ms_ready"), u0 + n - 1)
                        mm(XB[1 + n % 2][:, 0:T - b * P], big[half(hh), XK + hh // 2, blk(b)],
                           big[half(hh), XQ + hh // 2, b * P:T]).then_inc(s("mqk_done"), 1)
                    if n:
                        weighted(n - 1)
                pl.got("em_rows")
                for cp in range(2):
                    if cp:
                        pl.got("em_taken")
                    mm(XB[3][:, :], cc("sel4", cp * P, P)[0:4, :], gate_row(slice(0, 4), 6)).then_inc(s("em_ready"), 1)
                    square_sum(1, cc("blk64"))
                pl.got("em_taken")

                for cp in range(2):
                    for step in range(10):
                        pl.got("z_ready")
                        for j in range(2):
                            k = (l * 2 + cp) * 20 + 2 * step + j
                            r = half(j)
                            if k >= 4:
                                pe.wait_ge(s("level_taken"), k - 3)
                            bank, z = XB[k % 4], E[r, step % 2, :]
                            if step == 0:
                                for b in range(NB):
                                    last = mm(bank[:, blk(b)], big[r, SP + cp, blk(b)], big[r, HQ + cp, blk(b)])
                            elif step < 8:
                                for b in range(NB):
                                    last = mm(bank[:, blk(b)], z[:, blk(b)], z[:, blk(b)])
                            elif step == 8:
                                for i, b in enumerate((0, 2)):
                                    last = mm(bank[:, blk(i)], z[:, blk(b)], z[:, blk(b + 1)])
                            else:
                                for b in range(2):
                                    last = mm(bank[:, b * 256:b * 256 + 256], z[:, blk(b)], z[:, 256:T])
                            last.then_inc(s("level_mm"), 1)
                    pl.got("a_done")
                    for j in range(2):
                        for b in range(NB):
                            v = hv[:, b, 64 * (2 * cp + j):64 * (2 * cp + j) + 64]
                            last = mm(LP[0][half(j), cp, blk(b)], v, wk[:, 2 + j, blk(b)],
                                      start=b == 0, stop=b == NB - 1)
                            if b < NB - 1:
                                o = (0, 384, 640)[b]
                                mm(LP[0][half(j), cp, (b + 1) * P:T], v,
                                   tmp[:, j, o:o + (NB - 1 - b) * P], start=False, stop=False)
                    last.then_inc(s("h_out"), 1)
                    square_sum(1, cc("blk64"))
                pl.got("mix_ready")
                linear(f"wo{l}", "fm", lambda c: u[:, c, :])
                linear(f"up{l}", "fm", norm(u_hi2))
                pl.groups_taken()
                linear(f"down{l}", "down", lambda c: big[:, c, :], parts=2)

        @block.scalar
        def _(act):
            pl = Place(act, s)

            def f(o, i, fn, **kw):
                return act.activation(o, i, fn, **kw)

            def rms(srcs, size):
                for c, src in enumerate(srcs):
                    if pl.sq + c >= 2:
                        act.wait_ge(s("sq_used"), pl.sq + c - 1)
                    f(sq[:, c % 2, :], src, ACT.Square).then_inc(s("sq_ready"), 1)
                pl.sq += len(srcs)
                act.wait_ge(s("sq_used"), pl.sq)
                if pl.norm:
                    act.wait_ge(s("rstd_ready"), pl.norm)
                f(rt[:, :], XB[0][:, :], ACT.Sqrt, scale=1.0 / size, bias=cc("eps")).then_inc(s("rt_ready"), 1)
                pl.norm += 1

            def rms_each(srcs, size):
                n = len(srcs)
                for i in range(n + 1):
                    if i < n:
                        if pl.sq + i >= 2:
                            act.wait_ge(s("sq_used"), pl.sq + i - 1)
                        f(sq[:, i % 2, :], srcs[i], ACT.Square).then_inc(s("sq_ready"), 1)
                    if i:
                        j = i - 1
                        act.wait_ge(s("sq_used"), pl.sq + j + 1)
                        act.wait_ge(s("rstd_ready"), pl.norm - (j > 0))
                        f(rts[j % 2], XB[j % 2][:, :], ACT.Sqrt, scale=1.0 / size, bias=cc("eps"))\
                            .then_inc(s("rt_ready"), 1)
                        pl.norm += 1
                pl.sq += n

            def high(j, it=0):
                slab, q = pl.slab + j, pl.cut + j
                slot = slab % RING
                act.wait_ge(s(f"w_in{slot}"), at(16 * (slab // RING + 1), it, 16))
                if j >= 2:
                    act.wait_ge(s("lin_done"), at(slab - 1, it, RING))
                elif pl.cut_end:
                    act.wait_ge(s("lin_done"), pl.cut_end)
                f(w_hi[:, q % 2, :], ring[:, slot, :], ACT.Copy).then_inc(s("w_high"), 1)

            def run(name, evacuate=None):
                n = sum(WIDTH[x_][0] for x_ in RUNS[name])

                def body(k, it):
                    if evacuate:
                        evacuate(k, it)
                    high(k + 2, it)

                slab_loop(act, n - 2, body)
                if evacuate:
                    evacuate(n - 2, 0)
                    evacuate(n - 1, 0)
                for x_ in RUNS[name]:
                    skip(x_)
                pl.cut += n
                pl.cut_end = pl.slab

            def high_input(dst, shift=None):
                for c in range(DC + 1):
                    if c < DC:
                        act.wait_ge(s("u_scaled"), pl.tu + c + 1)
                        if shift is not None:
                            f(u[:, c, :], u[:, c, :], ACT.Identity, bias=mod[:, shift + c:shift + c + 1])\
                                .then_inc(s("u_shifted"), 1)
                    if c:
                        if shift is not None:
                            pl.got("u_shifted")
                        f(dst[:, c - 1, :], u[:, c - 1, :], ACT.Copy).then_inc(s("u_high"), 1)
                pl.tu += DC

            def hrms(per=1, cut_at=(6, 7)):
                if pl.norm:
                    act.wait_ge(s("total_ready"), pl.seen.get("total_ready", 0))
                for c in range(DC):
                    for j, chunk in enumerate(cut_at):
                        if chunk == c:
                            high(j)
                    pl.chunk_final(c, per)
                    if c >= 3:
                        act.wait_ge(s("sq_added"), pl.seen.get("sq_added", 0) + c - 2)
                    f(sq[:, c % 2, :] if c else sqa, h[:, c, :], ACT.Square).then_inc(s("h_squared"), 1)
                pl.passed("sq_added", DC - 1)
                pl.got("total_ready")
                if pl.norm:
                    act.wait_ge(s("rstd_ready"), pl.norm)
                f(rt[:, :], XB[0][:, :], ACT.Sqrt, scale=1.0 / D, bias=cc("eps")).then_inc(s("rt_ready"), 1)
                pl.norm += 1

            def skip(name, parts=1):
                n = WIDTH[name][0]
                pl.slab += n
                pl.group += n // parts

            def ffn(l, j, up, down, per=1):
                first = up == "gu00"
                hrms(per, () if first else (4, 6) if per == 2 else (6, 7))
                high_input(u_hi1, (l * N_MOD + 3 * j) * DC)
                if first:
                    high(0)
                    high(1)
                g0, s0 = pl.group, pl.slab

                def silu(k, it):
                    act.wait_ge(s("lin_done"), at(s0 + k + 1, it, RING))
                    p = (g0 + k) % 2
                    f(tmp[:, p, 0:T], LP[p][:, 0, :], ACT.Silu).then_inc(s("silu_done"), 1)

                run(up, silu)
                skip(down, 2)

            def attention(heads, scale, hd, maps=1):
                n_units = heads * NB
                u0, p0 = pl.unit, pl.prob
                for n in range(n_units + 2):
                    if n < n_units:
                        W = (n % NB + 1) * P
                        for m in range(maps):
                            k = u0 + n * maps + m
                            act.wait_ge(s("smax_done"), k + 1)
                            if maps == 2:
                                if p0 + n >= 2:
                                    act.wait_ge(s("probs_done"), p0 + n - 1)
                            elif p0 + n >= 4:
                                act.wait_ge(s("transposed"), p0 + n - 3)
                            e = (2 * (p0 + n) + m) % 4 if maps == 2 else (p0 + n) % 4
                            f(E[:, e, 0:W], S[:, k % 2, 0:W], ACT.Exp, scale=scale, bias=stat[:, k % 4, 0:1],
                              accum_out=stat[:, k % 4, 1:2]).then_inc(s("exp_done"), 1)
                    if n >= 2:
                        k = p0 + n - 2
                        W = ((n - 2) % NB + 1) * P
                        act.wait_ge(s("transposed"), k + 1)
                        if k >= 2:
                            act.wait_ge(s("pv_done"), k - 1)
                        f(ET[:, k % 2, 0:W], XB[2 + k % 2][:, 0:W], ACT.Copy).then_inc(s("pt_done"), 1)
                pl.unit += n_units * maps
                pl.prob += n_units

            act.wait_ge(s("const_in"), 80)
            f(csil[:, :], sp_("cond", 0, DC), ACT.Silu).then_inc(s("cond_ready"), 1)
            ffn(0, 0, "gu00", "dn00")
            for i in range(4):
                pl.got("ang_ready")
                f(tabs[:, i, :], wk[:, 4 + i % 2, :], ACT.Sin).then_inc(s("tab_ready"), 1)

            hrms()
            high_input(u_hi1, (3 * 1) * DC)
            run("hyb")

            def log_sigmoid_parts(row):
                pl.got("gate_abs")
                r = slice(0, row)
                f(gate_row(r, 2), gate_row(r, 2), ACT.Exp, scale=-1.0).then_inc(s("scalar_chain"), 1)
                pl.got("scalar_chain")
                f(gate_row(r, 2), gate_row(r, 2), ACT.Ln, bias=1.0).then_inc(s("gate_ln"), 1)

            log_sigmoid_parts(8)
            attention(FOX_H, 0.125, 64)
            for n in range(3 * IDX_H):
                act.wait_ge(s("idx_done"), n + 1)
                if n >= 2:
                    act.wait_ge(s("idx_used"), n - 1)
                W = (n // IDX_H + 2) * P
                f(S[:, n % 2, 0:W], XB[n % 2][:, 0:W], ACT.Relu, scale=0.125).then_inc(s("idx_relu"), 1)
            attention(DSA_H, 0.125, 64)
            skip("hybo")
            ffn(0, 2, "gu01", "dn01", 2)

            ffn(1, 0, "gu10", "dn10")
            hrms()
            high_input(u_hi1, (N_MOD + 3 * 1) * DC)
            run("mlad")
            pl.groups_taken()
            rms([big[:, CQ + c, :] for c in range(3)], 384)
            rms([big[:, CKV + c, :] for c in range(2)], 256)
            skip("mlaq")
            skip("mlak")
            skip("mlav")
            attention(MLA_H, 192.0 ** -0.5, P)
            skip("mlao")
            ffn(1, 2, "gu11", "dn11", 2)

            hrms()
            pl.tu += DC
            act.wait_ge(s("u_scaled"), 7 * DC)
            pl.got("lb_shifted")
            f(st[:, 22:26], st[:, 18:22], ACT.Exp).then_inc(s("lb_exp"), 1)
            pl.got("lam_dots")
            f(st[:, 46:50], st[:, 42:46], ACT.Exp).then_inc(s("lam_exp"), 1)
            for l in range(DEPTH):
                hrms(cut_at=(6, 7) if l else ())
                high_input(u_hi2)
                run(f"in{l}")
                pl.groups_taken()
                rms_each([big[:, AQ + c, :] for c in range(8)], 64)
                attention(DIFF_H, 0.125, P, maps=2)
                act.wait_ge(s("o_taken"), 4 + 4 + 8 + 4 * (l + 1))
                rms_each([u[:, 2 + c, :] for c in range(DIFF_H)], P)

                for c in range(4):
                    pl.got("conv_raw")
                    f(big[:, XQ + c, :], wk[:, c % 2, :], ACT.Silu).then_inc(s("conv_silu"), 1)
                for c in range(2):
                    f(big[:, XO + c, :], big[:, XO + c, :], ACT.Sigmoid).then_inc(s("o_sigmoid"), 1)
                log_sigmoid_parts(4)
                pl.got("em_log")
                f(gate_row(slice(0, 4), 6), gate_row(slice(0, 4), 6), ACT.Exp, scale=-1.0).then_inc(s("em_rows"), 1)
                for n in range(4 * NB):
                    hh, b = divmod(n, NB)
                    pl.got("g_diag")
                    bias = tokw[:, 4 * b + hh:4 * b + hh + 1]
                    last = f(E[:, n % 4, 0:P], wk[:, 2 + n % 2, 0:P], ACT.Exp, bias=bias)
                    if b < NB - 1:
                        last = f(E[:, n % 4, P:T - b * P], wk[:, hh % 2, (b + 1) * P:T], ACT.Exp, bias=bias)
                    last.then_inc(s("me_done"), 1)
                for cp in range(2):
                    pl.got("m_mix")
                    rms([u[:, cp, :]], 64)

                for cp in range(2):
                    f(big[:, HQ + cp, :], big[:, HQ + cp, :], ACT.Silu)
                    f(big[:, HG + cp, :], big[:, HG + cp, :], ACT.Silu)
                    f(wk[:, 4, :], big[:, HF + cp, :], ACT.Sigmoid, scale=-1.0).then_inc(s("scalar_chain"), 1)
                    pl.got("scalar_chain")
                    f(big[:, HF + cp, :], big[:, HF + cp, :], ACT.Sigmoid).then_inc(s("h_sig"), 1)
                    pl.got("h_f")
                    f(big[:, HF + cp, :], big[:, HF + cp, :], ACT.Ln).then_inc(s("h_lnf"), 1)
                    for step in range(1, 10):
                        pl.got("x_ready")
                        k = (l * 2 + cp) * 10 + step
                        act.wait_ge(s("z_ready"), k - 1)
                        f(S[:, step % 2, :], wk[:, step % 2, :], ACT.Exp).then_inc(s("ex_ready"), 1)
                    pl.got("h_mix")
                    rms([u[:, 6 + cp, :]], 64)
                skip(f"wo{l}")
                hrms(2, (4, 6))
                high_input(u_hi2)
                g0, s0 = pl.group, pl.slab

                def relu(k, it):
                    act.wait_ge(s("lin_done"), at(s0 + k + 1, it, RING))
                    p = (g0 + k) % 2
                    f(tmp[:, p, :], LPF[p], ACT.Relu).then_inc(s("silu_done"), 1)

                run(f"up{l}", relu)
                skip(f"down{l}", 2)

        @block.gpsimd
        def _(gp):
            pl = Place(gp, s)

            def rest(j, it=0):
                slot, q = (pl.slab + j) % RING, pl.cut + j
                gp.wait_ge(s("w_high"), at(q + 1, it, RING))
                gp.tensor_tensor(w_lo[:, slot, :], ring[:, slot, :], w_hi[:, q % 2, :].bitcast(F32), ALU.subtract)\
                    .then_inc(s("w_cut"), 1)

            def skip(*names):
                pl.slab += sum(WIDTH[x_][0] for x_ in names)

            def run(name):
                n = sum(WIDTH[x_][0] for x_ in RUNS[name])
                slab_loop(gp, n - 2, lambda k, it: rest(k + 2, it))
                skip(*RUNS[name])
                pl.cut += n

            def squares(cut_at=(6, 7)):
                h0 = pl.seen.get("h_squared", 0)
                for c in range(1, DC):
                    for j, chunk in enumerate(cut_at):
                        if chunk == c:
                            rest(j)
                    gp.wait_ge(s("h_squared"), h0 + c + 1)
                    gp.tensor_tensor(sqa, sqa, sq[:, c % 2, :], ALU.add).then_inc(s("sq_added"), 1)
                    pl.got("sq_added")
                gp.nop().then_inc(s("squares_summed"), 1)
                pl.passed("h_squared", DC)

            def rest_input(high):
                for c in range(DC):
                    pl.got("u_high")
                    gp.tensor_tensor(u_lo[:, c, :], u[:, c, :], high[:, c, :].bitcast(F32), ALU.subtract)\
                        .then_inc(s("u_ready"), 1)

            def sublayer(run_name, cut_at=(6, 7)):
                squares(cut_at)
                rest_input(u_hi1)
                if not cut_at:
                    rest(0)
                    rest(1)
                run(run_name)

            def turn(chunks, t):
                for i, c in enumerate(chunks):
                    k = pl.rope + i
                    if k >= 2:
                        gp.wait_ge(s("rope_done"), k - 1)
                    gp.wait_ge(s("rot_done"), k + 1)
                    gp.tensor_tensor(S[:, k % 2, :], big[:, c, :], t, ALU.mult).then_inc(s("rope_cos"), 1)
                pl.rope += len(chunks)

            gp.wait_ge(s("const_in"), 80)
            sublayer("gu00", ())
            skip("dn00")
            sublayer("hyb")
            turn(list(range(DQ, DQ + 8)) + [IQ, IQ + 1, IK], tabs[:, 1, :])
            skip("hybo")
            sublayer("gu01", (4, 6))
            skip("dn01")
            sublayer("gu10")
            skip("dn10")
            sublayer("mlad")
            skip("mlaq", "mlak", "mlav", "mlao")
            turn([KR] + list(range(QR, QR + 4)), tabs[:, 3, :])
            sublayer("gu11", (4, 6))
            skip("dn11")
            gp.wait_ge(s("const2_in"), 16)
            squares()
            for l in range(DEPTH):
                squares((6, 7) if l else ())
                rest_input(u_hi2)
                run(f"in{l}")
                turn(range(AQ, AQ + 8), cc("diff_cos"))
                for cp in range(2):
                    pl.got("h_kb")
                    for step in range(10):
                        k = (l * 2 + cp) * 10 + step
                        if step == 0:
                            gp.nop().then_inc(s("z_ready"), 1)
                            continue
                        pl.got("ex_ready")
                        b = 1 << (step - 1)
                        if k >= 2:
                            gp.wait_ge(s("level_mm"), 2 * (k - 1))
                        z, e, kk, q = (t.rearrange("p (j i b) -> p j i b", i=2, b=b) for t in
                                       (E[:, step % 2, :], S[:, step % 2, :], big[:, SP + cp, :], big[:, HQ + cp, :]))
                        gp.tensor_tensor(z[:, :, 0, :], e[:, :, 0, :], kk[:, :, 0, :], ALU.mult)
                        gp.tensor_tensor(z[:, :, 1, :], e[:, :, 1, :], q[:, :, 1, :], ALU.mult)\
                            .then_inc(s("z_ready"), 1)
                skip(f"wo{l}")
                squares((4, 6))
                rest_input(u_hi2)
                run(f"up{l}")
                skip(f"down{l}")

        @block.vector
        def _(dve):
            pl = Place(dve, s)
            link = Chain(dve, s("vector_chain"))
            tt, ts, stt = dve.tensor_tensor, dve.tensor_scalar, dve.scalar_tensor_tensor

            def ada_acc_(a, it):
                dve.wait_ge(s(f"ada_in{a % 2}"), at(16 * (a // 2 + 1), it, 16 * RING // 2))
                wv = ada_in[:, a % 2, :]
                link(ts(ada_acc[:, :], wv[:, 0:256], csil[:, 0:1], None, ALU.mult))
                for c in range(1, DC):
                    ins = stt(ada_acc[:, :], wv[:, c * 256:(c + 1) * 256], csil[:, c:c + 1], ada_acc[:, :],
                              ALU.mult, ALU.add)
                    if c < DC - 1:
                        link(ins)
                ins.then_inc(s("ada_summed"), 1)

            def ada_take(a, it):
                if a < UP0 and isinstance(it, int):
                    dve.wait_ge(s("ada_summed"), a + 1)
                else:
                    dve.wait_ge(s("ada_col"), at(a + 1 - UP0, it, RING))
                if isinstance(it, int):
                    o, b = mod[:, 2 * a:2 * a + 2], modb[:, 2 * a:2 * a + 2]
                else:
                    o, b = (t[:, bass.ds(it * 2 * RING + 2 * a, 2)] for t in (mod, modb))
                tt(o, XB[3][:, 0:2], b, ALU.add).then_inc(s("ada_done"), 1)

            def take(name, body, parts=1, chains=()):
                n = WIDTH[name][0]
                n_ada = beside(pl, name)

                def one(k, it):
                    last_slab = pl.slab + (k + 1) * parts
                    dve.wait_ge(s("lin_done"), at(last_slab, it, RING))
                    body(k, it, (pl.group + k) % 2)
                    if n_ada == n or k < n_ada:
                        ada_take(UP0 + pl.ada + k, it)
                        a = UP0 + 1 + pl.ada + k
                        if a < N_ADA or not isinstance(it, int):
                            ada_acc_(a, it)

                slab_loop(dve, n // parts, one, unroll=RING // parts,
                          chains=[(link, DC - 1)] if n_ada == n else (),
                          peel=4 if pl.slab == 0 else n_ada if 0 < n_ada < n else 2)
                pl.slab += n
                pl.group += n // parts
                pl.ada += n_ada

            def dyn(t, k, it, step, n):
                a = step * k
                return slice(a, a + n) if isinstance(it, int) else bass.ds(it * step * RING + a, n)

            def root(i=0):
                dve.wait_ge(s("rt_ready"), pl.norm + 1)
                pl.norm += 1
                dve.reciprocal(rstds[i % 2], rts[i % 2]).then_inc(s("rstd_ready"), 1)
                dve.wait_ge(s("rstd_ready"), pl.norm)

            def scale_in(dst, gains):
                root()
                for c in range(DC):
                    stt(dst[:, c, :], h[:, c, :], gains[:, c:c + 1], rstd[:, :], ALU.mult, ALU.mult)\
                        .then_inc(s("u_scaled"), 1)
                pl.tu += DC

            def mod_vec(l, j):
                return mod[:, (l * N_MOD + j) * DC:(l * N_MOD + j + 1) * DC]

            def ada_ready(n):
                dve.wait_ge(s("ada_done"), n)

            def mod_in(l, j):
                ada_ready(min(N_ADA, ((l * N_MOD + 3 * j + 2) * DC) // 2))
                link(stt(gain[:, :], mod_vec(l, 3 * j + 1), 1.0, sp_("norm_g", (l * 3 + j) * DC, DC),
                         ALU.add, ALU.mult))
                scale_in(u, gain)

            def mod_gate(l, j, weight):
                ada_ready(min(N_ADA, ((l * N_MOD + 3 * j + 3) * DC) // 2))
                link(ts(gate[:, :], mod_vec(l, 3 * j + 2), weight, None, ALU.mult))

            def hidden(k, it, p):
                dve.wait_ge(s("silu_done"), at(pl.silu + k + 1, it, RING))
                tt(big[:, dyn(big, k, it, 1, 1), :], tmp[:, p, 0:T].unsqueeze(1), LP[p][:, 1:2, :], ALU.mult)\
                    .then_inc(s(f"lin_taken{p}"), 1)

            def position_tables():
                C1 = 6.28125
                C2 = float(np.float32(2 * math.pi - C1).view(np.int32) & ~0xfff and
                           (np.array(2 * math.pi - C1, np.float32).view(np.int32) & np.int32(~0xfff)).view(np.float32))
                C3 = 2 * math.pi - C1 - C2
                MAGIC = 1.5 * 2 ** 23
                link(dve.tensor_copy(wk[:, 0, :], posi))
                for i, (freq, quarter) in enumerate((("invf16", 0), ("invf16", 1), ("invf64", 0), ("invf64", 1))):
                    o = 4 + i % 2
                    if i >= 2:
                        dve.wait_ge(s("tab_ready"), i - 1)
                    link(ts(wk[:, 1, :], wk[:, 0, :], cc(freq), None, ALU.mult))
                    link(ts(wk[:, 2, :], wk[:, 1, :], 1 / (2 * math.pi), 0.25 * quarter, ALU.mult, ALU.add))
                    link(ts(wk[:, 2, :], wk[:, 2, :], MAGIC, None, ALU.add))
                    link(ts(wk[:, 2, :], wk[:, 2, :], MAGIC, None, ALU.subtract))
                    link(stt(wk[:, 1, :], wk[:, 2, :], -C1, wk[:, 1, :], ALU.mult, ALU.add))
                    link(stt(wk[:, 1, :], wk[:, 2, :], -C2, wk[:, 1, :], ALU.mult, ALU.add))
                    link(stt(wk[:, 1, :], wk[:, 2, :], -C3, wk[:, 1, :], ALU.mult, ALU.add))
                    link(ts(wk[:, 1, :], wk[:, 1, :], math.pi / 2 * quarter, -3.1415925, ALU.add, ALU.max))
                    ts(wk[:, o, :], wk[:, 1, :], 3.1415925, None, ALU.min).then_inc(s("ang_ready"), 1)
                    dve.wait_ge(s("ang_ready"), i + 1)

            def ffn(l, j, up, down):
                mod_in(l, j)
                if up == "gu00":
                    ada_acc_(UP0, 0)
                take(up, hidden)
                pl.silu += FC
                if up == "gu10":
                    ada_take(N_ADA - 1, 0)
                if up == "gu00":
                    position_tables()
                mod_gate(l, j, 0.5)

                def add(k, it, p):
                    at_ = slice(k, k + 1) if isinstance(it, int) else bass.ds(it * (RING // 2) + k, 1)
                    o, g = h[:, at_, :], gate[:, at_]
                    stt(o, LP[p][:, 0:1, :], g, o, ALU.mult, ALU.add).then_inc(s(f"lin_taken{p}"), 1)
                take(down, add, parts=2)

            def residual(l, j, name):
                mod_gate(l, j, 1.0)

                def add(k, it, p):
                    for i in range(2):
                        c = 2 * k + i
                        ins = stt(h[:, c, :], LP[p][:, i, :], gate[:, c:c + 1], h[:, c, :], ALU.mult, ALU.add)
                    ins.then_inc(s(f"lin_taken{p}"), 1)
                take(name, add)

            def plain(dst0):
                def body(k, it, p):
                    ts(big[:, bass.ds(it * 2 * RING + 2 * k + dst0, 2) if not isinstance(it, int)
                           else slice(dst0 + 2 * k, dst0 + 2 * k + 2), :], LP[p][:, :, :], 1.0, None, ALU.mult)\
                        .then_inc(s(f"lin_taken{p}"), 1)
                return body

            def tokens(dsts):
                def body(k, it, p):
                    ts(dsts[k], LPF[p].rearrange("p (t c) -> p t c", c=256), 1.0, None, ALU.mult)\
                        .then_inc(s(f"lin_taken{p}"), 1)
                return body

            def turn(chunks, t):
                for i, c in enumerate(chunks):
                    k = pl.rope + i
                    dve.wait_ge(s("rot_done"), k + 1)
                    link(tt(wk[:, k % 2, :], t, XB[1 + k % 2][:, :], ALU.mult))
                    dve.wait_ge(s("rope_cos"), k + 1)
                    tt(big[:, c, :], wk[:, k % 2, :], S[:, k % 2, :], ALU.add).then_inc(s("rope_done"), 1)
                pl.rope += len(chunks)
                dve.wait_ge(s("rope_done"), pl.rope)

            def attention(heads, scale, hd, mask, dst, maps=1, lam=None):
                per = P // hd
                n_units = heads * NB
                u0, p0, h0 = pl.unit, pl.prob, pl.head

                def out_of(g):
                    dve.wait_ge(s("pv_done"), p0 + (g + 1) * per * NB)
                    dve.tensor_copy(u[:, dst + g, :], LP[0][:, (h0 + g) % 2, :]).then_inc(s("o_taken"), 1)

                for n in range(n_units + 3):
                    if n < n_units:
                        qb = n % NB
                        W = (qb + 1) * P
                        for m in range(maps):
                            k = u0 + n * maps + m
                            dve.wait_ge(s("scores_done"), k + 1)
                            if k >= 2:
                                dve.wait_ge(s("exp_done"), k - 1)
                            link(dve.tensor_tensor_reduce(
                                out=S[:, k % 2, 0:W], in0=XB[k % 2][:, 0:W], in1=mask(qb, W), scale=1.0,
                                scalar=LOWEST, op0=ALU.add, op1=ALU.max, accum_out=stat[:, k % 4, 2:3]))
                            ts(stat[:, k % 4, 0:1], stat[:, k % 4, 2:3], -scale, None, ALU.mult)\
                                .then_inc(s("smax_done"), 1)
                    if 1 <= n <= n_units:
                        i = n - 1
                        W = (i % NB + 1) * P
                        k = p0 + i
                        for m in range(maps):
                            q = u0 + i * maps + m
                            dve.wait_ge(s("exp_done"), q + 1)
                            link(dve.reciprocal(stat[:, q % 4, 3:4], stat[:, q % 4, 1:2]))
                        if maps == 1:
                            ts(E[:, k % 4, 0:W], E[:, k % 4, 0:W], stat[:, q % 4, 3:4], None, ALU.mult)\
                                .then_inc(s("probs_done"), 1)
                        else:
                            q0 = u0 + 2 * i
                            link(ts(stat[:, q % 4, 3:4], stat[:, q % 4, 3:4], lam, None, ALU.mult))
                            link(ts(wk[:, 3, 0:W], E[:, 2 * k % 4, 0:W], stat[:, q0 % 4, 3:4], None, ALU.mult))
                            if k >= 2:
                                dve.wait_ge(s("transposed"), k - 1)
                            stt(wk[:, 4 + k % 2, 0:W], E[:, (2 * k + 1) % 4, 0:W], stat[:, q % 4, 3:4],
                                wk[:, 3, 0:W], ALU.mult, ALU.add).then_inc(s("probs_done"), 1)
                    if n >= 3 and (n - 2) % (per * NB) == 0:
                        out_of((n - 2) // (per * NB) - 1)
                pl.unit += n_units * maps
                pl.prob += n_units
                pl.head += heads // per

            def log_sigmoid(src, rows, bias):
                link(ts(gate_row(rows, 0), src, bias, None, ALU.add))
                link(ts(gate_row(rows, 1), gate_row(rows, 0), 0.0, None, ALU.min))
                stt(gate_row(rows, 2), gate_row(rows, 0), -1.0, gate_row(rows, 0), ALU.mult, ALU.max).then_inc(s("gate_abs"), 1)
                pl.got("gate_ln")
                link(tt(gate_row(rows, 0), gate_row(rows, 1), gate_row(rows, 2), ALU.subtract))

            dve.wait_ge(s("const_in"), 80)
            dve.wait_ge(s("cond_ready"), 1)
            for a in range(UP0):
                ada_take(a, 0)

            ffn(0, 0, "gu00", "dn00")
            pl.got("tab_ready", 4)

            mod_in(0, 1)
            take("hyb", plain(0))
            take("hybv", tokens([fv[:, :, 0:256], fv[:, :, 256:512], dv[:, :, 0:256], dv[:, :, 256:512]]))
            turn(list(range(DQ, DQ + 8)) + [IQ, IQ + 1, IK], tabs[:, 0, :])
            r8 = slice(0, 8)
            log_sigmoid(big[0:8, GT, :], r8, sp_("foxb")[0:8, :])
            link(dve.tensor_tensor_scan(gate_row(r8, 1), ones_row(r8), gate_row(r8, 0), 0.0,
                                        ALU.mult, ALU.add))
            link(ts(gate_row(r8, 3), gate_row(r8, 1), 8.0, None, ALU.mult))
            ts(gate_row(r8, 0), gate_row(r8, 1), -8.0, None, ALU.mult).then_inc(s("cum_ready"), 1)
            pl.got("iw_raw")
            link(ts(tokw[:, :], XB[3][:, 0:16], 0.5, None, ALU.mult))

            def causal(qb, W):
                return cc("causal", T - W, W)

            def chunked(qb, W):
                return cc("chunk", T - W, W)

            attention(FOX_H, 0.125, 64, causal, 0)

            for qb in range(1, NB):
                W = (qb + 1) * P
                sc, work, eq = wk[:, 0, 0:W], wk[:, 1, 0:W], wk[:, 2, 0:W]
                for i in range(IDX_H):
                    n = (qb - 1) * IDX_H + i
                    dve.wait_ge(s("idx_relu"), n + 1)
                    iwc = tokw[:, 4 * qb + i:4 * qb + i + 1]
                    if i == 0:
                        ins = ts(sc, S[:, n % 2, 0:W], iwc, None, ALU.mult)
                    else:
                        ins = stt(sc, S[:, n % 2, 0:W], iwc, sc, ALU.mult, ALU.add)
                    ins.then_inc(s("idx_used"), 1)
                    dve.wait_ge(s("idx_used"), n + 1)
                link(tt(sc, sc, chunked(qb, W), ALU.add))
                for i in range(TOPK // 8):
                    src = work if i else sc
                    link(dve.max(st[:, 0:8], src))
                    if i < TOPK // 8 - 1:
                        link(dve.match_replace(work, st[:, 0:8], src, LOWEST))
                thr = st[:, 7:8]
                link(ts(work, sc, thr, 0.0, ALU.is_gt, ALU.add, accum_out=st[:, 8:9]))
                link(ts(st[:, 9:10], st[:, 8:9], -1.0, float(TOPK), ALU.mult, ALU.add))
                link(ts(eq, sc, thr, None, ALU.is_equal))
                link(dve.tensor_tensor_scan(sc, ones_row(slice(0, P), W), eq, 0.0, ALU.mult, ALU.add))
                link(stt(sc, sc, st[:, 9:10], eq, ALU.is_le, ALU.mult))
                link(tt(sc, sc, work, ALU.add))
                link(ts(big[:, DMASK + qb, 0:W], sc, -NEG, NEG, ALU.mult, ALU.add))

            def selected(qb, W):
                return big[:, DMASK + qb, 0:W] if qb else chunked(0, P)

            attention(DSA_H, 0.125, 64, selected, 4)
            residual(0, 1, "hybo")
            ffn(0, 2, "gu01", "dn01")

            ffn(1, 0, "gu10", "dn10")
            mod_in(1, 1)
            take("mlad", plain(0))
            for c0, n, name in ((CQ, 3, "q_norm"), (CKV, 2, "kv_norm")):
                root()
                for c in range(n):
                    ins = stt(big[:, c0 + c, :], big[:, c0 + c, :], sp_(name, c), rstd[:, :], ALU.mult, ALU.mult)
                ins.then_inc(s("latent_ready"), 1)
                pl.got("latent_ready")
            take("mlaq", plain(QN))
            take("mlak", plain(KN))
            take("mlav", tokens(mv))
            turn([KR] + list(range(QR, QR + 4)), tabs[:, 2, :])
            attention(MLA_H, 192.0 ** -0.5, P, chunked, 0)
            residual(1, 1, "mlao")
            ffn(1, 2, "gu11", "dn11")

            dve.wait_ge(s("const2_in"), 16)
            scale_in(h, sp_("final_g", 0, DC))
            dve.wait_ge(s("u_scaled"), pl.tu)
            lb = sp_("lb", 0, 4)
            link(tt(st[:, 16:18], lb[:, 0:2], lb[:, 2:4], ALU.max))
            for l in range(DEPTH):
                ins = tt(st[:, 18 + 2 * l:20 + 2 * l], lb[:, 2 * l:2 * l + 2], st[:, 16:18], ALU.subtract)
            ins.then_inc(s("lb_shifted"), 1)
            pl.got("lb_exp")
            link(tt(st[:, 26:28], st[:, 22:24], st[:, 24:26], ALU.add))
            link(dve.reciprocal(st[:, 28:30], st[:, 26:28]))
            for l in range(DEPTH):
                link(tt(st[:, 30 + 2 * l:32 + 2 * l], st[:, 22 + 2 * l:24 + 2 * l], st[:, 28:30], ALU.mult))
            link(tt(st[:, 34:36], st[:, 30:32], st[:, 30:32], ALU.subtract))
            link(tt(st[:, 36:38], st[:, 30:32], st[:, 32:34], ALU.add))
            link(tt(st[:, 36:38], st[:, 36:38], st[:, 30:32], ALU.subtract))
            link(ts(st[:, 38:42], st[:, 34:38], -1.0, 1.0, ALU.mult, ALU.add))
            for l in range(DEPTH):
                for i in range(2):
                    a = l * 256 + 128 * i
                    link(dve.tensor_tensor_reduce(
                        out=wk[:, 0, 0:64], in0=cc("lam", a, 64), in1=cc("lam", a + 64, 64), scale=1.0,
                        scalar=0.0, op0=ALU.mult, op1=ALU.add, accum_out=st[:, 42 + 2 * l + i:43 + 2 * l + i]))
            dve.nop().then_inc(s("lam_dots"), 1)
            pl.got("lam_exp")
            for l in range(DEPTH):
                init = 0.8 - 0.6 * math.exp(-0.3 * l)
                link(tt(st[:, 50 + l:51 + l], st[:, 47 + 2 * l:48 + 2 * l], st[:, 46 + 2 * l:47 + 2 * l], ALU.subtract))
                link(ts(st[:, 50 + l:51 + l], st[:, 50 + l:51 + l], -init, None, ALU.add))

            for l in range(DEPTH):
                init = 0.8 - 0.6 * math.exp(-0.3 * l)
                scale_in(u, sp_("norm1", l * DC, DC))
                take(f"in{l}", plain(0))
                take(f"inv{l}", tokens([xv[:, :, :], av[:, :, 0:256], av[:, :, 256:512], hv[:, :, :]]))
                for i in range(8):
                    root(i)
                    stt(big[:, AQ + i, :], big[:, AQ + i, :], sp_("qn" if i < 4 else "kn", l), rstds[i % 2],
                        ALU.mult, ALU.mult).then_inc(s("qk_normed"), 1)
                    pl.got("qk_normed")
                turn(range(AQ, AQ + 8), cc("diff_sin"))
                attention(DIFF_H, 0.125, P, causal, 2, maps=2, lam=st[:, 50 + l:51 + l])
                link(ts(st[:, 52:53], sp_("subln", l), 1.0 - init, None, ALU.mult))
                for c in range(DIFF_H):
                    root(c)
                    link(stt(u[:, 2 + c, :], u[:, 2 + c, :], st[:, 52:53], rstds[c % 2], ALU.mult, ALU.mult))

                for c in range(4):
                    if c >= 2:
                        pl.got("conv_silu")
                    y, xx = wk[:, c % 2, :], big[:, XQ + c, :]
                    tap = [sp_("conv", (l * 4 + c) * 4 + i) for i in range(4)]
                    link(ts(y, xx, tap[3], None, ALU.mult))
                    for d in (1, 2, 3):
                        ins = stt(y[:, d:T], xx[:, 0:T - d], tap[3 - d], y[:, d:T], ALU.mult, ALU.add)
                        if d < 3:
                            link(ins)
                    ins.then_inc(s("conv_raw"), 1)
                pl.got("conv_silu", 2)
                r4 = slice(0, 4)
                log_sigmoid(big[0:4, GF, :], r4, sp_("gateb", 2 * l + 1)[0:4, :])
                link(ts(gate_row(r4, 1), big[0:4, GI, :], sp_("gateb", 2 * l)[0:4, :], None, ALU.add))
                link(dve.tensor_tensor_scan(gate_row(r4, 4), ones_row(r4), gate_row(r4, 0), 0.0,
                                            ALU.mult, ALU.add))
                link(tt(gate_row(r4, 3), gate_row(r4, 1), gate_row(r4, 4), ALU.subtract))
                link(dve.tensor_tensor_scan(gate_row(r4, 2), gate_row(r4, 3), gate_row(r4, 3), 0.0,
                                            ALU.max, ALU.max))
                link(tt(gate_row(r4, 6), gate_row(r4, 2), gate_row(r4, 4), ALU.add))
                dve.nop().then_inc(s("em_log"), 1)
                link(ts(gate_row(r4, 5), gate_row(r4, 2), -1.0, None, ALU.mult))
                dve.nop().then_inc(s("gates_rows"), 1)
                pl.got("a_cols")
                link(dve.tensor_copy(tokw[:, :], XB[3][:, 0:16]))
                u0 = l * 4 * NB
                for n in range(4 * NB + 1):
                    if n < 4 * NB:
                        hh, b = divmod(n, NB)
                        if b == 0:
                            pl.got("g_ready")
                            dve.tensor_copy(wk[:, hh % 2, :], XB[0][:, :]).then_inc(s("g_taken"), 1)
                            dve.wait_ge(s("g_taken"), l * 4 + hh + 1)
                        tt(wk[:, 2 + n % 2, 0:P], wk[:, hh % 2, blk(b)], cc("tri"), ALU.add)\
                            .then_inc(s("g_diag"), 1)
                    if n:
                        i = n - 1
                        hh, b = divmod(i, NB)
                        W = T - b * P
                        dve.wait_ge(s("me_done"), u0 + i + 1)
                        dve.wait_ge(s("mqk_done"), u0 + i + 1)
                        if u0 + i >= 2:
                            dve.wait_ge(s("m_out"), u0 + i - 1)
                        stt(S[:, i % 2, 0:W], XB[1 + i % 2][:, 0:W], 0.125, E[:, i % 4, 0:W], ALU.mult, ALU.mult)\
                            .then_inc(s("ms_ready"), 1)
                dve.wait_ge(s("m_out"), u0 + 4 * NB)
                for cp in range(2):
                    pl.got("em_ready")
                    dve.tensor_copy(wk[:, 2, :], XB[3][:, :]).then_inc(s("em_taken"), 1)
                    dve.wait_ge(s("em_taken"), 2 * l + cp + 1)
                    link(stt(wk[:, 3, :], LP[1][:, cp, :], -1.0, wk[:, 2, :], ALU.mult, ALU.max))
                    link(tt(wk[:, 3, :], wk[:, 3, :], LP[1][:, cp, :], ALU.max))
                    link(dve.reciprocal(wk[:, 3, :], wk[:, 3, :]))
                    tt(u[:, cp, :], wk[:, 3, :], LP[0][:, cp, :], ALU.mult).then_inc(s("m_mix"), 1)
                    root()
                    link(stt(u[:, cp, :], u[:, cp, :], sp_("mnorm", l), rstd[:, :], ALU.mult, ALU.mult))
                    pl.got("o_sigmoid")
                    link(tt(u[:, cp, :], u[:, cp, :], big[:, XO + cp, :], ALU.mult))

                for cp in range(2):
                    c = 2 * l + cp
                    lbc, olb = st[:, 34 + c:35 + c], st[:, 38 + c:39 + c]
                    pl.got("h_sig")
                    ts(big[:, HF + cp, :], big[:, HF + cp, :], olb, lbc, ALU.mult, ALU.add)\
                        .then_inc(s("h_f"), 1)
                    link(ts(big[:, SP + cp, :], wk[:, 4, :], olb, None, ALU.mult))
                    pl.got("h_lnf")
                    link(dve.tensor_tensor_scan(big[:, XQ + cp, :], ones_row(slice(0, P)), big[:, HF + cp, :], 0.0,
                                                ALU.mult, ALU.add))
                    dve.nop().then_inc(s("h_kb"), 1)
                    B = big[:, XQ + cp, :]

                    def exponents(step):
                        b = 1 << (step - 1)
                        Bv, X = (t.rearrange("p (j i b) -> p j i b", i=2, b=b) for t in (B, wk[:, step % 2, :]))
                        ref = Bv[:, :, 0, b - 1:b].to_broadcast([P, T // (2 * b), b])
                        if step >= 3:
                            dve.wait_ge(s("ex_ready"), (2 * l + cp) * 9 + step - 2)
                        tt(X[:, :, 0, :], ref, Bv[:, :, 0, :], ALU.subtract)
                        tt(X[:, :, 1, :], Bv[:, :, 1, :], ref, ALU.subtract).then_inc(s("x_ready"), 1)

                    exponents(1)
                    for step in range(10):
                        if 1 <= step < 9:
                            exponents(step + 1)
                        for j in range(2):
                            k = (l * 2 + cp) * 20 + 2 * step + j
                            bank = XB[k % 4]
                            dve.wait_ge(s("level_mm"), k + 1)
                            ad = wk[:, 2 + j, :].rearrange("p (b t) -> p b t", b=NB)
                            bk = bank[:, :].rearrange("p (b t) -> p b t", b=NB)
                            m = cc("levels", step * P, P).unsqueeze(1).to_broadcast([P, NB, P]) if step < 8 else None
                            if step == 0:
                                ins = tt(ad, m, bk, ALU.mult)
                            elif step < 8:
                                ins = dve.copy_predicated(ad, m.bitcast(U32), bk)
                            elif step == 8:
                                dve.tensor_copy(tmp[:, j, 0:P], bank[:, 0:P])
                                ins = dve.tensor_copy(tmp[:, j, 640:768], bank[:, P:2 * P])
                            else:
                                ins = dve.tensor_copy(tmp[:, j, P:640], bank[:, :])
                            ins.then_inc(s("level_taken"), 1)
                            dve.wait_ge(s("level_taken"), k + 1)
                    dve.nop().then_inc(s("a_done"), 1)
                    pl.got("h_out")
                    dve.tensor_copy(u[:, 6 + cp, :], LP[0][:, cp, :]).then_inc(s("h_mix"), 1)
                    root()
                    link(stt(u[:, 6 + cp, :], u[:, 6 + cp, :], sp_("hnorm", l), rstd[:, :], ALU.mult, ALU.mult))
                    link(tt(u[:, 6 + cp, :], u[:, 6 + cp, :], big[:, HG + cp, :], ALU.mult))
                dve.nop().then_inc(s("mix_ready"), 1)

                def add2(k, it, p):
                    tt(h[:, 2 * k:2 * k + 2, :], h[:, 2 * k:2 * k + 2, :], LP[p][:, :, :], ALU.add)\
                        .then_inc(s(f"lin_taken{p}"), 1)

                take(f"wo{l}", add2)
                scale_in(u, sp_("norm2", l * DC, DC))

                def square(k, it, p):
                    dve.wait_ge(s("silu_done"), at(pl.silu + k + 1, it, RING))
                    t = tmp[:, p, :].rearrange("p (a b) -> p a b", a=2)
                    tt(big[:, dyn(big, k, it, 2, 2), :], t, t, ALU.mult).then_inc(s(f"lin_taken{p}"), 1)

                take(f"up{l}", square)
                pl.silu += 16

                def add1(k, it, p):
                    a = k
                    o = h[:, a:a + 1, :] if isinstance(it, int) else h[:, bass.ds(it * 2 + a, 1), :]
                    tt(o, o, LP[p][:, 0:1, :], ALU.add).then_inc(s(f"lin_taken{p}"), 1)

                take(f"down{l}", add1, parts=2)


GROUPS = 4 * (FC + DC) + 18 + 3 + 6 + 4 + 4 + 4 + DEPTH * (11 + 4 + 4 + 16 + 8)



def _const_table(lam):
    c = np.zeros((P, NCONST), np.float32)
    c2 = np.zeros((P, NCONST2), np.float32)

    def put(name, a):
        t, (o, wd) = (c, COFF[name]) if name in COFF else (c2, COFF2[name])
        t[:a.shape[0], o:o + a.shape[1]] = a

    put("lam", np.broadcast_to(lam.reshape(1, -1), (P, DEPTH * 256)))

    i = np.arange(P)
    t = np.arange(T)
    put("ident", np.eye(P))
    put("ones", np.ones((P, P)))
    put("blk64", (i[:, None] // 64 == i[None, :] // 64) * 1.0)
    for name, half in (("rot16", 8), ("rot64", 32)):
        r = np.zeros((P, P))
        for b in (0, 64):
            for k in range(half):
                r[b + half + k, b + k] = -1.0
                r[b + k, b + half + k] = 1.0
        put(name, r)
    m = np.zeros((P, T))
    m[:, T - P:] = np.where(i[None, :] <= i[:, None], 0.0, NEG)
    put("causal", m)
    m = np.zeros((P, T))
    m[:, T - P:] = np.where(i[None, :] // 64 <= i[:, None] // 64, 0.0, NEG)
    put("chunk", m)
    put("tri", np.where(i[:, None] <= i[None, :], 0.0, NEG))
    lv = [np.eye(P)]
    for k in range(7):
        b = 1 << k
        same = i[:, None] // (2 * b) == i[None, :] // (2 * b)
        lv.append((same & (i[:, None] // b % 2 == 0) & (i[None, :] // b % 2 == 1)) * 1.0)
    put("levels", np.concatenate(lv, 1))
    for name, rot, theta in (("invf16", 16, 500000.0), ("invf64", 64, 10000.0)):
        half = rot // 2
        f = np.exp(np.float32(-math.log(theta) * 2.0) * np.arange(half, dtype=np.float32) / np.float32(rot))
        col = np.zeros((64, 1), np.float32)
        col[:half, 0] = f
        col[half:rot, 0] = f
        put(name, np.concatenate([col, col]))
    put("eps", np.full((P, 1), RMS_EPS))
    half = 8
    inv = np.float32(500000.0) ** (-np.arange(half, dtype=np.float32) / half)
    ang = t.astype(np.float32)[None, :] * inv[:, None].astype(np.float32)
    cos, sin = np.ones((64, T)), np.zeros((64, T))
    for k in (0, half):
        cos[k:k + half] = np.cos(ang.astype(np.float64))
        sin[k:k + half] = np.sin(ang.astype(np.float64))
    put("diff_cos", np.concatenate([cos, cos]))
    put("diff_sin", np.concatenate([sin, sin]))
    sel = np.zeros((4, 2 * P))
    for cp in range(2):
        for half in range(2):
            sel[2 * cp + half, cp * P + 64 * half:cp * P + 64 * half + 64] = 1.0
    put("sel4", sel)
    return c, c2


def _columns(v):
    return np.asarray(v).reshape(-1, P).T


def _fm(wt):
    K, F = wt.shape
    return np.ascontiguousarray(wt.reshape(K // P, P, F // 256, 256).transpose(2, 1, 0, 3)).reshape(F // 256, P, -1)


def _halves(wt):
    K = wt.shape[0]
    return np.ascontiguousarray(
        wt.reshape(2, K // (2 * P), P, DC, P).transpose(3, 0, 2, 1, 4)).reshape(2 * DC, P, -1)


def kernel(**inp):
    import concourse.bacc as _bacc
    from concourse.bass_utils import run_bass_kernel_spmd as _run

    a = {k: np.asarray(v) for k, v in inp.items()}
    small = np.zeros((P, NSMALL), np.float32)

    def put(name, v, at=0, rows=P):
        o = SOFF[name][0] + at
        small[:rows, o:o + v.shape[1]] = v

    put("norm_g", _columns(a["norm_g"]))
    put("final_g", _columns(a["final_g"]))
    put("norm1", _columns(a["norm1_g_2"]))
    put("norm2", _columns(a["norm2_g_2"]))
    put("q_norm", _columns(a["mla_q_norm"]))
    put("kv_norm", _columns(a["mla_kv_norm"]))
    put("conv", a["mlstm_conv_w_2"].reshape(DEPTH, 4, 4, P).transpose(3, 0, 2, 1).reshape(P, -1))
    for l in range(DEPTH):
        for name, key in (("mnorm", "mlstm_norm_g_2"), ("qn", "diff_q_norm_g_2"), ("kn", "diff_k_norm_g_2"),
                          ("hnorm", "hgrn_norm_g_2")):
            put(name, np.tile(a[key][l], 2)[:, None], l)
        put("subln", a["diff_subln_g_2"][l][:, None], l)
        for i in range(2):
            put("gateb", a["mlstm_gate_b_2"][l, i][:, None], 2 * l + i, rows=4)
    put("lb", _columns(a["hgrn_lb_param_2"]))
    put("cond", _columns(a["c"]))
    put("foxb", a["fox_b_f"][0][:, None], rows=8)
    W = {"ada": np.concatenate([_fm(a["ada_w"][l]) for l in range(DEPTH)])}
    for l in range(DEPTH):
        for j in range(2):
            g, up, dn = (a[k][l, j] for k in ("ffn_w_gate", "ffn_w_up", "ffn_w_down"))
            gu = np.stack([g.reshape(D, FC, P), up.reshape(D, FC, P)], 2).reshape(D, 2 * FF)
            W[f"gu{l}{j}"] = _fm(gu)
            W[f"dn{l}{j}"] = _halves(dn)
    hw = a["hyb_w_in"][0]
    off = np.cumsum([0, 512, 512, 512, 8, 512, 512, 512, 256, 4, 64])
    fq, fk, fvw, ff, dq, dk, dvw, iq, iwt, ik = (hw[:, off[i]:off[i + 1]] for i in range(10))
    z = lambda n: np.zeros((D, n), np.float32)
    W["hyb"] = _fm(np.concatenate([fq, fk, dq, dk, iq, ik, ik, ff, z(24), iwt, z(92)], 1))
    W["hybv"] = _fm(np.concatenate([fvw, dvw], 1))
    W["hybo"] = _fm(a["hyb_w_out"][0])
    md = a["mla_w_down"][0]
    W["mlad"] = _fm(np.concatenate([md, md[:, 640:704]], 1))
    uq = a["mla_w_uq"][0].reshape(384, MLA_H, 192)
    W["mlaq"] = _fm(np.concatenate([uq[:, :, :128].reshape(384, -1), uq[:, :, 128:].reshape(384, -1)], 1))
    ukv = a["mla_w_ukv"][0].reshape(256, MLA_H, 256)
    W["mlak"] = _fm(np.ascontiguousarray(ukv[:, :, :128]).reshape(256, -1))
    W["mlav"] = _fm(np.ascontiguousarray(ukv[:, :, 128:]).reshape(256, -1))
    W["mlao"] = _fm(a["mla_w_out"][0])
    for l in range(DEPTH):
        wi = a["w_in_2"][l]
        off = np.cumsum([0, 256, 256, 256, 256, 4, 4, 512, 512, 512, 256, 256, 256, 256])
        mq, mk, mvw, mo, mi, mf, aq, ak, avw, hq, hf, hi, hg = (wi[:, off[i]:off[i + 1]] for i in range(13))
        W[f"in{l}"] = _fm(np.concatenate([mq, mk, mo, aq, ak, hq, hf, hg, mi, z(124), mf, z(124)], 1))
        W[f"inv{l}"] = _fm(np.concatenate([mvw, avw, hi], 1))
        W[f"wo{l}"] = _fm(a["w_out_2"][l])
        W[f"up{l}"] = _fm(a["w_up_2"][l])
        W[f"down{l}"] = _halves(a["w_down_2"][l])

    consts, consts2 = _const_table(a["diff_lambda_2"])
    arrays = {
        "x": np.ascontiguousarray(a["x"][0].T.reshape(DC, P, T).transpose(1, 0, 2)),
        "small": small,
        "consts": consts,
        "consts2": consts2,
        "pos": np.ascontiguousarray(np.broadcast_to(a["positions"].astype(np.int32), (P, T))),
        "adab": np.ascontiguousarray(_columns(a["ada_b"])),
    }
    nc = _bacc.Bacc("TRN2", target_bir_lowering=False, num_devices=1)

    def dram(name, arr):
        return nc.dram_tensor(name, arr.shape, mybir.dt.from_np(arr.dtype), kind="ExternalInput").ap()

    aps = {k: dram(k, v) for k, v in arrays.items()}
    w = {k: dram("w_" + k, v) for k, v in W.items()}
    arrays.update({"w_" + k: v for k, v in W.items()})
    out = nc.dram_tensor("out", (P, DC, T), F32, kind="ExternalOutput").ap()
    build(nc, aps["x"], aps["small"], aps["consts"], aps["consts2"], aps["pos"], aps["adab"], w, out)
    r = _run(nc, [arrays], core_ids=[0])
    got = r.results[0]["out"]
    return np.ascontiguousarray(got.transpose(1, 0, 2).reshape(D, T).T)[None]
```

```python
import math
from contextlib import ExitStack

import numpy as np

import concourse.bass as bass
from concourse import mybir

F32 = mybir.dt.float32
F32R = mybir.dt.float32r
I32 = mybir.dt.int32
U32 = mybir.dt.uint32
ALU = mybir.AluOpType
ACT = mybir.ActivationFunctionType
AX = mybir.AxisListType

P = 128
T = 512
NB = T // P
D = 1024
DC = D // P
FF = 2816
FC = FF // P
FF2 = 4 * D
FC2 = FF2 // P
DEPTH = 2
N_MOD = 9
TOPK = 128
NEG = -1e30
LOWEST = -3e38
RMS_EPS = 1e-6

FOX_H = 8
DSA_H = 8
IDX_H = 4
MLA_H = 8
DIFF_H = 4
RING = 4
SLAB = 16 * P
UP0 = 10
N_ADA = DEPTH * N_MOD * D // 256

CONSTS = [("ident", P), ("ones", P), ("blk64", P), ("rot16", P), ("rot64", P),
          ("causal", T), ("chunk", T), ("sel4", 2 * P), ("invf16", 1), ("invf64", 1), ("eps", 1)]
CONSTS2 = [("tri", P), ("levels", 8 * P), ("diff_cos", T), ("diff_sin", T), ("lam", DEPTH * 4 * 64)]


def _offsets(table):
    off, n = {}, 0
    for name, width in table:
        off[name] = (n, width)
        n += width
    return off, n


COFF, NCONST = _offsets(CONSTS)
COFF2, NCONST2 = _offsets(CONSTS2)

SMALL = [("norm_g", DEPTH * 3 * DC), ("final_g", DC), ("norm1", DEPTH * DC), ("norm2", DEPTH * DC),
         ("q_norm", 3), ("kv_norm", 2), ("conv", DEPTH * 4 * 4), ("mnorm", DEPTH),
         ("qn", DEPTH), ("kn", DEPTH), ("subln", DEPTH), ("lb", DEPTH * 2), ("hnorm", DEPTH),
         ("cond", DC), ("foxb", 1), ("gateb", DEPTH * 2)]
SOFF, NSMALL = _offsets(SMALL)


def slab_loop(eng, n, body, chains=(), unroll=RING, peel=None):
    peel = n % unroll if peel is None else min(peel, n)
    for r in range(peel):
        body(r, 0)
    turns = (n - peel) // unroll
    done = peel
    if turns >= 2:
        for ch, per in chains:
            ch.enter(per * unroll)
        with eng.Fori(0, turns) as it:
            for ch, _ in chains:
                ch.it = it
            for u in range(unroll):
                body(peel + u, it)
        for ch, _ in chains:
            ch.leave(turns)
        done += turns * unroll
    for r in range(done, n):
        body(r, 0)


class Chain:

    def __init__(self, eng, sem):
        self.eng, self.sem, self.n = eng, sem, 0
        self.it, self.per, self.base = None, 0, 0

    def enter(self, per):
        self.base, self.per = self.n, per

    def leave(self, turns):
        assert self.n - self.base == self.per, (self.n - self.base, self.per)
        self.n = self.base + self.per * turns
        self.it = None

    def __call__(self, ins):
        self.n += 1
        ins.then_inc(self.sem, 1)
        self.eng.wait_ge(self.sem, self.n if self.it is None else self.it * self.per + self.n)


class Place:

    def __init__(self, eng, sems):
        self.eng, self.sems = eng, sems
        self.slab = self.group = self.ada = 0
        self.cut = 0
        self.low = 0
        self.norm = self.sq = self.silu = self.tu = self.ur = 0
        self.rope = self.unit = self.prob = self.head = 0
        self.seen = {}

    def got(self, name, n=1):
        self.seen[name] = self.seen.get(name, 0) + n
        self.eng.wait_ge(self.sems(name), self.seen[name])

    def passed(self, name, n=1):
        self.seen[name] = self.seen.get(name, 0) + n

    def groups_taken(self):
        if self.group:
            self.eng.wait_ge(self.sems("lin_taken0"), (self.group + 1) // 2)
        if self.group > 1:
            self.eng.wait_ge(self.sems("lin_taken1"), self.group // 2)


    def chunk_final(self, c, per):
        g = self.group - DC // per + c // per
        if self.group:
            self.eng.wait_ge(self.sems(f"lin_taken{g % 2}"), g // 2 + 1)


def at(value, it, per):
    return value if isinstance(it, int) else it * per + value


FQ, FK, DQ, DK, IQ, IK, GT, FV, DV, DMASK = 0, 4, 8, 12, 16, 18, 19, 20, 24, 28
CQ, CKV, KR, QN, QR, KN, MV = 0, 3, 5, 6, 14, 18, 26
XQ, XK, XO, AQ, AK, HQ, HF, HG, GI, GF, XV, AV, HV, SP = 0, 2, 4, 6, 10, 14, 16, 18, 20, 21, 22, 24, 28, 30


def build(nc, x, small, consts, consts2, pos, adab, w, out):
    with ExitStack() as ctx:
        sems = {}

        def s(name):
            if name not in sems:
                sems[name] = ctx.enter_context(nc.semaphore(name))
            return sems[name]

        place = {}

        def sb(name, shape, dt=F32):
            place[name] = -(-place.get("end", nc.sbuf_base) // 32) * 32
            place["end"] = place[name] + 4 * int(np.prod(shape[1:]))
            assert place["end"] <= nc.sbuf_usable_end, (name, place["end"], nc.sbuf_usable_end)
            return nc.alloc_sbuf_tensor_at(name, shape, dt, offset=place[name])

        def over(name, shape, base, chunk=0):
            return nc.alloc_sbuf_tensor_at(name, shape, F32R, offset=place[base] + 4 * T * chunk)

        h = sb("h", [P, DC, T])
        u = sb("u", [P, DC, T])
        big = sb("big", [P, 32, T])
        wk = sb("wk", [P, 6, T])
        tabs = sb("tabs", [P, 4, T])
        ring = sb("ring", [P, RING, SLAB])
        S = sb("S", [P, 2, T])
        E = sb("E", [P, 4, T])
        ET = sb("ET", [P, 2, T])
        ada_in = sb("ada_in", [P, 2, DC * 256])
        ada_acc = sb("ada_acc", [P, 256])
        cst = sb("cst", [P, NCONST])
        sm = sb("sm", [P, NSMALL])
        mod = sb("mod", [P, N_ADA * 2])
        modb = sb("modb", [P, N_ADA * 2])
        gain = sb("gain", [P, DC])
        gate = sb("gate", [P, DC])
        tmp = sb("tmp", [P, 2, 2 * T])
        rt = sb("rt", [P, T])
        rstd = sb("rstd", [P, T])
        sq = sb("sq", [P, 2, T])
        st = sb("st", [P, 64])
        stat = sb("stat", [P, 4, 4])
        csil = sb("csil", [P, DC])
        tokw = sb("tokw", [P, 4 * NB])
        u_lo = over("u_lo", [P, DC, T], "u")
        u_hi1 = over("u_hi1", [P, DC, T], "big", 28)
        u_hi2 = over("u_hi2", [P, DC, T], "wk")
        w_lo = over("w_lo", [P, RING, SLAB], "ring")
        w_hi = over("w_hi", [P, 2, SLAB], "S")
        big_r = over("big_r", [P, 32, T], "big")
        posi = big[:, 24, :].bitcast(I32)
        sqa = wk[:, 3, :]
        tmpf = tmp[:, :, :].rearrange("p a b -> p (a b)")

        cst2 = ada_in[:, :, :].rearrange("p a b -> p (a b)")

        LP = [ctx.enter_context(nc.psum_tensor(f"LP{i}", [P, 2, T], F32)) for i in range(2)]
        XB = [ctx.enter_context(nc.psum_tensor(f"XB{i}", [P, T], F32)) for i in range(4)]
        LPF = [t[:, :, :].rearrange("p a b -> p (a b)") for t in LP]

        rts, rstds = [rt[:, :], cst2[:, NCONST2:NCONST2 + T]], [rstd[:, :], cst2[:, NCONST2 + T:NCONST2 + 2 * T]]

        def cc(name, a=0, n=None):
            t, (o, wd) = (cst, COFF[name]) if name in COFF else (cst2, COFF2[name])
            return t[:, o + a:o + (wd if n is None else a + n)]

        def gate_row(rows, i):
            return tmpf[rows, i * T:(i + 1) * T] if i < 4 else tabs[rows, i - 2, :]

        def ones_row(rows, n=T):
            return cc("ones", 0, 1)[rows, :].to_broadcast([rows.stop - rows.start, n])

        def sp_(name, a=0, n=1):
            return sm[:, SOFF[name][0] + a:SOFF[name][0] + a + n]

        def blk(b):
            return slice(b * P, (b + 1) * P)

        def half(i):
            return slice(64 * (i % 2), 64 * (i % 2) + 64)

        def vals(c0, width):
            n = NB * width // T
            return big[:, c0:c0 + n, :].rearrange("p a b -> p (a b)").rearrange("p (t c) -> p t c", c=width)

        fv, dv = vals(FV, T), vals(DV, T)
        mv = [vals(MV + 2 * i, 256) for i in range(3)] + [tmpf[:, 0:1024].rearrange("p (t c) -> p t c", c=256)]
        xv, av, hv = vals(XV, 256), vals(AV, T), vals(HV, 256)

        def ffn_order(up, down, ada):
            return [(up + "a", FC // 2, DC * 256, ada, 1), (down + "a", DC, FC // 2 * P, 0, 1),
                    (up + "b", FC // 2, DC * 256, ada, 1), (down + "b", DC, FC // 2 * P, 0, 1)]

        ORDER = ffn_order("gu00", "dn00", 1)
        ORDER += [("hyb", 10, DC * 256, 0, 1), ("hybv", 4, DC * 256, 0, 1), ("hybo", 4, DC * 256, 0, 0)]
        ORDER += ffn_order("gu01", "dn01", 1) + ffn_order("gu10", "dn10", 1)
        ORDER += [("mlad", 3, DC * 256, 0, 1), ("mlaq", 6, 3 * 256, 0, 0), ("mlak", 4, 2 * 256, 0, 0),
                  ("mlav", 4, 2 * 256, 0, 0), ("mlao", 4, DC * 256, 0, 0)]
        ORDER += ffn_order("gu11", "dn11", 0)
        for l in range(DEPTH):
            ORDER += [(f"in{l}", 11, DC * 256, 0, 1), (f"inv{l}", 4, DC * 256, 0, 1), (f"wo{l}", 4, DC * 256, 0, 0)]
            for part in "ab":
                ORDER += [(f"up{l}{part}", 8, DC * 256, 0, 1), (f"down{l}{part}", DC, 16 * P, 0, 1)]
        WIDTH = {name: (n, width, ada) for name, n, width, ada, _ in ORDER}
        CUT = {name for name, _, _, _, two in ORDER if two}
        CUT_SLABS, slabs = [], 0
        for name, n, width, _, two in ORDER:
            CUT_SLABS += [(slabs + k, width) for k in range(n if two else 0)]
            slabs += n

        def beside(pl, name):
            n, _, ada = WIDTH[name]
            return min(n, N_ADA - (UP0 + 1) - pl.ada) if ada else 0

        def first_ada(eng, a):
            if a < RING:
                eng.wait_ge(s(f"ada_ring{a}"), 16)
                return ring[:, a, :]
            eng.wait_ge(s(f"ada_in{a % 2}"), 16 * (a // 2 - 1))
            return ada_in[:, a % 2, :]

        block = ctx.enter_context(nc.Block())

        @block.sync
        def _(sp):
            pl = Place(sp, s)
            for dst, src in ((sm[:, :], small), (cst[:, :], consts), (posi, pos), (modb[:, :], adab)):
                sp.dma_start(dst, src).then_inc(s("const_in"), 16)

            def load_ada(a, it):
                if a < RING:
                    sp.dma_start(ring[:, a, 0:DC * 256], w["ada"][a]).then_inc(s(f"ada_ring{a}"), 16)
                    return
                if a >= RING + 2:
                    sp.wait_ge(s("ada_summed"), at(a - 1, it, RING))
                src = w["ada"][a] if isinstance(it, int) else w["ada"][it * RING + a]
                sp.dma_start(ada_in[:, a % 2, :], src).then_inc(s(f"ada_in{a % 2}"), 16)

            for a in range(UP0 - 2):
                load_ada(a, 0)
                if a == RING + 1:
                    sp.dma_start(h[:, :, :], x).then_inc(s("x_in"), 16)
            consts2_at = "gu11a"
            for name, n, width, _, _ in ORDER:
                n_ada = beside(pl, name)
                if name == consts2_at:
                    sp.wait_ge(s("ada_summed"), N_ADA)
                    sp.dma_start(cst2[:, 0:NCONST2], consts2).then_inc(s("const2_in"), 16)

                def load(k, it):
                    slab = pl.slab + k
                    if slab >= RING:
                        sp.wait_ge(s("lin_done"), at(slab - RING + 1, it, RING))
                    else:
                        sp.wait_ge(s("ada_summed"), slab + 1)
                    src = w[name][k] if isinstance(it, int) else w[name][it * RING + k]
                    sp.dma_start(ring[:, slab % RING, 0:width], src).then_inc(s(f"w_in{slab % RING}"), 16)
                    if slab == 0:
                        for a in range(UP0 - 2, UP0 + 1):
                            load_ada(a, 0)
                    if n_ada == n or k < n_ada:
                        load_ada(UP0 + 1 + pl.ada + k, it)

                slab_loop(sp, n, load, peel=4 if pl.slab == 0 else n_ada if 0 < n_ada < n else None)
                pl.slab += n
                pl.ada += n_ada
            sp.wait_ge(s("lin_taken0"), GROUPS // 2 + GROUPS % 2)
            sp.wait_ge(s("lin_taken1"), GROUPS // 2)
            sp.dma_start(out, h[:, :, :]).then_inc(s("out_stored"), 16)
            sp.wait_ge(s("out_stored"), 16)

        @block.tensor
        def _(pe):
            pl = Place(pe, s)

            def mm(o, lhsT, rhs, start=True, stop=True):
                return pe.matmul(o, lhsT=lhsT, rhs=rhs, start=start, stop=stop)

            def ada_sum(a, it):
                pe.wait_ge(s("ada_summed"), at(a + 1, it, RING))
                for f in range(2):
                    last = mm(XB[3][:, f:f + 1], ada_acc[:, f * P:(f + 1) * P], cc("ones", 0, 1))
                last.then_inc(s("ada_col"), 1)

            def linear(name, kind, src, after=None):
                n, width, _ = WIDTH[name]
                n_ada = beside(pl, name)
                cut = name in CUT

                def products(o, c, n_c, a, b):
                    passes = ((a[0], b[0]), (a[0], b[1]), (a[1], b[0])) if cut else ((a, b),)
                    for i, (x_, y_) in enumerate(passes):
                        last = mm(o, x_, y_, start=c == 0 and i == 0, stop=c == n_c - 1 and i == len(passes) - 1)
                    return last

                def body(k, it):
                    slab, group = pl.slab + k, pl.group + k
                    slot, p = slab % RING, group % 2
                    if group >= 2:
                        pe.wait_ge(s(f"lin_taken{p}"), at(group // 2, it, RING // 2))
                    if cut:
                        pe.wait_ge(s("w_cut"), at(pl.cut + k + 1, it, RING))
                        high, rest = w_hi[:, (pl.cut + k) % 2, 0:width], w_lo[:, slot, 0:width]
                    else:
                        pe.wait_ge(s(f"w_in{slot}"), at(16 * (slab // RING + 1), it, 16))
                    r = ring[:, slot, 0:width]

                    def weights(cols):
                        return (high[:, cols], rest[:, cols]) if cut else r[:, cols]

                    def tokens_of(c, b):
                        return tuple(x_[:, blk(b)] for x_ in src(c)) if cut else src(c)[:, blk(b)]

                    if kind == "down":
                        for c in range(width // P):
                            last = products(LP[p][:, 0, :], c, width // P, weights(blk(c)), src(c))
                    elif kind == "fm":
                        for c in range(width // 256):
                            for f in range(2):
                                last = products(LP[p][:, f, :], c, width // 256,
                                                weights(slice(c * 256 + f * P, c * 256 + f * P + P)), src(c))
                    else:
                        for b in range(NB):
                            for c in range(width // 256):
                                last = products(LPF[p][:, b * 256:(b + 1) * 256], c, width // 256,
                                                tokens_of(c, b), weights(slice(c * 256, (c + 1) * 256)))
                    last.then_inc(s("lin_done"), 1)
                    if after:
                        after(k)
                    if n_ada == n or k < n_ada:
                        ada_sum(UP0 + pl.ada + k, it)

                slab_loop(pe, n, body, peel=4 if pl.slab == 0 else n_ada if 0 < n_ada < n else None)
                pl.slab += n
                pl.group += n
                pl.ada += n_ada
                pl.cut += n if cut else 0

            def square_sum(n, weights):
                if pl.norm:
                    pe.wait_ge(s("rt_ready"), pl.norm)
                for c in range(n):
                    pe.wait_ge(s("sq_ready"), pl.sq + c + 1)
                    mm(XB[0][:, :], weights, sq[:, c % 2, :], start=c == 0, stop=c == n - 1)\
                        .then_inc(s("sq_used"), 1)
                pl.sq += n
                pl.norm += 1

            def square_sums(n, weights):
                for i in range(n) if isinstance(n, int) else n:
                    pe.wait_ge(s("rt_ready"), pl.norm - (i > 0))
                    pe.wait_ge(s("sq_ready"), pl.sq + 1)
                    mm(XB[i % 2][:, :], weights, sq[:, i % 2, :]).then_inc(s("sq_used"), 1)
                    pl.sq += 1
                    pl.norm += 1

            def total_sum():
                if pl.norm:
                    pe.wait_ge(s("rt_ready"), pl.norm)
                pl.got("squares_summed")
                mm(XB[0][:, :], cc("ones"), sqa, stop=False)
                pl.got("h_squared", DC)
                mm(XB[0][:, :], cc("ones"), sq[:, (DC - 1) % 2, :], start=False).then_inc(s("total_ready"), 1)
                pl.norm += 1

            def norm(high):
                total_sum()
                first = pl.ur
                pl.ur += DC
                used = set()

                def src(c):
                    if c not in used:
                        used.add(c)
                        pe.wait_ge(s("u_ready"), first + c + 1)
                    return high[:, c, :], u_lo[:, c, :]
                return src

            def hidden_src(n, per=1):
                first, high, low = pl.low, big_r[:, 0:n, :], big_r[:, n:2 * n, :]
                pl.low += n // per
                used = set()

                def src(c):
                    if c // per not in used:
                        used.add(c // per)
                        pe.wait_ge(s("h_cut"), first + c // per + 1)
                    return high[:, c, :], low[:, c, :]
                return src

            def ffn(up, down):
                src = norm(u_hi1)
                linear(up + "a", "fm", src)
                linear(down + "a", "down", hidden_src(FC // 2))
                linear(up + "b", "fm", src)
                if up == "gu10":
                    ada_sum(N_ADA - 1, 0)
                linear(down + "b", "down", hidden_src(FC // 2))

            def rotate(chunks, weights, ready=None):
                for i, c in enumerate(chunks):
                    if ready:
                        pl.got(ready)
                    if pl.rope + i >= 2:
                        pe.wait_ge(s("rope_done"), pl.rope + i - 1)
                    mm(XB[1 + (pl.rope + i) % 2][:, :], weights, big[:, c, :]).then_inc(s("rot_done"), 1)
                pl.rope += len(chunks)

            def attention(heads, score, val, hd, maps=1):
                per = P // hd
                n_units = heads * NB
                pl.groups_taken()
                if pl.rope:
                    pe.wait_ge(s("rope_done"), pl.rope)
                u0, p0, h0 = pl.unit, pl.prob, pl.head
                for n in range(n_units + 3):
                    if n < n_units:
                        hh, qb = divmod(n, NB)
                        for m in range(maps):
                            k = u0 + n * maps + m
                            if k >= 2:
                                pe.wait_ge(s("smax_done"), k - 1)
                            score(hh, m, qb, XB[k % 2]).then_inc(s("scores_done"), 1)
                    if 0 <= n - 2 < n_units:
                        i, qb = n - 2, (n - 2) % NB
                        k = p0 + i
                        if k >= 2:
                            pe.wait_ge(s("pt_done"), k - 1)
                        pe.wait_ge(s("probs_done"), k + 1)
                        src = wk[:, 4 + k % 2, :] if maps == 2 else E[:, k % 4, :]
                        for b in range(qb + 1):
                            last = pe.transpose(XB[2 + k % 2][:, blk(b)], src[:, blk(b)], cc("ident"))
                        last.then_inc(s("transposed"), 1)
                    if n >= 3:
                        i = n - 3
                        hh, qb = divmod(i, NB)
                        k, g = p0 + i, h0 + hh // per
                        if i % (per * NB) == 0 and g >= 2:
                            pe.wait_ge(s("o_taken"), g - 1)
                        pe.wait_ge(s("pt_done"), k + 1)
                        o = LP[0][half(hh) if per == 2 else slice(0, P), g % 2, blk(qb)]
                        for b in range(qb + 1):
                            last = mm(o, val(hh, b), ET[:, k % 2, blk(b)], start=b == 0, stop=b == qb)
                        last.then_inc(s("pv_done"), 1)
                pl.unit += n_units * maps
                pl.prob += n_units
                pl.head += heads // per

            pe.wait_ge(s("const_in"), 64)
            pe.wait_ge(s("cond_ready"), 1)
            for a in range(0, UP0, 2):
                wa = first_ada(pe, a)
                if a:
                    pe.wait_ge(s("ada_done"), a)
                for f in range(2):
                    for c in range(DC):
                        mm(XB[3][:, f:f + 1], wa[:, c * 256 + f * P:c * 256 + f * P + P],
                           csil[:, c:c + 1], start=c == 0, stop=c == DC - 1)
                pl.got("ada_acc")
                for f in range(2):
                    last = mm(XB[3][:, 2 + f:3 + f], ada_acc[:, f * P:(f + 1) * P], cc("ones", 0, 1))
                last.then_inc(s("ada_summed"), 2)
            ffn("gu00", "dn00")

            src = norm(u_hi1)
            linear("hyb", "fm", src)
            linear("hybv", "tm", src)
            rotate(list(range(DQ, DQ + 8)) + [IQ, IQ + 1, IK], cc("rot16"))
            for b in range(NB):
                last = mm(XB[3][:, 4 * b:4 * b + 4], big[32:36, GT, blk(b)], cc("ident")[32:36, 32:36])
            last.then_inc(s("iw_raw"), 1)

            def fox_score(hh, _, qb, bank):
                W = (qb + 1) * P
                r, o = half(hh), bank[:, 0:(qb + 1) * P]
                mm(o, big[r, FQ + hh // 2, blk(qb)], big[r, FK + hh // 2, 0:W], stop=False)
                one = cc("ident")[0:8, hh:hh + 1]
                mm(o, gate_row(slice(0, 8), 3)[:, blk(qb)], one.to_broadcast([8, W]), start=False, stop=False)
                return mm(o, one.to_broadcast([8, P]), gate_row(slice(0, 8), 0)[:, 0:W], start=False)

            pl.groups_taken()
            pe.wait_ge(s("rope_done"), pl.rope)
            for n in range(3 * IDX_H):
                qb, i = n // IDX_H + 1, n % IDX_H
                if n >= 2:
                    pe.wait_ge(s("idx_relu"), n - 1)
                mm(XB[n % 2][:, 0:(qb + 1) * P], big[half(i), IQ + i // 2, blk(qb)],
                   big[half(i), IK, 0:(qb + 1) * P]).then_inc(s("idx_done"), 1)
            pe.wait_ge(s("idx_relu"), 3 * IDX_H)

            pl.got("cum_ready")
            attention(FOX_H, fox_score, lambda hh, b: fv[:, b, 64 * hh:64 * hh + 64], 64)

            def dsa_score(hh, _, qb, bank):
                r = half(hh)
                return mm(bank[:, 0:(qb + 1) * P], big[r, DQ + hh // 2, blk(qb)],
                          big[r, DK + hh // 2, 0:(qb + 1) * P])

            attention(DSA_H, dsa_score, lambda hh, b: dv[:, b, 64 * hh:64 * hh + 64], 64)
            pe.wait_ge(s("o_taken"), pl.head)
            linear("hybo", "fm", lambda c: u[:, c, :])
            ffn("gu01", "dn01")

            ffn("gu10", "dn10")
            linear("mlad", "fm", norm(u_hi1))
            square_sum(3, cc("ones"))
            square_sum(2, cc("ones"))
            pl.got("latent_ready", 2)
            linear("mlaq", "fm", lambda c: big[:, CQ + c, :])
            linear("mlak", "fm", lambda c: big[:, CKV + c, :])
            linear("mlav", "tm", lambda c: big[:, CKV + c, :])
            rotate([KR] + list(range(QR, QR + 4)), cc("rot64"))

            def mla_score(hh, _, qb, bank):
                W = (qb + 1) * P
                mm(bank[:, 0:W], big[:, QN + hh, blk(qb)], big[:, KN + hh, 0:W], stop=False)
                return mm(bank[:, 0:W], big[half(hh), QR + hh // 2, blk(qb)], big[half(hh), KR, 0:W],
                          start=False)

            attention(MLA_H, mla_score, lambda hh, b: mv[hh // 2][:, b, blk(hh % 2)], P)
            pe.wait_ge(s("o_taken"), pl.head)
            linear("mlao", "fm", lambda c: u[:, c, :])
            ffn("gu11", "dn11")

            pe.wait_ge(s("const2_in"), 16)
            total_sum()
            for l in range(DEPTH):
                src = norm(u_hi2)
                linear(f"in{l}", "fm", src)
                linear(f"inv{l}", "tm", src,
                       after=lambda k: square_sums(range(2 * k, 2 * k + 2), cc("blk64")))
                pe.wait_ge(s("rt_ready"), pl.norm)
                rotate(range(AQ, AQ + 8), cc("rot16"), "qk_normed")

                def diff_score(hh, m, qb, bank):
                    return mm(bank[:, 0:(qb + 1) * P], big[half(m), AQ + hh, blk(qb)],
                              big[half(m), AK + hh, 0:(qb + 1) * P])

                attention(DIFF_H, diff_score, lambda hh, b: av[:, b, blk(hh)], P, maps=2)
                square_sums(DIFF_H, cc("ones"))

                pe.wait_ge(s("rt_ready"), pl.norm)
                pl.got("gates_rows")
                for b in range(NB):
                    last = mm(XB[3][:, 4 * b:4 * b + 4], gate_row(slice(0, 4), 3)[:, blk(b)], cc("ident")[0:4, 0:4])
                last.then_inc(s("a_cols"), 1)
                pl.got("conv_silu", 4)
                u0 = l * 4 * NB

                def weighted(n):
                    hh, b = divmod(n, NB)
                    pe.wait_ge(s("ms_ready"), u0 + n + 1)
                    o = (half(hh), hh // 2, slice(b * P, T))
                    mm(LP[0][o], xv[:, b, 64 * hh:64 * hh + 64], S[:, n % 2, 0:T - b * P],
                       start=b == 0, stop=b == NB - 1)
                    mm(LP[1][o], cc("ones", 0, 64), S[:, n % 2, 0:T - b * P],
                       start=b == 0, stop=b == NB - 1).then_inc(s("m_out"), 1)

                for n in range(4 * NB + 1):
                    hh, b = divmod(n, NB)
                    if n < 4 * NB:
                        if b == 0:
                            if l * 4 + hh:
                                pe.wait_ge(s("g_taken"), l * 4 + hh)
                            mm(XB[0][:, :], cc("ident")[0:4, hh:hh + 1].to_broadcast([4, P]),
                               gate_row(slice(0, 4), 5)).then_inc(s("g_ready"), 1)
                        if u0 + n >= 2:
                            pe.wait_ge(s("ms_ready"), u0 + n - 1)
                        mm(XB[1 + n % 2][:, 0:T - b * P], big[half(hh), XK + hh // 2, blk(b)],
                           big[half(hh), XQ + hh // 2, b * P:T]).then_inc(s("mqk_done"), 1)
                    if n:
                        weighted(n - 1)
                pl.got("em_rows")
                for cp in range(2):
                    if cp:
                        pl.got("em_taken")
                    mm(XB[3][:, :], cc("sel4", cp * P, P)[0:4, :], gate_row(slice(0, 4), 1)).then_inc(s("em_ready"), 1)
                    square_sum(1, cc("blk64"))
                pl.got("em_taken")

                for cp in range(2):
                    for step in range(10):
                        pl.got("z_ready")
                        for j in range(2):
                            k = (l * 2 + cp) * 20 + 2 * step + j
                            r = half(j)
                            if k >= 4:
                                pe.wait_ge(s("level_taken"), k - 3)
                            bank, z = XB[k % 4], E[r, step % 2, :]
                            if step == 0:
                                for b in range(NB):
                                    last = mm(bank[:, blk(b)], big[r, SP + cp, blk(b)], big[r, HQ + cp, blk(b)])
                            elif step < 8:
                                for b in range(NB):
                                    last = mm(bank[:, blk(b)], z[:, blk(b)], z[:, blk(b)])
                            elif step == 8:
                                for i, b in enumerate((0, 2)):
                                    last = mm(bank[:, blk(i)], z[:, blk(b)], z[:, blk(b + 1)])
                            else:
                                for b in range(2):
                                    last = mm(bank[:, b * 256:b * 256 + 256], z[:, blk(b)], z[:, 256:T])
                            last.then_inc(s("level_mm"), 1)
                    pl.got("a_done")
                    for j in range(2):
                        for b in range(NB):
                            v = hv[:, b, 64 * (2 * cp + j):64 * (2 * cp + j) + 64]
                            last = mm(LP[0][half(j), cp, blk(b)], v, wk[:, 2 + j, blk(b)],
                                      start=b == 0, stop=b == NB - 1)
                            if b < NB - 1:
                                o = (0, 384, 640)[b]
                                mm(LP[0][half(j), cp, (b + 1) * P:T], v,
                                   tmp[:, j, o:o + (NB - 1 - b) * P], start=False, stop=False)
                    last.then_inc(s("h_out"), 1)
                    square_sum(1, cc("blk64"))
                pl.got("mix_ready")
                linear(f"wo{l}", "fm", lambda c: u[:, c, :])
                src = norm(u_hi2)
                for part in "ab":
                    linear(f"up{l}{part}", "fm", src)
                    linear(f"down{l}{part}", "down", hidden_src(16, 2))

        @block.scalar
        def _(act):
            pl = Place(act, s)

            def f(o, i, fn, **kw):
                return act.activation(o, i, fn, **kw)

            def rms(srcs, size):
                for c, src in enumerate(srcs):
                    if pl.sq + c >= 2:
                        act.wait_ge(s("sq_used"), pl.sq + c - 1)
                    f(sq[:, c % 2, :], src, ACT.Square).then_inc(s("sq_ready"), 1)
                pl.sq += len(srcs)
                act.wait_ge(s("sq_used"), pl.sq)
                if pl.norm:
                    act.wait_ge(s("rstd_ready"), pl.norm)
                f(rt[:, :], XB[0][:, :], ACT.Sqrt, scale=1.0 / size, bias=cc("eps")).then_inc(s("rt_ready"), 1)
                pl.norm += 1

            def square_one(i, src):
                if pl.sq >= 2:
                    act.wait_ge(s("sq_used"), pl.sq - 1)
                f(sq[:, i % 2, :], src, ACT.Square).then_inc(s("sq_ready"), 1)
                pl.sq += 1

            def root_one(i, used, size):
                act.wait_ge(s("sq_used"), used)
                act.wait_ge(s("rstd_ready"), pl.norm - (i > 0))
                f(rts[i % 2], XB[i % 2][:, :], ACT.Sqrt, scale=1.0 / size, bias=cc("eps"))\
                    .then_inc(s("rt_ready"), 1)
                pl.norm += 1

            def rms_each(srcs, size):
                n, sq0 = len(srcs), pl.sq
                for i in range(n + 1):
                    if i < n:
                        square_one(i, srcs[i])
                    if i:
                        root_one(i - 1, sq0 + i, size)

            def high(q, it=0):
                slab, width = CUT_SLABS[q]
                slot = slab % RING
                act.wait_ge(s(f"w_in{slot}"), at(16 * (slab // RING + 1), it, 16))
                if q >= 2:
                    act.wait_ge(s("lin_done"), at(CUT_SLABS[q - 2][0] + 1, it, RING))
                f(w_hi[:, q % 2, 0:width], ring[:, slot, 0:width], ACT.Copy).then_inc(s("w_high"), 1)

            def layer(name, take=None, last=False):
                n = WIDTH[name][0]

                def body(k, it):
                    if take:
                        take(k, it)
                    high(pl.cut + k + 2, it)

                slab_loop(act, n - 2, body)
                for k in (n - 2, n - 1):
                    if take:
                        take(k, 0)
                    if not last:
                        high(pl.cut + k + 2)
                pl.slab += n
                pl.group += n
                pl.cut += n

            def high_input(dst, shift=None):
                for c in range(DC + 1):
                    if c < DC:
                        act.wait_ge(s("u_scaled"), pl.tu + c + 1)
                        if shift is not None:
                            f(u[:, c, :], u[:, c, :], ACT.Identity, bias=mod[:, shift + c:shift + c + 1])\
                                .then_inc(s("u_shifted"), 1)
                    if c:
                        if shift is not None:
                            pl.got("u_shifted")
                        f(dst[:, c - 1, :], u[:, c - 1, :], ACT.Copy).then_inc(s("u_high"), 1)
                pl.tu += DC

            def hrms(per=1, cut_at=(7,), normed=False):
                if pl.norm:
                    act.wait_ge(s("total_ready"), pl.seen.get("total_ready", 0))
                for c in range(DC):
                    for j, chunk in enumerate(cut_at):
                        if chunk == c:
                            high(pl.cut + j)
                    if normed:
                        act.wait_ge(s("u_scaled"), pl.tu - DC + c + 1)
                    else:
                        pl.chunk_final(c, per)
                    if c >= 3:
                        act.wait_ge(s("sq_added"), pl.seen.get("sq_added", 0) + c - 2)
                    f(sq[:, c % 2, :] if c else sqa, h[:, c, :], ACT.Square).then_inc(s("h_squared"), 1)
                pl.passed("sq_added", DC - 2)
                pl.got("total_ready")
                if pl.norm:
                    act.wait_ge(s("rstd_ready"), pl.norm)
                f(rt[:, :], XB[0][:, :], ACT.Sqrt, scale=1.0 / D, bias=cc("eps")).then_inc(s("rt_ready"), 1)
                pl.norm += 1

            def skip(name):
                n = WIDTH[name][0]
                pl.slab += n
                pl.group += n

            def ffn(l, j, up, down, per=1):
                cut_at = (4, 6) if per == 2 else (7,)
                hrms(per, cut_at)
                high_input(u_hi1, (l * N_MOD + 3 * j) * DC)
                for q in range(len(cut_at), 2):
                    high(pl.cut + q)

                for part in "ab":
                    g0, s0 = pl.group, pl.slab

                    def silu(k, it):
                        act.wait_ge(s("lin_done"), at(s0 + k + 1, it, RING))
                        p = (g0 + k) % 2
                        f(tmp[:, p, 0:T], LP[p][:, 0, :], ACT.Silu).then_inc(s("silu_done"), 1)

                    layer(up + part, silu)
                    pl.low += FC // 2
                    if up + part == "gu11a":
                        pl.got("lb_shifted")
                        f(st[:, 22:26], st[:, 18:22], ACT.Exp).then_inc(s("lb_exp"), 1)
                        pl.got("lam_dots")
                        f(st[:, 46:50], st[:, 42:46], ACT.Exp).then_inc(s("lam_exp"), 1)
                    layer(down + part, last=part == "b")

            def attention(heads, scale, hd, maps=1):
                n_units = heads * NB
                u0, p0 = pl.unit, pl.prob
                for n in range(n_units + 2):
                    if n < n_units:
                        W = (n % NB + 1) * P
                        for m in range(maps):
                            k = u0 + n * maps + m
                            act.wait_ge(s("smax_done"), k + 1)
                            if maps == 2:
                                if p0 + n >= 2:
                                    act.wait_ge(s("probs_done"), p0 + n - 1)
                            elif p0 + n >= 4:
                                act.wait_ge(s("transposed"), p0 + n - 3)
                            e = (2 * (p0 + n) + m) % 4 if maps == 2 else (p0 + n) % 4
                            f(E[:, e, 0:W], S[:, k % 2, 0:W], ACT.Exp, scale=scale, bias=stat[:, k % 4, 0:1],
                              accum_out=stat[:, k % 4, 1:2]).then_inc(s("exp_done"), 1)
                    if n >= 2:
                        k = p0 + n - 2
                        W = ((n - 2) % NB + 1) * P
                        act.wait_ge(s("transposed"), k + 1)
                        if k >= 2:
                            act.wait_ge(s("pv_done"), k - 1)
                        f(ET[:, k % 2, 0:W], XB[2 + k % 2][:, 0:W], ACT.Copy).then_inc(s("pt_done"), 1)
                pl.unit += n_units * maps
                pl.prob += n_units

            act.wait_ge(s("const_in"), 64)
            f(csil[:, :], sp_("cond", 0, DC), ACT.Silu).then_inc(s("cond_ready"), 1)
            for i in range(4):
                pl.got("ang_ready")
                f(tabs[:, i, :], wk[:, 4 + i % 2, :], ACT.Sin).then_inc(s("tab_ready"), 1)
            act.wait_ge(s("x_in"), 16)
            ffn(0, 0, "gu00", "dn00")

            hrms()
            high_input(u_hi1, (3 * 1) * DC)
            high(pl.cut + 1)
            layer("hyb")
            layer("hybv", last=True)

            def log_sigmoid_parts(row):
                pl.got("gate_abs")
                r = slice(0, row)
                f(gate_row(r, 2), gate_row(r, 2), ACT.Exp, scale=-1.0).then_inc(s("scalar_chain"), 1)
                pl.got("scalar_chain")
                f(gate_row(r, 2), gate_row(r, 2), ACT.Ln, bias=1.0).then_inc(s("gate_ln"), 1)

            log_sigmoid_parts(8)
            for n in range(3 * IDX_H):
                act.wait_ge(s("idx_done"), n + 1)
                if n >= 2:
                    act.wait_ge(s("idx_used"), n - 1)
                W = (n // IDX_H + 2) * P
                f(S[:, n % 2, 0:W], XB[n % 2][:, 0:W], ACT.Relu, scale=0.125).then_inc(s("idx_relu"), 1)
            attention(FOX_H, 0.125, 64)
            attention(DSA_H, 0.125, 64)
            skip("hybo")
            ffn(0, 2, "gu01", "dn01", 2)

            ffn(1, 0, "gu10", "dn10")
            hrms()
            high_input(u_hi1, (N_MOD + 3 * 1) * DC)
            high(pl.cut + 1)
            layer("mlad", last=True)
            pl.groups_taken()
            rms([big[:, CQ + c, :] for c in range(3)], 384)
            rms([big[:, CKV + c, :] for c in range(2)], 256)
            skip("mlaq")
            skip("mlak")
            skip("mlav")
            attention(MLA_H, 192.0 ** -0.5, P)
            skip("mlao")
            ffn(1, 2, "gu11", "dn11", 2)

            hrms()
            pl.tu += DC
            for l in range(DEPTH):
                if l:
                    hrms()
                else:
                    hrms(cut_at=(), normed=True)
                high_input(u_hi2)
                high(pl.cut + 1)
                layer(f"in{l}")
                log_sigmoid_parts(4)
                pl.groups_taken()
                sq0 = pl.sq
                for i in range(2):
                    square_one(i, big[:, AQ + i, :])

                def roots_and_conv(k):
                    for i in (2 * k, 2 * k + 1):
                        root_one(i, sq0 + i + 1, 64)
                    pl.got("conv_raw")
                    f(big[:, XQ + k, :], big[:, SP + k % 2, :], ACT.Silu).then_inc(s("conv_silu"), 1)

                def beside_values(k, it):
                    if k:
                        roots_and_conv(k - 1)
                        for i in (2 * k, 2 * k + 1):
                            square_one(i, big[:, AQ + i, :])

                layer(f"inv{l}", beside_values, last=True)
                roots_and_conv(3)
                attention(DIFF_H, 0.125, P, maps=2)
                act.wait_ge(s("o_taken"), 4 + 4 + 8 + 4 * (l + 1))
                rms_each([u[:, 2 + c, :] for c in range(DIFF_H)], P)

                for c in range(2):
                    f(big[:, XO + c, :], big[:, XO + c, :], ACT.Sigmoid).then_inc(s("o_sigmoid"), 1)
                pl.got("em_log")
                f(gate_row(slice(0, 4), 1), gate_row(slice(0, 4), 1), ACT.Exp, scale=-1.0).then_inc(s("em_rows"), 1)
                for n in range(4 * NB):
                    hh, b = divmod(n, NB)
                    pl.got("g_diag")
                    bias = tokw[:, 4 * b + hh:4 * b + hh + 1]
                    last = f(E[:, n % 4, 0:P], wk[:, 2 + n % 2, 0:P], ACT.Exp, bias=bias)
                    if b < NB - 1:
                        last = f(E[:, n % 4, P:T - b * P], wk[:, hh % 2, (b + 1) * P:T], ACT.Exp, bias=bias)
                    last.then_inc(s("me_done"), 1)
                for cp in range(2):
                    pl.got("m_mix")
                    rms([u[:, cp, :]], 64)

                for cp in range(2):
                    f(big[:, HQ + cp, :], big[:, HQ + cp, :], ACT.Silu)
                    f(big[:, HG + cp, :], big[:, HG + cp, :], ACT.Silu)
                    f(wk[:, 4, :], big[:, HF + cp, :], ACT.Sigmoid, scale=-1.0).then_inc(s("scalar_chain"), 1)
                    pl.got("scalar_chain")
                    f(big[:, HF + cp, :], big[:, HF + cp, :], ACT.Sigmoid).then_inc(s("h_sig"), 1)
                    pl.got("h_f")
                    f(big[:, HF + cp, :], big[:, HF + cp, :], ACT.Ln).then_inc(s("h_lnf"), 1)
                    for step in range(1, 10):
                        pl.got("x_ready")
                        k = (l * 2 + cp) * 10 + step
                        act.wait_ge(s("z_ready"), k - 1)
                        f(S[:, step % 2, :], wk[:, step % 2, :], ACT.Exp).then_inc(s("ex_ready"), 1)
                    pl.got("h_mix")
                    rms([u[:, 6 + cp, :]], 64)
                skip(f"wo{l}")
                hrms(2, (4, 6))
                high_input(u_hi2)
                for part in "ab":
                    g0, s0, low0 = pl.group, pl.slab, pl.low
                    pl.low += 8

                    def relu(k, it):
                        act.wait_ge(s("lin_done"), at(s0 + k + 1, it, RING))
                        act.wait_ge(s("h_cut"), at(low0 + k - 1, it, RING))
                        p = (g0 + k) % 2
                        f(tmp[:, p, :], LPF[p], ACT.Relu).then_inc(s("silu_done"), 1)

                    layer(f"up{l}{part}", relu)
                    layer(f"down{l}{part}", last=part == "b")

        @block.gpsimd
        def _(gp):
            pl = Place(gp, s)

            def rest(q, it=0):
                slab, width = CUT_SLABS[q]
                gp.wait_ge(s("w_high"), at(q + 1, it, RING))
                gp.tensor_tensor(w_lo[:, slab % RING, 0:width], ring[:, slab % RING, 0:width],
                                 w_hi[:, q % 2, 0:width].bitcast(F32), ALU.subtract).then_inc(s("w_cut"), 1)

            def layer(name, take=None, last=False):
                n = WIDTH[name][0]

                def body(k, it):
                    if take:
                        take(k, it)
                    rest(pl.cut + k + 2, it)

                slab_loop(gp, n - 2, body)
                for k in (n - 2, n - 1):
                    if take:
                        take(k, 0)
                    if not last:
                        rest(pl.cut + k + 2)
                pl.group += n
                pl.cut += n

            def skip(*names):
                pl.group += sum(WIDTH[x_][0] for x_ in names)

            def low_hidden(n, per):
                g0, first = pl.group, pl.low
                pl.low += n // per

                def take(k, it):
                    p = (g0 + k) % 2
                    gp.wait_ge(s("h_high"), at(first + k + 1, it, RING))
                    a = k * per
                    hi, lo = (slice(c, c + per) if isinstance(it, int) else bass.ds(it * per * RING + c, per)
                              for c in (a, n + a))
                    src = tmp[:, p, (2 - per) * T:2 * T].rearrange("p (a b) -> p a b", a=per)
                    gp.tensor_tensor(big_r[:, lo, :], src, big_r[:, hi, :].bitcast(F32), ALU.subtract)\
                        .then_inc(s("h_cut"), 1)
                return take

            def squares(cut_at=(7,)):
                h0 = pl.seen.get("h_squared", 0)
                for c in range(1, DC):
                    if c == DC - 1:
                        gp.nop().then_inc(s("squares_summed"), 1)
                    for j, chunk in enumerate(cut_at):
                        if chunk == c:
                            rest(pl.cut + j)
                    if c == DC - 1:
                        break
                    gp.wait_ge(s("h_squared"), h0 + c + 1)
                    gp.tensor_tensor(sqa, sqa, sq[:, c % 2, :], ALU.add).then_inc(s("sq_added"), 1)
                    pl.got("sq_added")
                pl.passed("h_squared", DC)

            def rest_input(high):
                for c in range(DC):
                    pl.got("u_high")
                    gp.tensor_tensor(u_lo[:, c, :], u[:, c, :], high[:, c, :].bitcast(F32), ALU.subtract)\
                        .then_inc(s("u_ready"), 1)

            def first_input(high, cut_at=(7,)):
                squares(cut_at)
                rest_input(high)
                for q in range(len(cut_at), 2):
                    rest(pl.cut + q)

            def ffn(up, down, cut_at=(7,)):
                first_input(u_hi1, cut_at)
                for part in "ab":
                    layer(up + part, low_hidden(FC // 2, 1))
                    layer(down + part, last=part == "b")

            def turn(chunks, t):
                for i, c in enumerate(chunks):
                    k = pl.rope + i
                    if k >= 2:
                        gp.wait_ge(s("rope_done"), k - 1)
                    gp.wait_ge(s("rot_done"), k + 1)
                    gp.tensor_tensor(S[:, k % 2, :], big[:, c, :], t, ALU.mult).then_inc(s("rope_cos"), 1)
                pl.rope += len(chunks)

            gp.wait_ge(s("const_in"), 64)
            ffn("gu00", "dn00")
            first_input(u_hi1)
            layer("hyb")
            layer("hybv", last=True)
            turn(list(range(DQ, DQ + 8)) + [IQ, IQ + 1, IK], tabs[:, 1, :])
            skip("hybo")
            ffn("gu01", "dn01", (4, 6))
            ffn("gu10", "dn10")
            first_input(u_hi1)
            layer("mlad", last=True)
            skip("mlaq", "mlak", "mlav", "mlao")
            turn([KR] + list(range(QR, QR + 4)), tabs[:, 3, :])
            ffn("gu11", "dn11", (4, 6))
            gp.wait_ge(s("const2_in"), 16)
            squares()
            for l in range(DEPTH):
                squares((7,) if l else ())
                rest_input(u_hi2)
                rest(pl.cut + 1)
                layer(f"in{l}")
                layer(f"inv{l}", last=True)
                turn(range(AQ, AQ + 8), cc("diff_cos"))
                for cp in range(2):
                    pl.got("h_kb")
                    for step in range(10):
                        k = (l * 2 + cp) * 10 + step
                        if step == 0:
                            gp.nop().then_inc(s("z_ready"), 1)
                            continue
                        pl.got("ex_ready")
                        b = 1 << (step - 1)
                        if k >= 2:
                            gp.wait_ge(s("level_mm"), 2 * (k - 1))
                        z, e, kk, q = (t.rearrange("p (j i b) -> p j i b", i=2, b=b) for t in
                                       (E[:, step % 2, :], S[:, step % 2, :], big[:, SP + cp, :], big[:, HQ + cp, :]))
                        gp.tensor_tensor(z[:, :, 0, :], e[:, :, 0, :], kk[:, :, 0, :], ALU.mult)
                        gp.tensor_tensor(z[:, :, 1, :], e[:, :, 1, :], q[:, :, 1, :], ALU.mult)\
                            .then_inc(s("z_ready"), 1)
                skip(f"wo{l}")
                first_input(u_hi2, (4, 6))
                for part in "ab":
                    layer(f"up{l}{part}", low_hidden(16, 2))
                    layer(f"down{l}{part}", last=part == "b")

        @block.vector
        def _(dve):
            pl = Place(dve, s)
            link = Chain(dve, s("vector_chain"))
            tt, ts, stt = dve.tensor_tensor, dve.tensor_scalar, dve.scalar_tensor_tensor

            def ada_acc_(a, it):
                if a < UP0:
                    wv, done = first_ada(dve, a), "ada_acc"
                else:
                    dve.wait_ge(s(f"ada_in{a % 2}"), at(16 * (a // 2 - 1), it, 16 * RING // 2))
                    wv, done = ada_in[:, a % 2, :], "ada_summed"
                link(ts(ada_acc[:, :], wv[:, 0:256], csil[:, 0:1], None, ALU.mult))
                for c in range(1, DC):
                    ins = stt(ada_acc[:, :], wv[:, c * 256:(c + 1) * 256], csil[:, c:c + 1], ada_acc[:, :],
                              ALU.mult, ALU.add)
                    if c < DC - 1:
                        link(ins)
                ins.then_inc(s(done), 1)

            def ada_take(a, it):
                dve.wait_ge(s("ada_col"), at(a + 1 - UP0, it, RING))
                if isinstance(it, int):
                    o, b = mod[:, 2 * a:2 * a + 2], modb[:, 2 * a:2 * a + 2]
                else:
                    o, b = (t[:, bass.ds(it * 2 * RING + 2 * a, 2)] for t in (mod, modb))
                tt(o, XB[3][:, 0:2], b, ALU.add).then_inc(s("ada_done"), 1)

            def take(name, body):
                n = WIDTH[name][0]
                n_ada = beside(pl, name)

                def one(k, it):
                    dve.wait_ge(s("lin_done"), at(pl.slab + k + 1, it, RING))
                    body(k, it, (pl.group + k) % 2)
                    if n_ada == n or k < n_ada:
                        ada_take(UP0 + pl.ada + k, it)
                        a = UP0 + 1 + pl.ada + k
                        if a < N_ADA or not isinstance(it, int):
                            ada_acc_(a, it)

                slab_loop(dve, n, one, chains=[(link, DC - 1)] if n_ada == n else (),
                          peel=4 if pl.slab == 0 else n_ada if 0 < n_ada < n else None)
                pl.slab += n
                pl.group += n
                pl.ada += n_ada

            def dyn(t, k, it, step, n):
                a = step * k
                return slice(a, a + n) if isinstance(it, int) else bass.ds(it * step * RING + a, n)

            def root(i=0):
                dve.wait_ge(s("rt_ready"), pl.norm + 1)
                pl.norm += 1
                dve.reciprocal(rstds[i % 2], rts[i % 2]).then_inc(s("rstd_ready"), 1)
                dve.wait_ge(s("rstd_ready"), pl.norm)

            def scale_in(dst, gains):
                root()
                for c in range(DC):
                    stt(dst[:, c, :], h[:, c, :], gains[:, c:c + 1], rstd[:, :], ALU.mult, ALU.mult)\
                        .then_inc(s("u_scaled"), 1)
                pl.tu += DC

            def mod_vec(l, j):
                return mod[:, (l * N_MOD + j) * DC:(l * N_MOD + j + 1) * DC]

            def ada_ready(n):
                dve.wait_ge(s("ada_done"), n)

            def mod_in(l, j):
                ada_ready(min(N_ADA, ((l * N_MOD + 3 * j + 2) * DC) // 2))
                link(stt(gain[:, :], mod_vec(l, 3 * j + 1), 1.0, sp_("norm_g", (l * 3 + j) * DC, DC),
                         ALU.add, ALU.mult))
                scale_in(u, gain)

            def mod_gate(l, j, weight):
                ada_ready(min(N_ADA, ((l * N_MOD + 3 * j + 3) * DC) // 2))
                link(ts(gate[:, :], mod_vec(l, 3 * j + 2), weight, None, ALU.mult))

            def cut_hidden(k, it, p, first, per, product):
                if first + k >= 2:
                    dve.wait_ge(s("h_cut"), at(first + k - 1, it, RING))
                o = tmp[:, p, (2 - per) * T:2 * T].rearrange("p (a b) -> p a b", a=per)
                product(o).then_inc(s(f"lin_taken{p}"), 1)
                dve.wait_ge(s(f"lin_taken{p}"), at((pl.group + k) // 2 + 1, it, RING // 2))
                ts(big_r[:, dyn(big, k, it, per, per), :], o, 1.0, None, ALU.mult).then_inc(s("h_high"), 1)

            def hidden(k, it, p):
                dve.wait_ge(s("silu_done"), at(pl.silu + k + 1, it, RING))
                cut_hidden(k, it, p, pl.low, 1, lambda o:
                           tt(o, tmp[:, p, 0:T].unsqueeze(1), LP[p][:, 1:2, :], ALU.mult))

            def position_table(i):
                C1 = 6.28125
                C2 = float(np.float32(2 * math.pi - C1).view(np.int32) & ~0xfff and
                           (np.array(2 * math.pi - C1, np.float32).view(np.int32) & np.int32(~0xfff)).view(np.float32))
                C3 = 2 * math.pi - C1 - C2
                MAGIC = 1.5 * 2 ** 23
                if i == 0:
                    link(dve.tensor_copy(wk[:, 0, :], posi))
                for freq, quarter in ((("invf16", 0), ("invf16", 1), ("invf64", 0), ("invf64", 1))[i],):
                    o = 4 + i % 2
                    if i >= 2:
                        dve.wait_ge(s("tab_ready"), i - 1)
                    link(ts(wk[:, 1, :], wk[:, 0, :], cc(freq), None, ALU.mult))
                    link(ts(wk[:, 2, :], wk[:, 1, :], 1 / (2 * math.pi), 0.25 * quarter, ALU.mult, ALU.add))
                    link(ts(wk[:, 2, :], wk[:, 2, :], MAGIC, None, ALU.add))
                    link(ts(wk[:, 2, :], wk[:, 2, :], MAGIC, None, ALU.subtract))
                    link(stt(wk[:, 1, :], wk[:, 2, :], -C1, wk[:, 1, :], ALU.mult, ALU.add))
                    link(stt(wk[:, 1, :], wk[:, 2, :], -C2, wk[:, 1, :], ALU.mult, ALU.add))
                    link(stt(wk[:, 1, :], wk[:, 2, :], -C3, wk[:, 1, :], ALU.mult, ALU.add))
                    link(ts(wk[:, 1, :], wk[:, 1, :], math.pi / 2 * quarter, -3.1415925, ALU.add, ALU.max))
                    ts(wk[:, o, :], wk[:, 1, :], 3.1415925, None, ALU.min).then_inc(s("ang_ready"), 1)
                    dve.wait_ge(s("ang_ready"), i + 1)

            def second_block_constants():
                dve.wait_ge(s("const2_in"), 16)
                lb = sp_("lb", 0, 4)
                link(tt(st[:, 16:18], lb[:, 0:2], lb[:, 2:4], ALU.max))
                for l in range(DEPTH):
                    ins = tt(st[:, 18 + 2 * l:20 + 2 * l], lb[:, 2 * l:2 * l + 2], st[:, 16:18], ALU.subtract)
                ins.then_inc(s("lb_shifted"), 1)
                pl.got("lb_exp")
                link(tt(st[:, 26:28], st[:, 22:24], st[:, 24:26], ALU.add))
                link(dve.reciprocal(st[:, 28:30], st[:, 26:28]))
                for l in range(DEPTH):
                    link(tt(st[:, 30 + 2 * l:32 + 2 * l], st[:, 22 + 2 * l:24 + 2 * l], st[:, 28:30], ALU.mult))
                link(tt(st[:, 34:36], st[:, 30:32], st[:, 30:32], ALU.subtract))
                link(tt(st[:, 36:38], st[:, 30:32], st[:, 32:34], ALU.add))
                link(tt(st[:, 36:38], st[:, 36:38], st[:, 30:32], ALU.subtract))
                link(ts(st[:, 38:42], st[:, 34:38], -1.0, 1.0, ALU.mult, ALU.add))
                for l in range(DEPTH):
                    for i in range(2):
                        a = l * 256 + 128 * i
                        link(dve.tensor_tensor_reduce(
                            out=rt[:, 0:64], in0=cc("lam", a, 64), in1=cc("lam", a + 64, 64), scale=1.0,
                            scalar=0.0, op0=ALU.mult, op1=ALU.add, accum_out=st[:, 42 + 2 * l + i:43 + 2 * l + i]))
                dve.nop().then_inc(s("lam_dots"), 1)
                pl.got("lam_exp")
                for l in range(DEPTH):
                    init = 0.8 - 0.6 * math.exp(-0.3 * l)
                    link(tt(st[:, 50 + l:51 + l], st[:, 47 + 2 * l:48 + 2 * l], st[:, 46 + 2 * l:47 + 2 * l], ALU.subtract))
                    link(ts(st[:, 50 + l:51 + l], st[:, 50 + l:51 + l], -init, None, ALU.add))

            def ffn(l, j, up, down):
                mod_in(l, j)
                if up == "gu00":
                    ada_acc_(UP0, 0)
                def add(k, it, p):
                    at_ = dyn(h, k, it, 1, 1)
                    o, g = h[:, at_, :], gate[:, at_]
                    stt(o, LP[p][:, 0:1, :], g, o, ALU.mult, ALU.add).then_inc(s(f"lin_taken{p}"), 1)

                for part in "ab":
                    take(up + part, hidden)
                    pl.silu += FC // 2
                    pl.low += FC // 2
                    if up + part == "gu10b":
                        ada_take(N_ADA - 1, 0)
                    if up + part == "gu11a":
                        second_block_constants()
                    if part == "a":
                        mod_gate(l, j, 0.5)
                    take(down + part, add)

            def residual(l, j, name):
                mod_gate(l, j, 1.0)

                def add(k, it, p):
                    for i in range(2):
                        c = 2 * k + i
                        ins = stt(h[:, c, :], LP[p][:, i, :], gate[:, c:c + 1], h[:, c, :], ALU.mult, ALU.add)
                    ins.then_inc(s(f"lin_taken{p}"), 1)
                take(name, add)

            def plain(dst0):
                def body(k, it, p):
                    ts(big[:, bass.ds(it * 2 * RING + 2 * k + dst0, 2) if not isinstance(it, int)
                           else slice(dst0 + 2 * k, dst0 + 2 * k + 2), :], LP[p][:, :, :], 1.0, None, ALU.mult)\
                        .then_inc(s(f"lin_taken{p}"), 1)
                return body

            def tokens(dsts):
                def body(k, it, p):
                    ts(dsts[k], LPF[p].rearrange("p (t c) -> p t c", c=256), 1.0, None, ALU.mult)\
                        .then_inc(s(f"lin_taken{p}"), 1)
                return body

            def turn(chunks, t):
                for i, c in enumerate(chunks):
                    k = pl.rope + i
                    dve.wait_ge(s("rot_done"), k + 1)
                    link(tt(wk[:, k % 2, :], t, XB[1 + k % 2][:, :], ALU.mult))
                    dve.wait_ge(s("rope_cos"), k + 1)
                    tt(big[:, c, :], wk[:, k % 2, :], S[:, k % 2, :], ALU.add).then_inc(s("rope_done"), 1)
                pl.rope += len(chunks)
                dve.wait_ge(s("rope_done"), pl.rope)

            def attention(heads, scale, hd, mask, dst, maps=1, lam=None, beside=None):
                per = P // hd
                n_units = heads * NB
                u0, p0, h0 = pl.unit, pl.prob, pl.head

                def out_of(g):
                    dve.wait_ge(s("pv_done"), p0 + (g + 1) * per * NB)
                    dve.tensor_copy(u[:, dst + g, :], LP[0][:, (h0 + g) % 2, :]).then_inc(s("o_taken"), 1)

                for n in range(n_units + 3):
                    if n < n_units:
                        qb = n % NB
                        W = (qb + 1) * P
                        for m in range(maps):
                            k = u0 + n * maps + m
                            dve.wait_ge(s("scores_done"), k + 1)
                            if k >= 2:
                                dve.wait_ge(s("exp_done"), k - 1)
                            link(dve.tensor_tensor_reduce(
                                out=S[:, k % 2, 0:W], in0=XB[k % 2][:, 0:W], in1=mask(qb, W), scale=1.0,
                                scalar=LOWEST, op0=ALU.add, op1=ALU.max, accum_out=stat[:, k % 4, 2:3]))
                            ts(stat[:, k % 4, 0:1], stat[:, k % 4, 2:3], -scale, None, ALU.mult)\
                                .then_inc(s("smax_done"), 1)
                    if 1 <= n <= n_units:
                        i = n - 1
                        W = (i % NB + 1) * P
                        k = p0 + i
                        for m in range(maps):
                            q = u0 + i * maps + m
                            dve.wait_ge(s("exp_done"), q + 1)
                            link(dve.reciprocal(stat[:, q % 4, 3:4], stat[:, q % 4, 1:2]))
                        if maps == 1:
                            ts(E[:, k % 4, 0:W], E[:, k % 4, 0:W], stat[:, q % 4, 3:4], None, ALU.mult)\
                                .then_inc(s("probs_done"), 1)
                        else:
                            q0 = u0 + 2 * i
                            link(ts(stat[:, q % 4, 3:4], stat[:, q % 4, 3:4], lam, None, ALU.mult))
                            link(ts(wk[:, 3, 0:W], E[:, 2 * k % 4, 0:W], stat[:, q0 % 4, 3:4], None, ALU.mult))
                            if k >= 2:
                                dve.wait_ge(s("transposed"), k - 1)
                            stt(wk[:, 4 + k % 2, 0:W], E[:, (2 * k + 1) % 4, 0:W], stat[:, q % 4, 3:4],
                                wk[:, 3, 0:W], ALU.mult, ALU.add).then_inc(s("probs_done"), 1)
                    if beside and n < n_units:
                        beside(n)
                    if n >= 3 and (n - 2) % (per * NB) == 0:
                        out_of((n - 2) // (per * NB) - 1)
                pl.unit += n_units * maps
                pl.prob += n_units
                pl.head += heads // per

            def log_sigmoid(src, rows, bias):
                link(ts(gate_row(rows, 0), src, bias, None, ALU.add))
                link(ts(gate_row(rows, 1), gate_row(rows, 0), 0.0, None, ALU.min))
                stt(gate_row(rows, 2), gate_row(rows, 0), -1.0, gate_row(rows, 0), ALU.mult, ALU.max).then_inc(s("gate_abs"), 1)
                pl.got("gate_ln")
                link(tt(gate_row(rows, 0), gate_row(rows, 1), gate_row(rows, 2), ALU.subtract))

            dve.wait_ge(s("const_in"), 64)
            dve.wait_ge(s("cond_ready"), 1)
            for a in range(0, UP0, 2):
                ada_acc_(a + 1, 0)
                if a < 8:
                    position_table(a // 2)
                dve.wait_ge(s("ada_summed"), a + 2)
                tt(mod[:, 2 * a:2 * a + 4], XB[3][:, 0:4], modb[:, 2 * a:2 * a + 4], ALU.add)\
                    .then_inc(s("ada_done"), 2)

            ffn(0, 0, "gu00", "dn00")
            pl.got("tab_ready", 4)

            mod_in(0, 1)
            take("hyb", plain(0))
            take("hybv", tokens([fv[:, :, 0:256], fv[:, :, 256:512], dv[:, :, 0:256], dv[:, :, 256:512]]))
            turn(list(range(DQ, DQ + 8)) + [IQ, IQ + 1, IK], tabs[:, 0, :])
            r8 = slice(0, 8)
            log_sigmoid(big[0:8, GT, :], r8, sp_("foxb")[0:8, :])
            link(dve.tensor_tensor_scan(gate_row(r8, 1), ones_row(r8), gate_row(r8, 0), 0.0,
                                        ALU.mult, ALU.add))
            link(ts(gate_row(r8, 3), gate_row(r8, 1), 8.0, None, ALU.mult))
            ts(gate_row(r8, 0), gate_row(r8, 1), -8.0, None, ALU.mult).then_inc(s("cum_ready"), 1)
            pl.got("iw_raw")
            link(ts(tokw[:, :], XB[3][:, 0:16], 0.5, None, ALU.mult))

            def causal(qb, W):
                return cc("causal", T - W, W)

            def chunked(qb, W):
                return cc("chunk", T - W, W)

            def scores(qb):
                return wk[:, 2 + qb, 0:(qb + 1) * P]

            for qb in range(1, NB):
                W, sc = (qb + 1) * P, scores(qb)
                for i in range(IDX_H):
                    n = (qb - 1) * IDX_H + i
                    dve.wait_ge(s("idx_relu"), n + 1)
                    iwc = tokw[:, 4 * qb + i:4 * qb + i + 1]
                    if i == 0:
                        ins = ts(sc, S[:, n % 2, 0:W], iwc, None, ALU.mult)
                    else:
                        ins = stt(sc, S[:, n % 2, 0:W], iwc, sc, ALU.mult, ALU.add)
                    ins.then_inc(s("idx_used"), 1)
                    dve.wait_ge(s("idx_used"), n + 1)
                link(tt(sc, sc, chunked(qb, W), ALU.add))

            def select(r):
                qb, i = 1 + r // (TOPK // 8), r % (TOPK // 8)
                W, sc = (qb + 1) * P, scores(qb)
                work, eq = wk[:, 1, 0:W], wk[:, 2, 0:W]
                src = work if i else sc
                link(dve.max(st[:, 0:8], src))
                if i < TOPK // 8 - 1:
                    link(dve.match_replace(work, st[:, 0:8], src, LOWEST))
                    return
                thr = st[:, 7:8]
                link(ts(work, sc, thr, 0.0, ALU.is_gt, ALU.add, accum_out=st[:, 8:9]))
                link(ts(st[:, 9:10], st[:, 8:9], -1.0, float(TOPK), ALU.mult, ALU.add))
                link(ts(eq, sc, thr, None, ALU.is_equal))
                link(dve.tensor_tensor_scan(sc, ones_row(slice(0, P), W), eq, 0.0, ALU.mult, ALU.add))
                link(stt(sc, sc, st[:, 9:10], eq, ALU.is_le, ALU.mult))
                link(tt(sc, sc, work, ALU.add))
                link(ts(big[:, DMASK + qb, 0:W], sc, -NEG, NEG, ALU.mult, ALU.add))

            rounds, units = (NB - 1) * TOPK // 8, FOX_H * NB

            def select_beside(n):
                for r in range(rounds * n // units, rounds * (n + 1) // units):
                    select(r)

            attention(FOX_H, 0.125, 64, causal, 0, beside=select_beside)

            def selected(qb, W):
                return big[:, DMASK + qb, 0:W] if qb else chunked(0, P)

            attention(DSA_H, 0.125, 64, selected, 4)
            residual(0, 1, "hybo")
            ffn(0, 2, "gu01", "dn01")

            ffn(1, 0, "gu10", "dn10")
            mod_in(1, 1)
            take("mlad", plain(0))
            for c0, n, name in ((CQ, 3, "q_norm"), (CKV, 2, "kv_norm")):
                root()
                for c in range(n):
                    ins = stt(big[:, c0 + c, :], big[:, c0 + c, :], sp_(name, c), rstd[:, :], ALU.mult, ALU.mult)
                ins.then_inc(s("latent_ready"), 1)
                pl.got("latent_ready")
            take("mlaq", plain(QN))
            take("mlak", plain(KN))
            take("mlav", tokens(mv))
            turn([KR] + list(range(QR, QR + 4)), tabs[:, 2, :])
            attention(MLA_H, 192.0 ** -0.5, P, chunked, 0)
            residual(1, 1, "mlao")
            ffn(1, 2, "gu11", "dn11")

            scale_in(h, sp_("final_g", 0, DC))
            dve.wait_ge(s("u_scaled"), pl.tu)
            for l in range(DEPTH):
                init = 0.8 - 0.6 * math.exp(-0.3 * l)
                scale_in(u, sp_("norm1", l * DC, DC))
                take(f"in{l}", plain(0))
                pl.groups_taken()
                r4 = slice(0, 4)
                log_sigmoid(big[0:4, GF, :], r4, sp_("gateb", 2 * l + 1)[0:4, :])
                link(ts(gate_row(r4, 1), big[0:4, GI, :], sp_("gateb", 2 * l)[0:4, :], None, ALU.add))
                link(dve.tensor_tensor_scan(gate_row(r4, 4), ones_row(r4), gate_row(r4, 0), 0.0,
                                            ALU.mult, ALU.add))
                link(tt(gate_row(r4, 3), gate_row(r4, 1), gate_row(r4, 4), ALU.subtract))
                link(dve.tensor_tensor_scan(gate_row(r4, 2), gate_row(r4, 3), gate_row(r4, 3), 0.0,
                                            ALU.max, ALU.max))
                link(tt(gate_row(r4, 1), gate_row(r4, 2), gate_row(r4, 4), ALU.add))
                dve.nop().then_inc(s("em_log"), 1)
                link(ts(gate_row(r4, 5), gate_row(r4, 2), -1.0, None, ALU.mult))
                dve.nop().then_inc(s("gates_rows"), 1)

                def conv(c):
                    if c >= 2:
                        pl.got("conv_silu")
                    y, xx = big[:, SP + c % 2, :], big[:, XQ + c, :]
                    tap = [sp_("conv", (l * 4 + c) * 4 + i) for i in range(4)]
                    link(ts(y, xx, tap[3], None, ALU.mult))
                    for d in (1, 2, 3):
                        ins = stt(y[:, d:T], xx[:, 0:T - d], tap[3 - d], y[:, d:T], ALU.mult, ALU.add)
                        if d < 3:
                            link(ins)
                    ins.then_inc(s("conv_raw"), 1)

                def norm_qk(i):
                    root(i)
                    stt(big[:, AQ + i, :], big[:, AQ + i, :], sp_("qn" if i < 4 else "kn", l), rstds[i % 2],
                        ALU.mult, ALU.mult).then_inc(s("qk_normed"), 1)
                    pl.got("qk_normed")

                values = tokens([xv[:, :, :], av[:, :, 0:256], av[:, :, 256:512], hv[:, :, :]])

                def values_and_others(k, it, p):
                    values(k, it, p)
                    conv(k)
                    for i in range(2 * k - 2, 2 * k) if k else ():
                        norm_qk(i)

                take(f"inv{l}", values_and_others)
                norm_qk(6)
                norm_qk(7)
                turn(range(AQ, AQ + 8), cc("diff_sin"))
                attention(DIFF_H, 0.125, P, causal, 2, maps=2, lam=st[:, 50 + l:51 + l])
                link(ts(st[:, 52:53], sp_("subln", l), 1.0 - init, None, ALU.mult))
                for c in range(DIFF_H):
                    root(c)
                    link(stt(u[:, 2 + c, :], u[:, 2 + c, :], st[:, 52:53], rstds[c % 2], ALU.mult, ALU.mult))

                pl.got("conv_silu", 2)
                pl.got("a_cols")
                link(dve.tensor_copy(tokw[:, :], XB[3][:, 0:16]))
                u0 = l * 4 * NB
                for n in range(4 * NB + 1):
                    if n < 4 * NB:
                        hh, b = divmod(n, NB)
                        if b == 0:
                            pl.got("g_ready")
                            dve.tensor_copy(wk[:, hh % 2, :], XB[0][:, :]).then_inc(s("g_taken"), 1)
                            dve.wait_ge(s("g_taken"), l * 4 + hh + 1)
                        tt(wk[:, 2 + n % 2, 0:P], wk[:, hh % 2, blk(b)], cc("tri"), ALU.add)\
                            .then_inc(s("g_diag"), 1)
                    if n:
                        i = n - 1
                        hh, b = divmod(i, NB)
                        W = T - b * P
                        dve.wait_ge(s("me_done"), u0 + i + 1)
                        dve.wait_ge(s("mqk_done"), u0 + i + 1)
                        if u0 + i >= 2:
                            dve.wait_ge(s("m_out"), u0 + i - 1)
                        stt(S[:, i % 2, 0:W], XB[1 + i % 2][:, 0:W], 0.125, E[:, i % 4, 0:W], ALU.mult, ALU.mult)\
                            .then_inc(s("ms_ready"), 1)
                dve.wait_ge(s("m_out"), u0 + 4 * NB)
                for cp in range(2):
                    pl.got("em_ready")
                    dve.tensor_copy(wk[:, 2, :], XB[3][:, :]).then_inc(s("em_taken"), 1)
                    dve.wait_ge(s("em_taken"), 2 * l + cp + 1)
                    link(stt(wk[:, 3, :], LP[1][:, cp, :], -1.0, wk[:, 2, :], ALU.mult, ALU.max))
                    link(tt(wk[:, 3, :], wk[:, 3, :], LP[1][:, cp, :], ALU.max))
                    link(dve.reciprocal(wk[:, 3, :], wk[:, 3, :]))
                    tt(u[:, cp, :], wk[:, 3, :], LP[0][:, cp, :], ALU.mult).then_inc(s("m_mix"), 1)
                    root()
                    link(stt(u[:, cp, :], u[:, cp, :], sp_("mnorm", l), rstd[:, :], ALU.mult, ALU.mult))
                    pl.got("o_sigmoid")
                    link(tt(u[:, cp, :], u[:, cp, :], big[:, XO + cp, :], ALU.mult))

                for cp in range(2):
                    c = 2 * l + cp
                    lbc, olb = st[:, 34 + c:35 + c], st[:, 38 + c:39 + c]
                    pl.got("h_sig")
                    ts(big[:, HF + cp, :], big[:, HF + cp, :], olb, lbc, ALU.mult, ALU.add)\
                        .then_inc(s("h_f"), 1)
                    link(ts(big[:, SP + cp, :], wk[:, 4, :], olb, None, ALU.mult))
                    pl.got("h_lnf")
                    link(dve.tensor_tensor_scan(big[:, XQ + cp, :], ones_row(slice(0, P)), big[:, HF + cp, :], 0.0,
                                                ALU.mult, ALU.add))
                    dve.nop().then_inc(s("h_kb"), 1)
                    B = big[:, XQ + cp, :]

                    def exponents(step):
                        b = 1 << (step - 1)
                        Bv, X = (t.rearrange("p (j i b) -> p j i b", i=2, b=b) for t in (B, wk[:, step % 2, :]))
                        ref = Bv[:, :, 0, b - 1:b].to_broadcast([P, T // (2 * b), b])
                        if step >= 3:
                            dve.wait_ge(s("ex_ready"), (2 * l + cp) * 9 + step - 2)
                        tt(X[:, :, 0, :], ref, Bv[:, :, 0, :], ALU.subtract)
                        tt(X[:, :, 1, :], Bv[:, :, 1, :], ref, ALU.subtract).then_inc(s("x_ready"), 1)

                    exponents(1)
                    for step in range(10):
                        if 1 <= step < 9:
                            exponents(step + 1)
                        for j in range(2):
                            k = (l * 2 + cp) * 20 + 2 * step + j
                            bank = XB[k % 4]
                            dve.wait_ge(s("level_mm"), k + 1)
                            ad = wk[:, 2 + j, :].rearrange("p (b t) -> p b t", b=NB)
                            bk = bank[:, :].rearrange("p (b t) -> p b t", b=NB)
                            m = cc("levels", step * P, P).unsqueeze(1).to_broadcast([P, NB, P]) if step < 8 else None
                            if step == 0:
                                ins = tt(ad, m, bk, ALU.mult)
                            elif step < 8:
                                ins = dve.copy_predicated(ad, m.bitcast(U32), bk)
                            elif step == 8:
                                dve.tensor_copy(tmp[:, j, 0:P], bank[:, 0:P])
                                ins = dve.tensor_copy(tmp[:, j, 640:768], bank[:, P:2 * P])
                            else:
                                ins = dve.tensor_copy(tmp[:, j, P:640], bank[:, :])
                            ins.then_inc(s("level_taken"), 1)
                            dve.wait_ge(s("level_taken"), k + 1)
                    dve.nop().then_inc(s("a_done"), 1)
                    pl.got("h_out")
                    dve.tensor_copy(u[:, 6 + cp, :], LP[0][:, cp, :]).then_inc(s("h_mix"), 1)
                    root()
                    link(stt(u[:, 6 + cp, :], u[:, 6 + cp, :], sp_("hnorm", l), rstd[:, :], ALU.mult, ALU.mult))
                    link(tt(u[:, 6 + cp, :], u[:, 6 + cp, :], big[:, HG + cp, :], ALU.mult))
                dve.nop().then_inc(s("mix_ready"), 1)

                def add2(k, it, p):
                    tt(h[:, 2 * k:2 * k + 2, :], h[:, 2 * k:2 * k + 2, :], LP[p][:, :, :], ALU.add)\
                        .then_inc(s(f"lin_taken{p}"), 1)

                take(f"wo{l}", add2)
                scale_in(u, sp_("norm2", l * DC, DC))

                def square(k, it, p):
                    dve.wait_ge(s("silu_done"), at(pl.silu + k + 1, it, RING))
                    cut_hidden(k, it, p, pl.low, 2, lambda o: tt(o, o, LP[p][:, :, :], ALU.mult))

                def add1(k, it, p):
                    o = h[:, dyn(h, k, it, 1, 1), :]
                    tt(o, o, LP[p][:, 0:1, :], ALU.add).then_inc(s(f"lin_taken{p}"), 1)

                for part in "ab":
                    take(f"up{l}{part}", square)
                    pl.silu += 8
                    pl.low += 8
                    take(f"down{l}{part}", add1)


GROUPS = 4 * (FC + 2 * DC) + 18 + 3 + 6 + 4 + 4 + 4 + DEPTH * (11 + 4 + 4 + 16 + 2 * DC)



def _const_table(lam):
    c = np.zeros((P, NCONST), np.float32)
    c2 = np.zeros((P, NCONST2), np.float32)

    def put(name, a):
        t, (o, wd) = (c, COFF[name]) if name in COFF else (c2, COFF2[name])
        t[:a.shape[0], o:o + a.shape[1]] = a

    put("lam", np.broadcast_to(lam.reshape(1, -1), (P, DEPTH * 256)))

    i = np.arange(P)
    t = np.arange(T)
    put("ident", np.eye(P))
    put("ones", np.ones((P, P)))
    put("blk64", (i[:, None] // 64 == i[None, :] // 64) * 1.0)
    for name, half in (("rot16", 8), ("rot64", 32)):
        r = np.zeros((P, P))
        for b in (0, 64):
            for k in range(half):
                r[b + half + k, b + k] = -1.0
                r[b + k, b + half + k] = 1.0
        put(name, r)
    m = np.zeros((P, T))
    m[:, T - P:] = np.where(i[None, :] <= i[:, None], 0.0, NEG)
    put("causal", m)
    m = np.zeros((P, T))
    m[:, T - P:] = np.where(i[None, :] // 64 <= i[:, None] // 64, 0.0, NEG)
    put("chunk", m)
    put("tri", np.where(i[:, None] <= i[None, :], 0.0, NEG))
    lv = [np.eye(P)]
    for k in range(7):
        b = 1 << k
        same = i[:, None] // (2 * b) == i[None, :] // (2 * b)
        lv.append((same & (i[:, None] // b % 2 == 0) & (i[None, :] // b % 2 == 1)) * 1.0)
    put("levels", np.concatenate(lv, 1))
    for name, rot, theta in (("invf16", 16, 500000.0), ("invf64", 64, 10000.0)):
        half = rot // 2
        f = np.exp(np.float32(-math.log(theta) * 2.0) * np.arange(half, dtype=np.float32) / np.float32(rot))
        col = np.zeros((64, 1), np.float32)
        col[:half, 0] = f
        col[half:rot, 0] = f
        put(name, np.concatenate([col, col]))
    put("eps", np.full((P, 1), RMS_EPS))
    half = 8
    inv = np.float32(500000.0) ** (-np.arange(half, dtype=np.float32) / half)
    ang = t.astype(np.float32)[None, :] * inv[:, None].astype(np.float32)
    cos, sin = np.ones((64, T)), np.zeros((64, T))
    for k in (0, half):
        cos[k:k + half] = np.cos(ang.astype(np.float64))
        sin[k:k + half] = np.sin(ang.astype(np.float64))
    put("diff_cos", np.concatenate([cos, cos]))
    put("diff_sin", np.concatenate([sin, sin]))
    sel = np.zeros((4, 2 * P))
    for cp in range(2):
        for half in range(2):
            sel[2 * cp + half, cp * P + 64 * half:cp * P + 64 * half + 64] = 1.0
    put("sel4", sel)
    return c, c2


def _columns(v):
    return np.asarray(v).reshape(-1, P).T


def _fm(wt):
    K, F = wt.shape
    return np.ascontiguousarray(wt.reshape(K // P, P, F // 256, 256).transpose(2, 1, 0, 3)).reshape(F // 256, P, -1)


def _down(wt):
    K = wt.shape[0]
    return np.ascontiguousarray(wt.reshape(K // P, P, DC, P).transpose(2, 1, 0, 3)).reshape(DC, P, -1)


def kernel(**inp):
    import concourse.bacc as _bacc
    from concourse.bass_utils import run_bass_kernel_spmd as _run

    a = {k: np.asarray(v) for k, v in inp.items()}
    small = np.zeros((P, NSMALL), np.float32)

    def put(name, v, at=0, rows=P):
        o = SOFF[name][0] + at
        small[:rows, o:o + v.shape[1]] = v

    put("norm_g", _columns(a["norm_g"]))
    put("final_g", _columns(a["final_g"]))
    put("norm1", _columns(a["norm1_g_2"]))
    put("norm2", _columns(a["norm2_g_2"]))
    put("q_norm", _columns(a["mla_q_norm"]))
    put("kv_norm", _columns(a["mla_kv_norm"]))
    put("conv", a["mlstm_conv_w_2"].reshape(DEPTH, 4, 4, P).transpose(3, 0, 2, 1).reshape(P, -1))
    for l in range(DEPTH):
        for name, key in (("mnorm", "mlstm_norm_g_2"), ("qn", "diff_q_norm_g_2"), ("kn", "diff_k_norm_g_2"),
                          ("hnorm", "hgrn_norm_g_2")):
            put(name, np.tile(a[key][l], 2)[:, None], l)
        put("subln", a["diff_subln_g_2"][l][:, None], l)
        for i in range(2):
            put("gateb", a["mlstm_gate_b_2"][l, i][:, None], 2 * l + i, rows=4)
    put("lb", _columns(a["hgrn_lb_param_2"]))
    put("cond", _columns(a["c"]))
    put("foxb", a["fox_b_f"][0][:, None], rows=8)
    W = {"ada": np.concatenate([_fm(a["ada_w"][l]) for l in range(DEPTH)])}
    for l in range(DEPTH):
        for j in range(2):
            g, up, dn = (a[k][l, j] for k in ("ffn_w_gate", "ffn_w_up", "ffn_w_down"))
            gu = np.stack([g.reshape(D, FC, P), up.reshape(D, FC, P)], 2).reshape(D, 2 * FF)
            for i, part in enumerate("ab"):
                W[f"gu{l}{j}{part}"] = _fm(gu[:, i * FF:(i + 1) * FF])
                W[f"dn{l}{j}{part}"] = _down(dn[i * FF // 2:(i + 1) * FF // 2])
    hw = a["hyb_w_in"][0]
    off = np.cumsum([0, 512, 512, 512, 8, 512, 512, 512, 256, 4, 64])
    fq, fk, fvw, ff, dq, dk, dvw, iq, iwt, ik = (hw[:, off[i]:off[i + 1]] for i in range(10))
    z = lambda n: np.zeros((D, n), np.float32)
    W["hyb"] = _fm(np.concatenate([fq, fk, dq, dk, iq, ik, ik, ff, z(24), iwt, z(92)], 1))
    W["hybv"] = _fm(np.concatenate([fvw, dvw], 1))
    W["hybo"] = _fm(a["hyb_w_out"][0])
    md = a["mla_w_down"][0]
    W["mlad"] = _fm(np.concatenate([md, md[:, 640:704]], 1))
    uq = a["mla_w_uq"][0].reshape(384, MLA_H, 192)
    W["mlaq"] = _fm(np.concatenate([uq[:, :, :128].reshape(384, -1), uq[:, :, 128:].reshape(384, -1)], 1))
    ukv = a["mla_w_ukv"][0].reshape(256, MLA_H, 256)
    W["mlak"] = _fm(np.ascontiguousarray(ukv[:, :, :128]).reshape(256, -1))
    W["mlav"] = _fm(np.ascontiguousarray(ukv[:, :, 128:]).reshape(256, -1))
    W["mlao"] = _fm(a["mla_w_out"][0])
    for l in range(DEPTH):
        wi = a["w_in_2"][l]
        off = np.cumsum([0, 256, 256, 256, 256, 4, 4, 512, 512, 512, 256, 256, 256, 256])
        mq, mk, mvw, mo, mi, mf, aq, ak, avw, hq, hf, hi, hg = (wi[:, off[i]:off[i + 1]] for i in range(13))
        W[f"in{l}"] = _fm(np.concatenate([mq, mk, mo, aq, ak, hq, hf, hg, mi, z(124), mf, z(124)], 1))
        W[f"inv{l}"] = _fm(np.concatenate([mvw, avw, hi], 1))
        W[f"wo{l}"] = _fm(a["w_out_2"][l])
        for i, part in enumerate("ab"):
            at = slice(i * FF2 // 2, (i + 1) * FF2 // 2)
            W[f"up{l}{part}"] = _fm(a["w_up_2"][l][:, at])
            W[f"down{l}{part}"] = _down(a["w_down_2"][l][at])

    consts, consts2 = _const_table(a["diff_lambda_2"])
    arrays = {
        "x": np.ascontiguousarray(a["x"][0].T.reshape(DC, P, T).transpose(1, 0, 2)),
        "small": small,
        "consts": consts,
        "consts2": consts2,
        "pos": np.ascontiguousarray(np.broadcast_to(a["positions"].astype(np.int32), (P, T))),
        "adab": np.ascontiguousarray(_columns(a["ada_b"])),
    }
    nc = _bacc.Bacc("TRN2", target_bir_lowering=False, num_devices=1)

    def dram(name, arr):
        return nc.dram_tensor(name, arr.shape, mybir.dt.from_np(arr.dtype), kind="ExternalInput").ap()

    aps = {k: dram(k, v) for k, v in arrays.items()}
    w = {k: dram("w_" + k, v) for k, v in W.items()}
    arrays.update({"w_" + k: v for k, v in W.items()})
    out = nc.dram_tensor("out", (P, DC, T), F32, kind="ExternalOutput").ap()
    build(nc, aps["x"], aps["small"], aps["consts"], aps["consts2"], aps["pos"], aps["adab"], w, out)
    r = _run(nc, [arrays], core_ids=[0])
    got = r.results[0]["out"]
    return np.ascontiguousarray(got.transpose(1, 0, 2).reshape(D, T).T)[None]
```
